# Optimizing a Trainium2 kernel written in Bass

```python
import jax, jax.numpy as jnp
from jax import lax
import numpy as np

D_MODEL = 1024
BATCH = 1
SEQ = 512
DEPTH = 2

GRID_W = 64
CTX_LEN = 256
EPS = 1e-6
ATTN_Q_BLOCK = 128

NA_HEADS = 4
NA_HEAD_DIM = 64
NA_WIN_H = 8
NA_WIN_W = 16
NA_WIDTH = NA_HEADS * NA_HEAD_DIM

MLA_HEADS = 4
MLA_Q_RANK = 256
MLA_KV_RANK = 128
MLA_NOPE_DIM = 64
MLA_ROPE_DIM = 32
MLA_V_DIM = 64
MLA_WIDTH = MLA_HEADS * MLA_V_DIM
ROPE_THETA = 10000.0

GLA_HEADS = 4
GLA_DK = 64
GLA_DV = 128
GLA_KW = GLA_HEADS * GLA_DK
GLA_VW = GLA_HEADS * GLA_DV
GLA_GATE_RANK = 16
GLA_TAU = 16.0
GLA_CHUNK = 64

N_BRANCH = 3
N_EXPERTS = 16
EXPERT_FF = 1024
EC_CAPACITY = 2

IN_SIZES = (NA_WIDTH, NA_WIDTH, NA_WIDTH,
            MLA_Q_RANK, MLA_KV_RANK, MLA_ROPE_DIM,
            GLA_KW, GLA_KW, GLA_VW, GLA_GATE_RANK, GLA_GATE_RANK, GLA_VW,
            D_MODEL, D_MODEL, D_MODEL)
D_IN = sum(IN_SIZES)

kernel_name = 'hybrid_na_mla_gla_ec_diffusion_block'

def rms_norm(x, g):
    xf = x.astype(jnp.float32)
    y = xf * lax.rsqrt(jnp.mean(xf * xf, axis=-1, keepdims=True) + EPS)
    return (y * g.astype(jnp.float32)).astype(x.dtype)

def modulate(h, shift, scale):
    return h * (1 + scale) + shift

def split_cols(z, sizes):
    parts, off = [], 0
    for s in sizes:
        parts.append(z[..., off:off + s])
        off += s
    return parts

def to_heads(z, n_heads):
    B, T, W = z.shape
    return z.reshape(B, T, n_heads, W // n_heads).transpose(0, 2, 1, 3)

def from_heads(z):
    B, H, T, d = z.shape
    return z.transpose(0, 2, 1, 3).reshape(B, T, H * d)

def axial_rope(x, rows, cols):
    half = x.shape[-1] // 2
    quarter = half // 2
    inv_freq = ROPE_THETA ** (-jnp.arange(quarter, dtype=jnp.float32) / quarter)

    def rot(xa, p):
        ang = p.astype(jnp.float32)[:, None] * inv_freq
        cos = jnp.cos(ang).astype(x.dtype)
        sin = jnp.sin(ang).astype(x.dtype)
        x1, x2 = xa[..., :quarter], xa[..., quarter:]
        return jnp.concatenate([x1 * cos - x2 * sin, x1 * sin + x2 * cos], axis=-1)

    return jnp.concatenate([rot(x[..., :half], rows), rot(x[..., half:], cols)], axis=-1)

def block_attention(q, k, v):
    B, H, T, dq = q.shape
    nb = T // ATTN_Q_BLOCK
    scale = dq ** -0.5
    qb = q.reshape(B, H, nb, ATTN_Q_BLOCK, dq).transpose(2, 0, 1, 3, 4)

    def one_block(qi):
        s = jnp.einsum('bhqd,bhkd->bhqk', qi, k).astype(jnp.float32) * scale
        p = jax.nn.softmax(s, axis=-1).astype(v.dtype)
        return jnp.einsum('bhqk,bhkd->bhqd', p, v)

    o = lax.map(one_block, qb)
    return o.transpose(1, 2, 0, 3, 4).reshape(B, H, T, v.shape[-1])

def neighbourhood_attention(q, k, v, k_ctx, v_ctx, rpb):
    B, H, T, dh = q.shape
    rows = T // GRID_W
    kh = min(NA_WIN_H, rows)
    kw = NA_WIN_W
    scale = dh ** -0.5
    qg = q.reshape(B, H, rows, GRID_W, dh)
    kg = k.reshape(B, H, rows, GRID_W, dh)
    vg = v.reshape(B, H, rows, GRID_W, dh)
    col = jnp.arange(GRID_W)
    col_start = jnp.clip(col - kw // 2, 0, GRID_W - kw)
    col_idx = col_start[:, None] + jnp.arange(kw)[None, :]
    col_off = col_idx - col[:, None] + (NA_WIN_W - 1)
    rpb_c = rpb[:, :, col_off]

    def one_row(r):
        rs = jnp.clip(r - kh // 2, 0, rows - kh)
        kb = lax.dynamic_slice_in_dim(kg, rs, kh, axis=2)[:, :, :, col_idx, :]
        vb = lax.dynamic_slice_in_dim(vg, rs, kh, axis=2)[:, :, :, col_idx, :]
        qr = lax.dynamic_index_in_dim(qg, r, axis=2, keepdims=False)
        s_loc = jnp.einsum('bhcd,bhicjd->bhcij', qr, kb).astype(jnp.float32) * scale
        row_off = rs + jnp.arange(kh) - r + (NA_WIN_H - 1)
        bias = jnp.take(rpb_c, row_off, axis=1).transpose(0, 2, 1, 3)
        s_loc = s_loc + bias[None].astype(jnp.float32)
        s_ctx = jnp.einsum('bhcd,bhnd->bhcn', qr, k_ctx).astype(jnp.float32) * scale
        s = jnp.concatenate([s_loc.reshape(B, H, GRID_W, kh * kw), s_ctx], axis=-1)
        p = jax.nn.softmax(s, axis=-1).astype(v.dtype)
        p_loc = p[..., :kh * kw].reshape(B, H, GRID_W, kh, kw)
        p_ctx = p[..., kh * kw:]
        return (jnp.einsum('bhcij,bhicjd->bhcd', p_loc, vb)
                + jnp.einsum('bhcn,bhnd->bhcd', p_ctx, v_ctx))

    o = lax.map(one_row, jnp.arange(rows))
    return o.transpose(1, 2, 0, 3, 4).reshape(B, H, T, dh)

def mla_heads(dq, dkv, kr, q_norm, w_uq, kv_norm, w_ukv, pos):
    B, T, _ = dq.shape
    qh = (rms_norm(dq, q_norm) @ w_uq).reshape(B, T, MLA_HEADS, MLA_NOPE_DIM + MLA_ROPE_DIM).transpose(0, 2, 1, 3)
    q_nope, q_rope = qh[..., :MLA_NOPE_DIM], qh[..., MLA_NOPE_DIM:]
    kvh = (rms_norm(dkv, kv_norm) @ w_ukv).reshape(B, T, MLA_HEADS, MLA_NOPE_DIM + MLA_V_DIM).transpose(0, 2, 1, 3)
    k_nope, v = kvh[..., :MLA_NOPE_DIM], kvh[..., MLA_NOPE_DIM:]
    k_rope = kr[:, None]
    if pos is not None:
        q_rope = axial_rope(q_rope, pos[0], pos[1])
        k_rope = axial_rope(k_rope, pos[0], pos[1])
    k_rope = jnp.broadcast_to(k_rope, (B, MLA_HEADS, T, MLA_ROPE_DIM))
    q = jnp.concatenate([q_nope, q_rope], axis=-1)
    k = jnp.concatenate([k_nope, k_rope], axis=-1)
    return q, k, v

def gla_log_decay(a_low, w2, b2):
    z = (a_low @ w2 + b2).astype(jnp.float32)
    return to_heads(jax.nn.log_sigmoid(z) / GLA_TAU, GLA_HEADS)

def gla_heads(q, k, v, a_f, a_b, w_af, b_af, w_ab, b_ab):
    return (to_heads(q, GLA_HEADS), to_heads(k, GLA_HEADS), to_heads(v, GLA_HEADS),
            gla_log_decay(a_f, w_af, b_af), gla_log_decay(a_b, w_ab, b_ab))

def gla_chunked(q, k, v, g, s0):
    B, H, T, dk = q.shape
    dv = v.shape[-1]
    C = GLA_CHUNK
    N = T // C
    qf = q.astype(jnp.float32).reshape(B, H, N, C, dk) * dk ** -0.5
    kf = k.astype(jnp.float32).reshape(B, H, N, C, dk)
    vf = v.astype(jnp.float32).reshape(B, H, N, C, dv)
    b = jnp.cumsum(g.reshape(B, H, N, C, dk), axis=3)
    b_last = b[:, :, :, -1:, :]
    q_dec = qf * jnp.exp(b)
    k_dec = kf * jnp.exp(-b)
    k_to_end = kf * jnp.exp(b_last - b)
    mask = jnp.tril(jnp.ones((C, C), dtype=bool))
    a = jnp.where(mask, jnp.einsum('bhntd,bhnsd->bhnts', q_dec, k_dec), 0.0)
    o_intra = jnp.einsum('bhnts,bhnsv->bhntv', a, vf)
    kv_chunk = jnp.einsum('bhnsd,bhnsv->bhndv', k_to_end, vf)
    decay = jnp.exp(b_last[:, :, :, 0, :])

    def step(s, inp):
        dec, kv = inp
        return dec[..., None] * s + kv, s

    s_fin, s_prev = lax.scan(step, s0, (jnp.moveaxis(decay, 2, 0), jnp.moveaxis(kv_chunk, 2, 0)))
    o_inter = jnp.einsum('bhntd,bhndv->bhntv', q_dec, jnp.moveaxis(s_prev, 0, 2))
    o = (o_intra + o_inter).reshape(B, H, T, dv)
    return o.astype(v.dtype), s_fin

def gla_bidirectional(qc, kc, vc, gfc, gbc, ql, kl, vl, gfl, gbl):
    B, H, _, dk = qc.shape
    s0 = jnp.zeros((B, H, dk, vc.shape[-1]), jnp.float32)
    rev = lambda u: jnp.flip(u, axis=2)
    oc_f, sc_f = gla_chunked(qc, kc, vc, gfc, s0)
    oc_b, sc_b = gla_chunked(rev(qc), rev(kc), rev(vc), rev(gbc), s0)
    ol_f, _ = gla_chunked(ql, kl, vl, gfl, sc_f)
    ol_b, _ = gla_chunked(rev(ql), rev(kl), rev(vl), rev(gbl), sc_b)
    return ol_f + rev(ol_b), oc_f + rev(oc_b)

def gla_output(o, og, o_norm):
    return from_heads(rms_norm(o, o_norm)) * jax.nn.silu(og)

def gated_merge(o_a, o_b, o_c, m_a, m_b, m_c, w_br_a, w_br_b, w_br_c, w_out):
    y = (jax.nn.sigmoid(m_a) * (o_a @ w_br_a)
         + jax.nn.sigmoid(m_b) * (o_b @ w_br_b)
         + jax.nn.sigmoid(m_c) * (o_c @ w_br_c))
    return y @ w_out

def expert_choice_moe(h, w_router, w_gate, w_up, w_down):
    B, T, D = h.shape
    cap = EC_CAPACITY * T // N_EXPERTS
    aff = jax.nn.softmax((h @ w_router).astype(jnp.float32), axis=-1)
    top_w, top_idx = lax.top_k(aff.transpose(0, 2, 1), cap)
    xg = jax.vmap(lambda hb, ib: hb[ib])(h, top_idx)
    hid = jax.nn.silu(jnp.einsum('becd,edf->becf', xg, w_gate)) * jnp.einsum('becd,edf->becf', xg, w_up)
    ye = jnp.einsum('becf,efd->becd', hid, w_down) * top_w[..., None].astype(h.dtype)
    return jax.vmap(lambda ib, yb: jnp.zeros((T, D), h.dtype).at[ib.reshape(-1)].add(yb.reshape(-1, D)))(top_idx, ye)

def hybrid_layer(x, ctx, c, c_ctx, ada_w, ada_b, norm1, norm2, w_in, na_rpb,
                 mla_q_norm, mla_w_uq, mla_kv_norm, mla_w_ukv,
                 gla_w_af, gla_b_af, gla_w_ab, gla_b_ab, gla_o_norm,
                 w_br_a, w_br_b, w_br_c, w_out,
                 moe_router, moe_w_gate, moe_w_up, moe_w_down, ctx_out):
    B, T, D = x.shape
    L = ctx.shape[1]
    t = jnp.arange(T)
    pos = (t // GRID_W, t % GRID_W)
    mod_l = [m[:, None, :] for m in jnp.split(jax.nn.silu(c) @ ada_w + ada_b, 6, axis=-1)]
    mod_c = jnp.split(jax.nn.silu(c_ctx) @ ada_w + ada_b, 6, axis=-1)

    h_l = modulate(rms_norm(x, norm1), mod_l[0], mod_l[1])
    h_c = modulate(rms_norm(ctx, norm1), mod_c[0], mod_c[1])
    z = jnp.concatenate([h_c, h_l], axis=1) @ w_in
    zc = split_cols(z[:, :L], IN_SIZES)
    zl = split_cols(z[:, L:], IN_SIZES)

    qa_l, ka_l, va_l = (to_heads(u, NA_HEADS) for u in zl[0:3])
    qa_c, ka_c, va_c = (to_heads(u, NA_HEADS) for u in zc[0:3])
    oa_l = from_heads(neighbourhood_attention(qa_l, ka_l, va_l, ka_c, va_c, na_rpb))

    qb_l, kb_l, vb_l = mla_heads(zl[3], zl[4], zl[5], mla_q_norm, mla_w_uq, mla_kv_norm, mla_w_ukv, pos)
    qb_c, kb_c, vb_c = mla_heads(zc[3], zc[4], zc[5], mla_q_norm, mla_w_uq, mla_kv_norm, mla_w_ukv, None)
    ob_l = from_heads(block_attention(qb_l, jnp.concatenate([kb_c, kb_l], axis=2),
                                      jnp.concatenate([vb_c, vb_l], axis=2)))

    gc = gla_heads(zc[6], zc[7], zc[8], zc[9], zc[10], gla_w_af, gla_b_af, gla_w_ab, gla_b_ab)
    gl = gla_heads(zl[6], zl[7], zl[8], zl[9], zl[10], gla_w_af, gla_b_af, gla_w_ab, gla_b_ab)
    oc_l_raw, oc_c_raw = gla_bidirectional(*gc, *gl)
    oc_l = gla_output(oc_l_raw, zl[11], gla_o_norm)

    y_l = gated_merge(oa_l, ob_l, oc_l, zl[12], zl[13], zl[14], w_br_a, w_br_b, w_br_c, w_out)
    x = x + mod_l[2] * y_l
    x = x + mod_l[5] * expert_choice_moe(modulate(rms_norm(x, norm2), mod_l[3], mod_l[4]),
                                         moe_router, moe_w_gate, moe_w_up, moe_w_down)

    if ctx_out:
        oa_c = from_heads(block_attention(qa_c, ka_c, va_c))
        ob_c = from_heads(block_attention(qb_c, kb_c, vb_c))
        oc_c = gla_output(oc_c_raw, zc[11], gla_o_norm)
        y_c = gated_merge(oa_c, ob_c, oc_c, zc[12], zc[13], zc[14], w_br_a, w_br_b, w_br_c, w_out)
        ctx = ctx + mod_c[2] * y_c
        ctx = ctx + mod_c[5] * expert_choice_moe(modulate(rms_norm(ctx, norm2), mod_c[3], mod_c[4]),
                                                 moe_router, moe_w_gate, moe_w_up, moe_w_down)
    return x, ctx

def setup_inputs(seed: int = 0) -> dict:
    key = jax.random.key(seed)
    ks = iter(jax.random.split(key, 32))

    def nrm(shape, std):
        return jax.random.normal(next(ks), shape, jnp.float32) * std

    def gain(shape):
        return 1.0 + nrm(shape, 0.02)

    D = D_MODEL
    return {
        'x': nrm((BATCH, SEQ, D), 1.0),
        'c': nrm((BATCH, D), 1.0),
        'ctx': nrm((BATCH, CTX_LEN, D), 1.0),
        'c_ctx': nrm((D,), 1.0),
        'ada_w': nrm((DEPTH, D, 6 * D), 0.5 * D ** -0.5),
        'ada_b': nrm((DEPTH, 6 * D), 0.01),
        'norm1': gain((DEPTH, D)),
        'norm2': gain((DEPTH, D)),
        'w_in': nrm((DEPTH, D, D_IN), D ** -0.5),
        'na_rpb': nrm((DEPTH, NA_HEADS, 2 * NA_WIN_H - 1, 2 * NA_WIN_W - 1), 0.1),
        'mla_q_norm': gain((DEPTH, MLA_Q_RANK)),
        'mla_w_uq': nrm((DEPTH, MLA_Q_RANK, MLA_HEADS * (MLA_NOPE_DIM + MLA_ROPE_DIM)), MLA_Q_RANK ** -0.5),
        'mla_kv_norm': gain((DEPTH, MLA_KV_RANK)),
        'mla_w_ukv': nrm((DEPTH, MLA_KV_RANK, MLA_HEADS * (MLA_NOPE_DIM + MLA_V_DIM)), MLA_KV_RANK ** -0.5),
        'gla_w_af': nrm((DEPTH, GLA_GATE_RANK, GLA_KW), GLA_GATE_RANK ** -0.5),
        'gla_b_af': 1.0 + nrm((DEPTH, GLA_KW), 0.5),
        'gla_w_ab': nrm((DEPTH, GLA_GATE_RANK, GLA_KW), GLA_GATE_RANK ** -0.5),
        'gla_b_ab': 1.0 + nrm((DEPTH, GLA_KW), 0.5),
        'gla_o_norm': gain((DEPTH, GLA_DV)),
        'w_br_a': nrm((DEPTH, NA_WIDTH, D), NA_WIDTH ** -0.5),
        'w_br_b': nrm((DEPTH, MLA_WIDTH, D), MLA_WIDTH ** -0.5),
        'w_br_c': nrm((DEPTH, GLA_VW, D), GLA_VW ** -0.5),
        'w_out': nrm((DEPTH, D, D), D ** -0.5),
        'moe_router': nrm((DEPTH, D, N_EXPERTS), D ** -0.5),
        'moe_w_gate': nrm((DEPTH, N_EXPERTS, D, EXPERT_FF), D ** -0.5),
        'moe_w_up': nrm((DEPTH, N_EXPERTS, D, EXPERT_FF), D ** -0.5),
        'moe_w_down': nrm((DEPTH, N_EXPERTS, EXPERT_FF, D), EXPERT_FF ** -0.5),
        'final_norm': gain((D,)),
    }

def reference(x, c, ctx, c_ctx, ada_w, ada_b, norm1, norm2, w_in, na_rpb,
              mla_q_norm, mla_w_uq, mla_kv_norm, mla_w_ukv,
              gla_w_af, gla_b_af, gla_w_ab, gla_b_ab, gla_o_norm,
              w_br_a, w_br_b, w_br_c, w_out,
              moe_router, moe_w_gate, moe_w_up, moe_w_down, final_norm):
    for l in range(DEPTH):
        x, ctx = hybrid_layer(x, ctx, c, c_ctx, ada_w[l], ada_b[l], norm1[l], norm2[l], w_in[l], na_rpb[l],
                              mla_q_norm[l], mla_w_uq[l], mla_kv_norm[l], mla_w_ukv[l],
                              gla_w_af[l], gla_b_af[l], gla_w_ab[l], gla_b_ab[l], gla_o_norm[l],
                              w_br_a[l], w_br_b[l], w_br_c[l], w_out[l],
                              moe_router[l], moe_w_gate[l], moe_w_up[l], moe_w_down[l],
                              ctx_out=(l < DEPTH - 1))
    return rms_norm(x, final_norm)


_drawn_inputs = setup_inputs


def setup_inputs(seed=0):
    import zlib

    import numpy as np

    out = dict(_drawn_inputs(seed))
    spreads = {}
    factors = {'ada_b': 4.844,
     'norm1': 7.158,
     'norm2': 6.112,
     'na_rpb': 8.0,
     'mla_q_norm': 8.0,
     'mla_kv_norm': 8.0,
     'gla_o_norm': 8.0,
     'final_norm': 3.116}
    for name, (base, spread) in spreads.items():
        noise = np.random.default_rng([zlib.crc32(name.encode()), seed]).standard_normal(out[name].shape)
        drawn = base * np.exp(spread * noise) if base else spread * noise
        out[name] = __import__('jax').numpy.asarray(drawn.astype(out[name].dtype))
    for name, factor in factors.items():
        out[name] = (out[name] * factor).astype(out[name].dtype)
    return out
```

```python
from contextlib import ExitStack

import numpy as np

import concourse.bass as bass
from concourse import mybir

F32 = mybir.dt.float32
ALU = mybir.AluOpType
ACT = mybir.ActivationFunctionType
AX_X = mybir.AxisListType.X

P = 128
D = 1024
KD = D // P
SEQ, CTX = 512, 256
TOK = SEQ + CTX
NT = TOK // P
CT = CTX // P
DEPTH = 2
EPS = 1e-6
GRID_W = 64
H = 4
DH = 64
ROPE = 32
QR, KVR = 256, 128
DQK = DH + ROPE
DV = 128
C = 64
NCH = TOK // C
RANK = 16
E = 16
CAPL, CAPC = 2 * SEQ // E, 2 * CTX // E
GE = 4
NEG = -1.0e30
WIN = 31
PADW = 2 * GRID_W - 1

O_NAQK, O_NAV, O_DQ, O_DKV = 0, 512, 768, 1024
O_GQK, O_GV, O_GA, O_OG, O_M = 1184, 1696, 2208, 2240, 2752
DMLA = QR + KVR + ROPE

K_ID, K_TRI, K_IOTA, K_WIN, K_COS, K_SIN, K_ONE = 0, 128, 384, 448, 512, 640, 768
K_ALL = 896

LAT, CX = slice(CTX, TOK), slice(0, CTX)

R_AB, R_N1, R_N2, R_C, R_CC, R_QN, R_KVN, R_ON, R_BF, R_BB, R_ALL = 0, 48, 56, 64, 72, 80, 82, 83, 84, 86, 88


def constants():
    k = np.zeros((P, K_ALL), np.float32)
    k[:, K_ID:K_ID + P] = np.eye(P)
    s, t = np.arange(P)[:, None], np.arange(P)[None, :]
    same = s // C == t // C
    k[:, K_TRI:K_TRI + P] = same & (s <= t)
    k[:, K_TRI + P:K_TRI + 2 * P] = same & (s >= t)
    k[:, K_IOTA:K_IOTA + 64] = np.arange(64)
    qc = np.arange(P) % GRID_W
    start = np.clip(qc - 8, 0, GRID_W - 16)[:, None]
    kc = np.arange(GRID_W)[None, :]
    k[:, K_WIN:K_WIN + 64] = np.where((kc >= start) & (kc < start + 16), 0.0, NEG)
    inv = np.float32(10000.0) ** (-np.arange(8, dtype=np.float32) / np.float32(8))
    for tile in range(SEQ // P):
        tok = tile * P + np.arange(P)
        for half, pos in enumerate((tok // GRID_W, tok % GRID_W)):
            ang = pos.astype(np.float32)[:, None] * inv
            at = tile * ROPE + half * 16
            for pair, sign in ((0, -1.0), (1, 1.0)):
                k[:, K_COS + at + 8 * pair:K_COS + at + 8 * pair + 8] = np.cos(ang)
                k[:, K_SIN + at + 8 * pair:K_SIN + at + 8 * pair + 8] = sign * np.sin(ang)
    k[:, K_ONE:K_ONE + P] = 1.0
    return k


def hybrid_kernel(nc, a, out):
    ctx = ExitStack()
    with ctx:
        def sb(name, shape):
            return ctx.enter_context(nc.sbuf_tensor(name, shape, F32))

        def sem(name):
            return ctx.enter_context(nc.semaphore(name))

        def sems(name):
            return [sem(f"{name}{l}") for l in range(DEPTH)]

        KB = 256
        x_sb = sb("x_sb", [P, NT, D])
        hT = sb("hT", [P, KD, TOK])
        oT = sb("oT", [P, KD, TOK])
        ring = sb("ring", [P, 2, 16 * KB])
        arena = sb("arena", [P, 96 * KB])
        cst = sb("cst", [P, K_ALL])
        vT = sb("vT", [P, R_ALL])
        silc = sb("silc", [P, 2, KD])
        modT = sb("modT", [P, 48, 2])
        scl = sb("scl", [P, 2, KD, 2])
        router = sb("router", [P, KD, E])
        st = sb("st", [P, 64])
        stm = sb("stm", [P, 4, 8])
        mst = sb("mst", [P, 4, 12])
        top8 = sb("top8", [P, 2, 8])
        turn_s = sb("turn_s", [P, 2, NT, GE])
        hTf = hT[:, :, :].rearrange("p a b -> p (a b)")
        oTf = oT[:, :, :].rearrange("p a b -> p (a b)")
        ringf = ring[:, :, :].rearrange("p a b -> p (a b)")

        def carve(flat, kb, *dims):
            n = int(np.prod(dims))
            v = flat[:, int(kb * KB):int(kb * KB) + n]
            if len(dims) == 1:
                return v
            names = "abcd"[:len(dims)]
            return v.rearrange(f"p ({' '.join(names)}) -> p {' '.join(names)}",
                               **{c: d for c, d in zip(names, dims)})

        ar = arena[:, :]
        ident = cst[:, K_ID:K_ID + P]
        tri = cst[:, K_TRI:K_TRI + 2 * P]
        iota = cst[:, K_IOTA:K_IOTA + 64]
        window = cst[:, K_WIN:K_WIN + 64]
        ones = cst[:, K_ONE:K_ONE + P]

        xn1 = carve(ar, 0, NT, D)
        xn2 = carve(oTf, 0, NT, D)
        vecs = carve(ar, 24, P)
        g_v = carve(ar, 0, NT, H * DV)
        g_raw = carve(ar, 12, 4, TOK)
        g_og = carve(ar, 12, NT, H * DV)
        qd = carve(ar, 24, 2, 2, TOK)
        kd = carve(ar, 36, 2, 2, TOK)
        ke_tok = carve(ar, 48, 2, NT, 256)
        states = carve(ar, 60, 2, NCH, 2, DV)
        w_decay = carve(ar, 84, 2, 256)
        a_mask = carve(ar, 86, 2, 256)
        a_sum = carve(ar, 88, 2, P)
        g_o = carve(ar, 89, 2, H, DV)
        g_sq = carve(ar, 93, H, DV)
        softp = carve(oTf, 0, TOK)
        g_log = carve(oTf, 3, TOK)
        b_cum = carve(oTf, 6, TOK)
        e_pos = carve(oTf, 9, TOK)
        e_neg = carve(oTf, 12, TOK)
        k_end = carve(oTf, 15, TOK)
        aT = carve(oTf, 18, 2, TOK)
        scan_keep = carve(ar, 89, TOK)
        decay = sb("decay", [P, 2, 2, NCH])
        naqT, nakT = carve(ar, 0, 2, TOK), carve(ar, 6, 2, TOK)
        nav = carve(ar, 12, NT, 256)
        bias = carve(ar, 18, H, 14, 64)
        bias_raw = carve(ar, 32, H, 14, 64)
        rpb_in, rpb_pad = carve(ar, 95.5, WIN), carve(ar, 95, PADW)
        dqb = carve(ar, 46, NT, DMLA)
        dqnT, dkvnT = carve(ar, 56, 2, TOK), carve(ar, 62, TOK)
        w_uq, w_ukv = carve(ar, 65, 2, H * DQK), carve(ar, 68, H * 128)
        q_tok, k_tok = carve(ar, 70, H, DQK), carve(ar, 71.5, H, DQK)
        rot = carve(ar, 73, 2, H, ROPE)
        s_bias = carve(ar, 74, 2, SEQ)
        qT, kT = carve(ar, 0, H, TOK), carve(ar, 32, H, TOK)
        mv = carve(ar, 12, NT, H, DH)
        prob = carve(ar, 78, 2, TOK)
        probT = carve(ar, 84, 2, NT, P)
        o_tok = carve(ar, 90, NT, 256)
        yT = carve(ar, 0, KD, TOK)
        w_br = carve(ar, 24, KD, D)
        w_out = carve(ar, 56, KD, D)
        gate_row = carve(ar, 88, 2, D)
        sig = [carve(ringf, 12, SEQ), carve(ringf, 14, SEQ)]
        part = carve(ringf, 30, SEQ)
        diag = carve(ringf, 30, 4, P)
        ex = [carve(ar, 16 * i, KD, 512) for i in range(6)]
        affT, work = carve(hTf, 0, TOK), carve(hTf, 3, TOK)
        chosen, slotT = carve(hTf, 6, TOK), carve(hTf, 9, TOK)
        xg = carve(hTf, 0, KD, GE, CAPL + CAPC)
        ye_l, ye_c = carve(hTf, 12, 2, D), carve(hTf, 20, D)
        hid = carve(ringf, 0, D)
        hidT = carve(ringf, 4, KD, CAPL + CAPC)
        g_act = carve(ringf, 7, 2, 512)
        sel_l, selw_l = carve(ringf, 11, 4, GE, CAPL), carve(ringf, 15, 4, GE, CAPL)
        sel_c, selw_c = carve(ringf, 19, CT, GE, CAPC), carve(ringf, 20, CT, GE, CAPC)
        selT_l, selT_c = carve(ringf, 21, 2, SEQ), carve(ringf, 25, CTX)
        gate5 = carve(ringf, 26, D)
        aff = sb("aff", [P, NT, E])
        slot = sb("slot", [P, NT, E])
        fin_row = carve(ar, 0, D)
        fin = carve(ar, 4, SEQ // P, D)

        ps = [ctx.enter_context(nc.psum_tensor(f"ps{i}", [P, 512], F32)) for i in range(8)]
        rpb_scratch = [nc.dram_tensor(f"rpb_scratch{l}", [H * 15, PADW], F32, kind="Internal").ap()
                       for l in range(DEPTH)]

        def ring_loads(l):
            w_in = a["w_in"][l]
            t = [("ada", a["ada_w"][l][:, 512 * j:512 * j + 512]) for j in range(12)]
            for name, c0, w in (("gqk", O_GQK, 512), ("ga", O_GA, 32), ("gv", O_GV, 512), ("og", O_OG, 512),
                                ("naqk", O_NAQK, 512), ("navdq", O_NAV, 512), ("dkv", O_DKV, 160)):
                t.append((name, w_in[:, c0:c0 + w]))
            t += [("m", j) for j in range(KD)]
            return t

        RL = len(ring_loads(0))
        R_AT = {"ada": 0, "gqk": 12, "ga": 13, "gv": 14, "og": 15, "naqk": 16, "navdq": 17, "dkv": 18, "m": 19}

        def ring_view(n, w):
            return carve(ringf, 16 * (n % 2), KD, w)

        def segments(l):
            return (LAT, CX) if l < DEPTH - 1 else (LAT,)

        def q_tiles(l):
            return list(range(NT)) if l < DEPTH - 1 else list(range(CT, NT))

        def projections(l):
            jobs = {"gqk": [], "ga": [], "gv": [], "og": [], "naqk": [], "navdq": [], "dkv": []}
            for c in range(4):
                for seg in (segments(l) if c < 2 else (LAT, CX)):
                    jobs["gqk"].append((c * P, P, "F", seg, g_raw[:, c, seg], DH ** -0.5 if c < 2 else 1.0))
                    jobs["naqk"].append((c * P, P, "F", seg, (naqT if c < 2 else nakT)[:, c % 2, seg],
                                         DH ** -0.5 if c < 2 else 1.0))
            for d in range(2):
                for seg in (LAT, CX):
                    jobs["ga"].append((RANK * d, RANK, "F", seg, aT[0:RANK, d, seg], 1.0))
            for t in range(NT):
                jobs["gv"].append((0, 512, "T", t, g_v[:, t, :], 1.0))
                if t in q_tiles(l):
                    jobs["og"].append((0, 512, "T", t, g_og[:, t, :], 1.0))
                jobs["navdq"].append((0, 256, "T", t, nav[:, t, :], 1.0))
                if t in q_tiles(l):
                    jobs["navdq"].append((256, 256, "T", t, dqb[:, t, 0:QR], 1.0))
                jobs["dkv"].append((0, 160, "T", t, dqb[:, t, QR:DMLA], 1.0))
            return jobs

        WIDTH = {"gqk": 512, "ga": 32, "gv": 512, "og": 512, "naqk": 512, "navdq": 512, "dkv": 160}
        ORDER = ("gqk", "ga", "gv", "og", "naqk", "navdq", "dkv")

        def first_job(l, name):
            js = projections(l)
            return sum(len(js[g]) for g in ORDER[:ORDER.index(name)])

        def last_job(l, name):
            return first_job(l, name) + len(projections(l)[name])

        cst_in, x_in = sem("cst_in"), sem("x_in")
        ring_in = [sem("ring_in0"), sem("ring_in1")]
        ada_used = sem("ada_used")
        vec_in, small_in, mla_in = sem("vec_in"), sem("small_in"), sem("mla_in")
        rpb_landed, rpb_flat, bias_in = sem("rpb_landed"), sem("rpb_flat"), sem("bias_in")
        rpb_padded, bias_ready = sem("rpb_padded"), sem("bias_ready")
        vecs_up, vecs_ok = sem("vecs_up"), sem("vecs_ok")
        silu_ok, mod_ok = sem("silu_ok"), sem("mod_ok")
        nrm_ss, nrm_ms, nrm_root = sem("nrm_ss"), sem("nrm_ms"), sem("nrm_root")
        xn_ok = sem("xn_ok")
        hl_up, hc_up, h_lat, h_ctx = sem("hl_up"), sem("hc_up"), sem("h_lat"), sem("h_ctx")
        proj_up, proj_act, proj_dve = sem("proj_up"), sem("proj_act"), sem("proj_dve")
        z_up, z_act, z_dve = sem("z_up"), sem("z_act"), sem("z_dve")
        sp_ok = sem("sp_ok")
        g_scan, g_exp, ke_ok, ke_up, ke_tok_ok = (sem("g_scan"), sem("g_exp"), sem("ke_ok"), sem("ke_up"),
                                                  sem("ke_tok_ok"))
        kv_up, state_ok = sem("kv_up"), sem("state_ok")
        a_up, a_ok, go_up, go_copied, go_ok, goT_up, goT_ok = (
            sem("a_up"), sem("a_ok"), sem("go_up"), sem("go_copied"), sem("go_ok"), sem("goT_up"),
            sem("goT_ok"))
        og_silu, go_ms, go_root = sem("og_silu"), sem("go_ms"), sem("go_root")
        s_up, s_max, s_exp = [sem(n) for n in ("s_up", "s_max", "s_exp")]
        p_up, p_act, p_dve = [sem(n) for n in ("p_up", "p_act", "p_dve")]
        o_up, o_ok, oT_up, oT_ok = [sem(n) for n in ("o_up", "o_ok", "oT_up", "oT_ok")]
        mla_ss, mla_ms, mla_root, mla_n = sem("mla_ss"), sem("mla_ms"), sem("mla_root"), sem("mla_n")
        mlaT_up, mlaT_ok = sem("mlaT_up"), sem("mlaT_ok")
        qkT_dve = sem("qkT_dve")
        qk_up, q_nope, qk_tok, qkT_up, qkT_act = (sem("qk_up"), sem("q_nope"), sem("qk_tok"), sem("qkT_up"),
                                                 sem("qkT_act"))
        wbr_in, wout_in = sem("wbr_in"), sem("wout_in")
        m_up, m_sig, m_ok = sem("m_up"), sem("m_sig"), sem("m_ok")
        diag_ok, grow_up, grow_ok = sem("diag_ok"), sem("grow_up"), sem("grow_ok")
        y_up, y_ok = sem("y_up"), sem("y_ok")
        lg_up, aff_exp, aff_sh, aff_ok, affT_up, top_ok, slot_up, slot_ok = (
            sem("lg_up"), sem("aff_exp"), sem("aff_sh"), sem("aff_ok"), sem("affT_up"), sem("top_ok"),
            sem("slot_up"), sem("slot_ok"))
        ex_in = [sem(f"ex_in{i}") for i in range(6)]
        sel_ok, selT_up, selT_ok = sem("sel_ok"), sem("selT_up"), sem("selT_ok")
        xg_up, xg_act, xg_dve = sem("xg_up"), sem("xg_act"), sem("xg_dve")
        gu_up, gu_silu, hid_ok = sem("gu_up"), sem("gu_silu"), sem("hid_ok")
        hidT_up, hidT_act, hidT_dve = sem("hidT_up"), sem("hidT_act"), sem("hidT_dve")
        ye_up, ye_ok, sc_up, x_ok = sem("ye_up"), sem("ye_ok"), sem("sc_up"), sem("x_ok")
        fin_in, fin_ok, stored = sem("fin_in"), sem("fin_ok"), sem("stored")
        dve_own, act_own = sem("dve_own"), sem("act_own")
        turn_own = sem("turn_own")
        started = sem("started")

        NJ = [sum(len(v) for v in projections(l).values()) for l in range(DEPTH)]
        NSEG = [len(segments(l)) for l in range(DEPTH)]
        NQ = [len(q_tiles(l)) for l in range(DEPTH)]
        UNITS = [H * n for n in NQ]
        NORMS = [n for l in range(DEPTH) for n in (NT, NQ[l])] + [SEQ // P]
        CTX_NORMS = [n for l in range(DEPTH) for n in (1, NSEG[l] - 1)]

        def col(row):
            return vT[:, row:row + 1]

        def moe_done(l):
            return E // GE * 2 * NQ[l]

        def ring_count(n):
            return 16 * sum(3 if i % RL >= R_AT["m"] else 1 for i in range(n % 2, n + 1, 2))

        def tile(t):
            return slice(t * P, (t + 1) * P)

        def jobs_done(eng, l, name):
            n = last_job(l, name)
            eng.wait_ge(proj_act, before("proj_act", l) + (n + 1) // 2)
            eng.wait_ge(proj_dve, before("proj_dve", l) + n // 2)

        def units(l):
            return [(h, t) for h in range(H) for t in q_tiles(l)]

        def order(d):
            c = list(range(CTX // C)), list(range(CTX // C, NCH))
            return c[0] + c[1] if d == 0 else c[0][::-1] + c[1][::-1]

        KV_STEPS = NCH - 1

        def before(name, l):
            if name in ATTENTION:
                return sum(ATTENTION[name](i // 2) for i in range(l))
            return sum(COUNTS[name](i) if callable(COUNTS[name]) else COUNTS[name] for i in range(l))

        ATTENTION = {n: lambda l: UNITS[l] for n in ("s_up", "s_max", "s_exp", "p_up", "p_dve", "o_up", "o_ok")}
        ATTENTION |= {"p_act": lambda l: H * (NT - CT), "oT_up": lambda l: NQ[l], "oT_ok": lambda l: NQ[l]}
        TURNS = E // GE
        COUNTS = {
            "vec_in": 160, "small_in": 48, "mla_in": 32, "rpb_landed": 16, "rpb_flat": 16, "bias_in": 128,
            "wbr_in": 48, "wout_in": 16,
            "proj_up": lambda l: NJ[l], "proj_act": lambda l: (NJ[l] + 1) // 2, "proj_dve": lambda l: NJ[l] // 2,
            "z_up": 8, "z_act": 8, "z_dve": 8, "sp_ok": 4, "g_scan": 4, "g_exp": 8, "ke_ok": 4, "ke_up": 8, "ke_tok_ok": 8,
            "kv_up": 2 * KV_STEPS, "state_ok": 2 * KV_STEPS, "go_copied": lambda l: 2 * NQ[l],
            "mla_n": NT, "mlaT_up": lambda l: 2 * NSEG[l] + 2, "mlaT_ok": lambda l: 2 * NSEG[l] + 2,
            "qk_up": NT, "q_nope": NT, "qk_tok": NT, "qkT_up": NT, "qkT_act": lambda l: NQ[l], "qkT_dve": NT,
            "y_up": lambda l: 2 * NQ[l], "y_ok": lambda l: 2 * NQ[l],
            "sel_ok": TURNS, "selT_up": lambda l: TURNS * (1 + NSEG[l]), "selT_ok": lambda l: TURNS * (1 + NSEG[l]),
            "xg_up": 8 * TURNS, "xg_act": 4 * TURNS, "xg_dve": 4 * TURNS, "gu_up": 4 * E, "gu_silu": 2 * E, "hid_ok": 2 * E,
            "hidT_up": 2 * E, "hidT_act": E, "hidT_dve": E, "ye_up": 2 * E, "ye_ok": 2 * E, "turn_own": 3 * TURNS,
            "sc_up": lambda l: 2 * TURNS * NQ[l], "x_ok": lambda l: 2 * TURNS * NQ[l],
        }
        COUNTS |= {n: 1 for n in ("rpb_padded", "vecs_up", "vecs_ok", "silu_ok", "mod_ok", "mla_ss", "mla_ms",
                                  "mla_root", "lg_up", "aff_exp", "aff_sh", "aff_ok", "affT_up", "top_ok", "slot_up",
                                  "slot_ok")}
        COUNTS |= {n: lambda l: UNITS[l] for n in ("a_up", "a_ok", "go_up")}
        COUNTS |= {n: lambda l: NQ[l] for n in ("go_ok", "goT_up", "goT_ok", "og_silu", "go_ms", "go_root")}
        COUNTS |= {n: lambda l: 24 * NSEG[l] for n in ("m_up", "m_sig", "m_ok")}
        COUNTS |= {n: lambda l: 4 * NSEG[l] for n in ("diag_ok", "grow_up", "grow_ok")}

        block = ctx.enter_context(nc.Block())


        @block.sync
        def _(sp):
            sp.dma_start(cst[:, :], a["constants"]).then_inc(cst_in, 16)
            sp.dma_start(x_sb[:, 0:CT, :], a["ctx"][0].rearrange("(t p) d -> p t d", p=P)).then_inc(x_in, 16)
            sp.dma_start(x_sb[:, CT:NT, :], a["x"][0].rearrange("(t p) d -> p t d", p=P)).then_inc(x_in, 16)

            def slot_read(l, i):
                kind, what = ring_loads(l)[i]
                if kind == "ada":
                    sp.wait_ge(ada_used, 12 * l + i + 1)
                elif kind == "m":
                    sp.wait_ge(m_up, before("m_up", l) + 3 * NSEG[l] * (what + 1))
                else:
                    sp.wait_ge(proj_up, before("proj_up", l) + last_job(l, kind))

            def expert_loads(l, g, first):
                for j in range(GE):
                    for i, (name, half) in enumerate((("moe_w_gate", 0), ("moe_w_up", 0), ("moe_w_gate", 1),
                                                      ("moe_w_up", 1), ("moe_w_down", 0), ("moe_w_down", 1))):
                        if not first or j:
                            if i < 4:
                                sp.wait_ge(gu_up, g * (4 * GE) + (before("gu_up", l) + 4 * (j - 1) + i + 1))
                            else:
                                sp.wait_ge(ye_up, g * (2 * GE) + (before("ye_up", l) + 2 * (j - 1) + i - 3))
                        src = a[name][l, bass.ds(g * GE + j, 1), :, 512 * half:512 * half + 512]
                        sp.dma_start(ex[i], src.rearrange("e (k p) n -> p (e k) n", p=P)).then_inc(ex_in[i], 16)

            for l in range(DEPTH):
                for i, (kind, what) in enumerate(ring_loads(l)):
                    n = l * RL + i
                    if i >= 2:
                        slot_read(l, i - 2)
                    if l and i == 0:
                        sp.wait_ge(x_ok, before("x_ok", l - 1) + moe_done(l - 1))
                    if kind == "m":
                        for b in range(3):
                            c0 = O_M + b * D + what * P
                            sp.dma_start(ring_view(n, 3 * P)[:, :, b * P:(b + 1) * P],
                                         a["w_in"][l][:, c0:c0 + P].rearrange("(k p) n -> p k n", p=P)
                                         ).then_inc(ring_in[n % 2], 16)
                    else:
                        sp.dma_start(ring_view(n, what.shape[1]), what.rearrange("(k p) n -> p k n", p=P)
                                     ).then_inc(ring_in[n % 2], 16)
                sp.wait_ge(y_ok, before("y_ok", l) + 2 * NQ[l])
                expert_loads(l, 0, True)
                with sp.Fori(1, TURNS) as g:
                    expert_loads(l, g, False)
            sp.wait_ge(fin_ok, SEQ // P)
            sp.dma_start(out[0].rearrange("(t p) d -> p t d", p=P), fin).then_inc(stored, 16)
            sp.wait_ge(stored, 16)

        @block.gpsimd
        def _(pool):
            nc.gpsimd.memset(mst[:, :, :], 1.0).then_inc(started, 1)
            for l in range(DEPTH):
                if l:
                    pool.wait_ge(x_ok, before("x_ok", l - 1) + moe_done(l - 1))
                rows = ((R_AB, 48, a["ada_b"][l]), (R_N1, 8, a["norm1"][l]), (R_N2, 8, a["norm2"][l]), (R_C, 8, a["c"][0]),
                        (R_CC, 8, a["c_ctx"]), (R_QN, 2, a["mla_q_norm"][l]), (R_KVN, 1, a["mla_kv_norm"][l]),
                        (R_ON, 1, a["gla_o_norm"][l]), (R_BF, 2, a["gla_b_af"][l]), (R_BB, 2, a["gla_b_ab"][l]))
                for r, n, src in rows:
                    pool.dma_start(vecs[r:r + n, :], src.rearrange("(r c) -> r c", c=P)).then_inc(vec_in, 16)
                pool.dma_start(router[:, :, :], a["moe_router"][l].rearrange("(k p) e -> p k e", p=P)
                               ).then_inc(small_in, 16)
                for d, name in enumerate(("gla_w_af", "gla_w_ab")):
                    pool.dma_start(w_decay[0:RANK, d, :], a[name][l]).then_inc(small_in, 16)
                pool.dma_start(rpb_in[0:H * 15, :], a["na_rpb"][l].rearrange("h r c -> (h r) c")).then_inc(rpb_landed, 16)
                pool.wait_ge(rpb_padded, before("rpb_padded", l) + 1)
                pool.dma_start(rpb_scratch[l], rpb_pad[0:H * 15, :]).then_inc(rpb_flat, 16)
                pool.wait_ge(rpb_flat, before("rpb_flat", l) + 16)
                pool.wait_ge(goT_ok, before("goT_ok", l) + NQ[l])
                for half in range(2):
                    for h in range(H):
                        src = bass.AP(rpb_scratch[l].tensor, (h * 15 + 1 - half) * PADW, [[1, 64], [PADW, 14], [1, 64]])
                        pool.dma_start(bias_raw[64 * half:64 * half + 64, h, :, :], src).then_inc(bias_in, 16)
                pool.dma_start(w_uq, a["mla_w_uq"][l].rearrange("(k p) n -> p k n", p=P)).then_inc(mla_in, 16)
                pool.dma_start(w_ukv, a["mla_w_ukv"][l]).then_inc(mla_in, 16)
                pool.wait_ge(oT_ok, before("oT_ok", 2 * l + 1) + NQ[l])
                at = 0
                for name, rows in (("w_br_a", 2), ("w_br_b", 2), ("w_br_c", 4)):
                    pool.dma_start(w_br[:, at:at + rows, :], a[name][l].rearrange("(k p) n -> p k n", p=P)
                                   ).then_inc(wbr_in, 16)
                    at += rows
                pool.dma_start(w_out, a["w_out"][l].rearrange("(k p) n -> p k n", p=P)).then_inc(wout_in, 16)
            pool.wait_ge(x_ok, before("x_ok", DEPTH - 1) + moe_done(DEPTH - 1))
            fn = a["final_norm"]
            pool.dma_start(fin_row, bass.AP(fn.tensor, fn.offset, [[0, P], [1, D]])).then_inc(fin_in, 16)

        @block.tensor
        def _(pe):
            mm, tr = nc.tensor.matmul, nc.tensor.transpose

            def ring_entry(l, name, width, j=0):
                n = l * RL + R_AT[name] + j
                pe.wait_ge(ring_in[n % 2], ring_count(n))
                return ring_view(n, width)

            def project(l, name):
                w = ring_entry(l, name, WIDTH[name])
                jobs = projections(l)[name]
                for i, (c0, width, kind, where, _, _) in enumerate(jobs):
                    n = first_job(l, name) + i
                    if n >= 4:
                        pe.wait_ge((proj_act, proj_dve)[n % 2], before(("proj_act", "proj_dve")[n % 2], l) + (n - 4) // 2 + 1)
                    for k in range(KD):
                        if kind == "F":
                            size = where.stop - where.start
                            last = mm(ps[n % 4][0:width, 0:size], w[:, k, c0:c0 + width], hT[:, k, where],
                                      start=k == 0, stop=k == KD - 1)
                        else:
                            last = mm(ps[n % 4][:, 0:width], hT[:, k, tile(where)], w[:, k, c0:c0 + width],
                                      start=k == 0, stop=k == KD - 1)
                    last.then_inc(proj_up, 1)

            def norm_transposes(l, i):
                s = 2 * l + i
                xn = (xn1, xn2)[i]
                pe.wait_ge(xn_ok, sum(NORMS[:s + 1]))
                for k in range(KD):
                    if k >= 2:
                        pe.wait_ge(h_lat, KD * s + k - 1)
                    for t in range(CT, NT):
                        last = tr(ps[2 + k % 2][:, tile(t - CT)], xn[:, t, tile(k)], ident)
                    last.then_inc(hl_up, 1)
                    if CTX_NORMS[s]:
                        if k >= 2:
                            pe.wait_ge(h_ctx, KD * sum(CTX_NORMS[:s]) + k - 1)
                        for t in range(CT):
                            last = tr(ps[4 + k % 2][:, tile(t)], xn[:, t, tile(k)], ident)
                        last.then_inc(hc_up, 1)
                pe.wait_ge(h_lat, KD * (s + 1))
                pe.wait_ge(h_ctx, KD * sum(CTX_NORMS[:s + 1]))

            def modulation(l):
                pe.wait_ge(cst_in, 16)
                pe.wait_ge(vec_in, before("vec_in", l) + 160)
                if l:
                    pe.wait_ge(x_ok, before("x_ok", l - 1) + moe_done(l - 1))
                tr(ps[1][:, 0:R_ALL], vecs[0:R_ALL, :], ident[0:R_ALL, 0:R_ALL]).then_inc(vecs_up, 1)
                pe.wait_ge(silu_ok, before("silu_ok", l) + 1)
                for j in range(12):
                    w = ring_entry(l, "ada", 512, j)
                    for c in range(4):
                        m = 4 * j + c
                        for k in range(KD):
                            last = mm(ps[0][:, 2 * m:2 * m + 2], w[:, k, tile(c)], silc[:, :, k], start=k == 0, stop=k == KD - 1)
                    last.then_inc(ada_used, 1)

            def gates(l):
                jobs_done(pe, l, "gv")
                pe.wait_ge(small_in, before("small_in", l) + 48)
                for u in range(4):
                    d, kt = u // 2, u % 2
                    for i, seg in enumerate((LAT, CX)):
                        if u >= 2:
                            pe.wait_ge(z_dve, before("z_dve", l) + 2 * (u - 2) + i + 1)
                        mm(ps[4 + 2 * (u % 2) + i][:, 0:seg.stop - seg.start], w_decay[0:RANK, d, tile(kt)],
                           aT[0:RANK, d, seg], start=True, stop=True).then_inc(z_up, 1)
                    if u:
                        keys_end(l, u - 1)
                keys_end(l, 3)

            def keys_end(l, u):
                pe.wait_ge(ke_ok, before("ke_ok", l) + u + 1)
                if u:
                    pe.wait_ge(ke_tok_ok, before("ke_tok_ok", l) + 2 * u)
                for t in range(CT, NT):
                    last = tr(ps[0][:, tile(t - CT)], k_end[:, tile(t)], ident)
                last.then_inc(ke_up, 1)
                for t in range(CT):
                    last = tr(ps[1][:, tile(t)], k_end[:, tile(t)], ident)
                last.then_inc(ke_up, 1)

            def chunk_states(l):
                pe.wait_ge(ke_tok_ok, before("ke_tok_ok", l) + 8)
                pe.wait_ge(z_dve, before("z_dve", l) + 8)
                for i in range(KV_STEPS):
                    for d in range(2):
                        c = order(d)[i]
                        t, r = c // 2, C * (c % 2)
                        bank = ps[4 + 2 * d + i % 2]
                        if i >= 2:
                            pe.wait_ge(state_ok, before("state_ok", l) + 2 * (i - 2) + d + 1)
                        for h in range(H):
                            last = mm(bank[64 * (h % 2):64 * (h % 2) + 64, tile(h // 2)],
                                      ke_tok[r:r + C, d, t, 64 * h:64 * h + 64], g_v[r:r + C, t, h * DV:(h + 1) * DV],
                                      start=True, stop=True)
                        last.then_inc(kv_up, 1)

            def gla_outputs(l):
                tiles = q_tiles(l)
                jobs_done(pe, l, "og")
                pe.wait_ge(state_ok, before("state_ok", l) + 2 * KV_STEPS)

                def scores(u):
                    t, h = tiles[u // H], u % H
                    r = 64 * (h % 2)
                    if u >= 2:
                        pe.wait_ge(a_ok, before("a_ok", l) + u - 1)
                    for d in range(2):
                        last = mm(ps[u % 2][:, tile(d)], kd[r:r + 64, d, h // 2, tile(t)], qd[r:r + 64, d, h // 2, tile(t)],
                                  start=True, stop=True)
                    last.then_inc(a_up, 1)

                def values(u):
                    ti, h = u // H, u % H
                    t, r = tiles[ti], 64 * (h % 2)
                    o = ps[2 + 2 * (ti % 2) + h % 2]
                    if h == 0 and ti >= 2:
                        pe.wait_ge(go_copied, before("go_copied", l) + 2 * (ti - 1))
                    pe.wait_ge(a_ok, before("a_ok", l) + u + 1)
                    mm(o[:, tile(h // 2)], a_sum[:, u % 2, :], g_v[:, t, h * DV:(h + 1) * DV], start=True, stop=False,
                       skip_group_check=True)
                    for c in range(2):
                        for d in range(2):
                            last = mm(o[C * c:C * c + C, tile(h // 2)], qd[r:r + 64, d, h // 2, t * P + C * c:t * P + C * c + C],
                                      states[r:r + 64, d, 2 * t + c, h // 2, :], start=False, stop=True, skip_group_check=True)
                    last.then_inc(go_up, 1)

                def turn(ti):
                    pe.wait_ge(go_ok, before("go_ok", l) + ti + 1)
                    if ti >= 2:
                        pe.wait_ge(goT_ok, before("goT_ok", l) + ti - 1)
                    for h in range(H):
                        last = tr(ps[6 + ti % 2][:, tile(h)], g_o[:, ti % 2, h, :], ident)
                    last.then_inc(goT_up, 1)

                n = H * len(tiles)
                for u in range(n + 1):
                    if u < n:
                        scores(u)
                    if u >= 1:
                        values(u - 1)
                    if u > H and u % H == 3:
                        turn(u // H - 1)
                turn(len(tiles) - 1)
                pe.wait_ge(goT_ok, before("goT_ok", l) + len(tiles))

            def attention(l, i):
                idx = 2 * l + i
                us = units(l)
                n = len(us)
                lats = [sum(1 for h, t in us[:u + 1] if t >= CT) for u in range(n)]

                def scores(u):
                    h, t = us[u]
                    if i == 0:
                        r = 64 * (h % 2)
                        q, kk = naqT[r:r + 64, h // 2, tile(t)], nakT[r:r + 64, h // 2, :]
                    else:
                        q, kk = qT[0:DQK, h, tile(t)], kT[0:DQK, h, :]
                    if u >= 2:
                        pe.wait_ge(s_exp, before("s_exp", idx) + u - 1)
                    if t >= CT:
                        mm(ps[2 * (u % 2)][:, :], q, kk[:, LAT], start=True, stop=True)
                    mm(ps[2 * (u % 2) + 1][:, 0:CTX], q, kk[:, CX], start=True, stop=True).then_inc(s_up, 1)

                def turn(u):
                    pe.wait_ge(s_exp, before("s_exp", idx) + u + 1)
                    if us[u][1] >= CT:
                        if lats[u] >= 2:
                            pe.wait_ge(p_act, before("p_act", idx) + lats[u] - 1)
                        for t in range(CT, NT):
                            tr(ps[4][:, tile(t - CT)], prob[:, u % 2, tile(t)], ident)
                    if u:
                        pe.wait_ge(p_dve, before("p_dve", idx) + u)
                    for t in range(CT):
                        last = tr(ps[5][:, tile(t)], prob[:, u % 2, tile(t)], ident)
                    last.then_inc(p_up, 1)

                def values(u):
                    h, t = us[u]
                    if t >= CT:
                        pe.wait_ge(p_act, before("p_act", idx) + lats[u])
                    pe.wait_ge(p_dve, before("p_dve", idx) + u + 1)
                    if u >= 2:
                        pe.wait_ge(o_ok, before("o_ok", idx) + u - 1)
                    keys = range(NT if t >= CT else CT)
                    for kt in keys:
                        v = nav[:, kt, 64 * h:64 * h + 64] if i == 0 else mv[:, kt, h, :]
                        last = mm(ps[6 + u % 2][:, 0:64], probT[:, u % 2, kt, :], v, start=kt == 0, stop=kt == keys[-1])
                    last.then_inc(o_up, 1)

                for u in range(n + 2):
                    if u < n:
                        scores(u)
                    if 1 <= u <= n:
                        turn(u - 1)
                    if u >= 2:
                        values(u - 2)
                pe.wait_ge(o_ok, before("o_ok", idx) + n)
                for ti, t in enumerate(q_tiles(l)):
                    if ti >= 2:
                        pe.wait_ge(oT_ok, before("oT_ok", idx) + ti - 1)
                    for k in range(2):
                        last = tr(ps[4 + ti % 2][:, tile(k)], o_tok[:, t, tile(k)], ident)
                    last.then_inc(oT_up, 1)
                pe.wait_ge(oT_ok, before("oT_ok", idx) + NQ[l])

            def latent_heads(l):
                pe.wait_ge(mla_n, before("mla_n", l) + NT)
                n = 0
                for f in range(3):
                    for seg in ((LAT, CX) if f == 2 else segments(l)):
                        if n >= 4:
                            pe.wait_ge(mlaT_ok, before("mlaT_ok", l) + n - 3)
                        tiles = range(CT, NT) if seg is LAT else range(CT)
                        for t in tiles:
                            last = tr(ps[n % 4][:, tile(t - tiles[0])], dqb[:, t, tile(f)], ident)
                        last.then_inc(mlaT_up, 1)
                        n += 1
                pe.wait_ge(mlaT_ok, before("mlaT_ok", l) + n)
                pe.wait_ge(mla_in, before("mla_in", l) + 32)

                def up(t):
                    if t >= 2:
                        pe.wait_ge(qk_tok, before("qk_tok", l) + t - 1)
                    if t in q_tiles(l):
                        for k in range(2):
                            mm(ps[4 + 2 * (t % 2)][:, 0:H * DQK], dqnT[:, k, tile(t)], w_uq[:, k, :], start=k == 0, stop=k == 1)
                    mm(ps[5 + 2 * (t % 2)][:, :], dkvnT[:, tile(t)], w_ukv, start=True, stop=True).then_inc(qk_up, 1)

                def turn(t):
                    pe.wait_ge(qk_tok, before("qk_tok", l) + t + 1)
                    if t in q_tiles(l):
                        if t > q_tiles(l)[0]:
                            pe.wait_ge(qkT_act, before("qkT_act", l) + t - q_tiles(l)[0])
                        for h in range(H):
                            tr(ps[0][0:DQK, tile(h)], q_tok[:, h, :], ident)
                    if t:
                        pe.wait_ge(qkT_dve, before("qkT_dve", l) + t)
                    for h in range(H):
                        last = tr(ps[1][0:DQK, tile(h)], k_tok[:, h, :], ident)
                    last.then_inc(qkT_up, 1)

                up(0)
                for t in range(NT):
                    if t + 1 < NT:
                        up(t + 1)
                    turn(t)
                pe.wait_ge(qkT_act, before("qkT_act", l) + NQ[l])
                pe.wait_ge(qkT_dve, before("qkT_dve", l) + NT)

            def merge(l):
                pe.wait_ge(wbr_in, before("wbr_in", l) + 48)
                q = 0
                for j in range(KD):
                    w = ring_entry(l, "m", 3 * P, j)
                    for seg in segments(l):
                        size = seg.stop - seg.start
                        for b, kts in enumerate(((0, 1), (2, 3), (4, 5, 6, 7))):
                            if q >= 4:
                                pe.wait_ge(m_ok, before("m_ok", l) + q - 3)
                            for k in range(KD):
                                mm(ps[2 * (q % 4)][:, 0:size], w[:, k, tile(b)], hT[:, k, seg], start=k == 0, stop=k == KD - 1)
                            for k in kts:
                                last = mm(ps[2 * (q % 4) + 1][:, 0:size], w_br[:, k, tile(j)], oT[:, k, seg],
                                          start=k == kts[0], stop=k == kts[-1])
                            last.then_inc(m_up, 1)
                            q += 1
                pe.wait_ge(m_ok, before("m_ok", l) + q)
                for n in range(4 * NSEG[l]):
                    pe.wait_ge(diag_ok, before("diag_ok", l) + n + 1)
                    if n >= 2:
                        pe.wait_ge(grow_ok, before("grow_ok", l) + n - 1)
                    mm(ps[n % 2][:, :], ones, diag.rearrange("p a b -> p (a b)"), start=True, stop=True).then_inc(grow_up, 1)
                pe.wait_ge(wout_in, before("wout_in", l) + 16)
                q = 0
                for t in q_tiles(l):
                    for half in range(2):
                        if q >= 4:
                            pe.wait_ge(y_ok, before("y_ok", l) + q - 3)
                        for k in range(KD):
                            last = mm(ps[2 + q % 4][:, :], yT[:, k, tile(t)], w_out[:, k, 512 * half:512 * half + 512],
                                      start=k == 0, stop=k == KD - 1)
                        last.then_inc(y_up, 1)
                        q += 1
                pe.wait_ge(y_ok, before("y_ok", l) + q)
                pe.wait_ge(grow_ok, before("grow_ok", l) + 4 * NSEG[l])

            def route(l):
                for t in q_tiles(l):
                    for k in range(KD):
                        last = mm(ps[0][:, t * E:(t + 1) * E], hT[:, k, tile(t)], router[:, k, :], start=k == 0, stop=k == KD - 1)
                last.then_inc(lg_up, 1)
                pe.wait_ge(aff_ok, before("aff_ok", l) + 1)
                for t in q_tiles(l):
                    bank, at = (ps[1], t - CT) if t >= CT else (ps[2], t)
                    last = tr(bank[0:E, tile(at)], aff[:, t, :], ident)
                last.then_inc(affT_up, 1)
                pe.wait_ge(top_ok, before("top_ok", l) + 1)
                for t in q_tiles(l):
                    last = tr(ps[3][:, t * E:(t + 1) * E], slotT[0:E, tile(t)], ident[0:E, 0:E])
                last.then_inc(slot_up, 1)

            def experts(l):
                has_ctx = NSEG[l] - 1
                rows = CAPL + CAPC * has_ctx
                ns = 2 + has_ctx
                nq = 2 * NQ[l]
                with pe.Fori(0, E // GE) as g:
                    pe.wait_ge(sel_ok, before("sel_ok", l) + g + 1)
                    for dt in range(KD):
                        if dt >= 2:
                            pe.wait_ge((xg_act, xg_dve)[dt % 2], before("xg_act", l) + g * 4 + ((dt - 2) // 2 + 1))
                        bank = ps[4 + dt % 2]
                        for t in range(4):
                            last = mm(bank[:, 0:GE * CAPL], xn2[:, CT + t, tile(dt)], sel_l[:, t, :, :].rearrange("p a b -> p (a b)"),
                                      start=t == 0, stop=t == 3)
                        for t in range(CT * has_ctx):
                            last = mm(bank[:, GE * CAPL:GE * (CAPL + CAPC)], xn2[:, t, tile(dt)],
                                      sel_c[:, t, :, :].rearrange("p a b -> p (a b)"), start=t == 0, stop=t == CT - 1)
                        last.then_inc(xg_up, 1)
                    for p in range(2):
                        for t in range(4):
                            last = tr(ps[6 + p][:, tile(t)], selw_l[:, t, 2 * p:2 * p + 2, :].rearrange("p a b -> p (a b)"), ident)
                        last.then_inc(selT_up, 1)
                    if has_ctx:
                        for t in range(CT):
                            last = tr(ps[0][:, tile(t)], selw_c[:, t, :, :].rearrange("p a b -> p (a b)"), ident)
                        last.then_inc(selT_up, 1)
                    pe.wait_ge(xg_act, before("xg_act", l) + g * 4 + 4)
                    pe.wait_ge(xg_dve, before("xg_dve", l) + g * 4 + 4)
                    pe.wait_ge(selT_ok, before("selT_ok", l) + g * ns + ns)

                    def gate_up(j):
                        for half in range(2):
                            if j:
                                pe.wait_ge(hid_ok, before("hid_ok", l) + g * 8 + (2 * (j - 1) + half + 1))
                            for which in range(2):
                                i = 2 * half + which
                                pe.wait_ge(ex_in[i], g * (16 * GE) + 16 * (l * E + j + 1))
                                for k in range(KD):
                                    last = mm(ps[i][0:rows, :], xg[:, k, j, 0:rows], ex[i][:, k, :], start=k == 0, stop=k == KD - 1)
                                last.then_inc(gu_up, 1)

                    gate_up(0)
                    for j in range(GE):
                        if j + 1 < GE:
                            gate_up(j + 1)
                        pe.wait_ge(hid_ok, before("hid_ok", l) + g * 8 + (2 * j + 2))
                        pe.nop(nofuse=True)
                        for part_i in range(2):
                            for k in range(4):
                                last = tr(ps[4 + part_i][:, k * rows:(k + 1) * rows], hid[0:rows, tile(4 * part_i + k)],
                                          ident[0:rows, 0:rows])
                            last.then_inc(hidT_up, 1)
                        pe.wait_ge(hidT_act, before("hidT_act", l) + g * 4 + (j + 1))
                        pe.wait_ge(hidT_dve, before("hidT_dve", l) + g * 4 + (j + 1))
                        for half in range(2):
                            if j:
                                pe.wait_ge(ye_ok, before("ye_ok", l) + g * 8 + (2 * (j - 1) + half + 1))
                            pe.wait_ge(ex_in[4 + half], g * (16 * GE) + 16 * (l * E + j + 1))
                            for k in range(KD):
                                last = mm(ps[6 + half][0:rows, :], hidT[:, k, 0:rows], ex[4 + half][:, k, :],
                                          start=k == 0, stop=k == KD - 1)
                            last.then_inc(ye_up, 1)
                    pe.wait_ge(ye_ok, before("ye_ok", l) + g * 8 + 8)
                    q = 0
                    for t in q_tiles(l):
                        for half in range(2):
                            if q >= 4:
                                pe.wait_ge(x_ok, before("x_ok", l) + g * nq + (q - 3))
                            cols = slice(512 * half, 512 * half + 512)
                            if t >= CT:
                                for p in range(2):
                                    last = mm(ps[q % 4][:, :], selT_l[:, p, tile(t - CT)], ye_l[:, p, cols], start=p == 0, stop=p == 1)
                            else:
                                last = mm(ps[q % 4][:, :], selT_c[:, tile(t)], ye_c[:, cols], start=True, stop=True)
                            last.then_inc(sc_up, 1)
                            q += 1

            for l in range(DEPTH):
                modulation(l)
                norm_transposes(l, 0)
                project(l, "gqk")
                project(l, "ga")
                project(l, "gv")
                gates(l)
                chunk_states(l)
                project(l, "og")
                gla_outputs(l)
                project(l, "naqk")
                project(l, "navdq")
                project(l, "dkv")
                jobs_done(pe, l, "dkv")
                attention(l, 0)
                latent_heads(l)
                attention(l, 1)
                merge(l)
                norm_transposes(l, 1)
                route(l)
                experts(l)

        @block.scalar
        def _(act):
            do = nc.scalar.activation
            own = [0]

            def link(ins):
                own[0] += 1
                ins.then_inc(act_own, 1)
                act.wait_ge(act_own, own[0])

            def copies(l, name):
                for i, (_, width, kind, where, dst, scale) in enumerate(projections(l)[name]):
                    n = first_job(l, name) + i
                    if n % 2 == 0:
                        act.wait_ge(proj_up, before("proj_up", l) + n + 1)
                        m, size = (width, where.stop - where.start) if kind == "F" else (P, width)
                        do(dst, ps[n % 4][0:m, 0:size], ACT.Copy, scale=scale).then_inc(proj_act, 1)

            def squares(s, junk):
                t0 = NT - NORMS[s]
                for t in range(t0, NT):
                    do(junk[:, t - (CT if s == 2 * DEPTH else 0), :], x_sb[:, t, :], ACT.Square, accum_out=st[:, t:t + 1]
                       ).then_inc(nrm_ss, 1)
                act.wait_ge(nrm_ms, s + 1)
                do(st[:, 16 + t0:16 + NT], st[:, 8 + t0:8 + NT], ACT.Sqrt).then_inc(nrm_root, 1)

            def modulate(l, i):
                s = 2 * l + i
                for k in range(KD):
                    act.wait_ge(hl_up, KD * s + k + 1)
                    do(hT[:, k, LAT], ps[2 + k % 2][:, :], ACT.Identity, scale=scl[:, i, k, 0:1],
                       bias=modT[:, 24 * i + k, 0:1]).then_inc(h_lat, 1)

            def attention(l, i):
                idx = 2 * l + i
                us = units(l)
                n = len(us)

                def exps(u):
                    t = us[u][1]
                    act.wait_ge(s_max, before("s_max", idx) + u + 1)
                    if u >= 2:
                        act.wait_ge(p_up, before("p_up", idx) + u - 1)
                        act.wait_ge(o_ok, before("o_ok", idx) + u - 1)
                    c = 32 + 8 * (u % 2)
                    if t >= CT:
                        src = s_bias[:, u % 2, :] if i == 0 else ps[2 * (u % 2)][:, :]
                        do(prob[:, u % 2, LAT], src, ACT.Exp, bias=st[:, c + 2:c + 3], accum_out=st[:, c + 3:c + 4])
                    do(prob[:, u % 2, CX], ps[2 * (u % 2) + 1][:, 0:CTX], ACT.Exp, bias=st[:, c + 2:c + 3],
                       accum_out=st[:, c + 4:c + 5]).then_inc(s_exp, 1)

                def copy(u):
                    if us[u][1] < CT:
                        return
                    act.wait_ge(p_up, before("p_up", idx) + u + 1)
                    if u >= 2:
                        act.wait_ge(o_up, before("o_up", idx) + u - 1)
                    do(probT[:, u % 2, CT:NT, :].rearrange("p a b -> p (a b)"), ps[4][:, :], ACT.Copy).then_inc(p_act, 1)

                for u in range(n + 1):
                    if u < n:
                        exps(u)
                    if u >= 1:
                        copy(u - 1)

            for l in range(DEPTH):
                act.wait_ge(vecs_ok, before("vecs_ok", l) + 1)
                do(silc[:, :, :], vT[:, R_C:R_C + 16].rearrange("p (a b) -> p a b", a=2), ACT.Silu).then_inc(silu_ok, 1)
                if l == 0:
                    act.wait_ge(x_in, 32)
                    act.wait_ge(started, 1)
                else:
                    act.wait_ge(x_ok, before("x_ok", l - 1) + moe_done(l - 1))
                squares(2 * l, xn1)
                act.wait_ge(mod_ok, before("mod_ok", l) + 1)
                modulate(l, 0)
                for name in ("gqk", "ga", "gv"):
                    copies(l, name)
                for u in range(4):
                    d, kt = u // 2, u % 2
                    if u:
                        act.wait_ge(g_scan, before("g_scan", l) + u)
                    for i, seg in enumerate((LAT, CX)):
                        act.wait_ge(z_up, before("z_up", l) + 2 * u + i + 1)
                        do(softp[:, seg], ps[4 + 2 * (u % 2) + i][:, 0:seg.stop - seg.start], ACT.Abs,
                           bias=col((R_BF, R_BB)[d] + kt)).then_inc(z_act, 1)
                    act.wait_ge(z_act, before("z_act", l) + 2 * u + 2)
                    link(do(softp, softp, ACT.Exp, scale=-1.0))
                    do(softp, softp, ACT.Ln, bias=1.0).then_inc(sp_ok, 1)
                    act.wait_ge(g_scan, before("g_scan", l) + u + 1)
                    if u:
                        act.wait_ge(ke_ok, before("ke_ok", l) + u)
                    do(e_pos, b_cum, ACT.Exp, scale=1.0 / 16).then_inc(g_exp, 1)
                    do(e_neg, b_cum, ACT.Exp, scale=-1.0 / 16).then_inc(g_exp, 1)
                    for i in range(2):
                        act.wait_ge(ke_up, before("ke_up", l) + 2 * u + i + 1)
                        ts = slice(CT, NT) if i == 0 else slice(0, CT)
                        m = ts.stop - ts.start
                        do(ke_tok[:, d, ts, tile(kt)], ps[i][:, 0:m * P].rearrange("p (a b) -> p a b", a=m), ACT.Copy
                           ).then_inc(ke_tok_ok, 1)
                act.wait_ge(ke_ok, before("ke_ok", l) + 4)
                copies(l, "og")
                jobs_done(act, l, "og")
                for ti, t in enumerate(q_tiles(l)):
                    do(g_og[:, t, :], g_og[:, t, :], ACT.Silu).then_inc(og_silu, 1)
                for ti, t in enumerate(q_tiles(l)):
                    act.wait_ge(go_up, before("go_up", l) + H * ti + H)
                    if ti >= 2:
                        act.wait_ge(goT_up, before("goT_up", l) + ti - 1)
                    for odd in range(2):
                        do(g_o[:, ti % 2, odd:H:2, :], ps[2 + 2 * (ti % 2) + odd][:, 0:2 * P].rearrange("p (a b) -> p a b", a=2),
                           ACT.Copy).then_inc(go_copied, 1)
                    act.wait_ge(go_ms, before("go_ms", l) + ti + 1)
                    do(stm[:, 2, 0:H], stm[:, 1, 0:H], ACT.Sqrt).then_inc(go_root, 1)
                for name in ("naqk", "navdq", "dkv"):
                    copies(l, name)
                attention(l, 0)
                jobs_done(act, l, "dkv")
                for t in range(NT):
                    if t in q_tiles(l):
                        do(s_bias[:, t % 2, 0:QR], dqb[:, t, 0:QR], ACT.Square, accum_out=mst[:, 0, 6 + t:7 + t])
                    last = do(s_bias[:, t % 2, QR:QR + KVR], dqb[:, t, QR:QR + KVR], ACT.Square, accum_out=mst[:, 0, t:t + 1])
                    if t % 2 and t < NT - 1:
                        link(last)
                last.then_inc(mla_ss, 1)
                act.wait_ge(mla_ms, before("mla_ms", l) + 1)
                do(mst[:, 2, :], mst[:, 1, :], ACT.Sqrt).then_inc(mla_root, 1)
                n = 0
                for f in range(3):
                    for seg in ((LAT, CX) if f == 2 else segments(l)):
                        act.wait_ge(mlaT_up, before("mlaT_up", l) + n + 1)
                        dst = dkvnT[:, seg] if f == 2 else dqnT[:, f, seg]
                        do(dst, ps[n % 4][:, 0:seg.stop - seg.start], ACT.Copy, scale=col(R_QN + f)).then_inc(mlaT_ok, 1)
                        n += 1
                q0 = q_tiles(l)[0]
                for t in range(NT):
                    act.wait_ge(qk_up, before("qk_up", l) + t + 1)
                    if t:
                        act.wait_ge(qkT_up, before("qkT_up", l) + t)
                    qs = ps[4 + 2 * (t % 2)][:, 0:H * DQK].rearrange("p (h d) -> p h d", h=H)
                    kv = ps[5 + 2 * (t % 2)][:, :].rearrange("p (h d) -> p h d", h=H)
                    if t >= q0:
                        w = DH if t >= CT else DQK
                        do(q_tok[:, :, 0:w], qs[:, :, 0:w], ACT.Copy)
                    do(k_tok[:, :, 0:DH], kv[:, :, 0:DH], ACT.Copy)
                    do(mv[:, t, :, :], kv[:, :, DH:128], ACT.Copy).then_inc(q_nope, 1)
                    if t >= q0:
                        act.wait_ge(qkT_up, before("qkT_up", l) + t + 1)
                        do(qT[0:DQK, :, tile(t)], ps[0][0:DQK, :].rearrange("p (h d) -> p h d", h=H), ACT.Copy,
                           scale=DQK ** -0.5).then_inc(qkT_act, 1)
                attention(l, 1)
                q = 0
                for j in range(KD):
                    for seg in segments(l):
                        size = seg.stop - seg.start
                        for b in range(3):
                            act.wait_ge(m_up, before("m_up", l) + q + 1)
                            if q >= 2:
                                act.wait_ge(m_ok, before("m_ok", l) + q - 1)
                            do(sig[q % 2][:, 0:size], ps[2 * (q % 4)][:, 0:size], ACT.Sigmoid).then_inc(m_sig, 1)
                            q += 1
                n = 0
                for i in range(2):
                    for s in range(NSEG[l]):
                        for half in range(2):
                            act.wait_ge(grow_up, before("grow_up", l) + n + 1)
                            cols = slice(512 * half, 512 * half + 512)
                            if i == 0:
                                do(gate_row[:, s, cols], ps[n % 2][:, :], ACT.Copy).then_inc(grow_ok, 1)
                            else:
                                r = slice(0, CAPL) if s == 0 else slice(CAPL, CAPL + CAPC)
                                do(gate5[r, cols], ps[n % 2][r, :], ACT.Copy).then_inc(grow_ok, 1)
                            n += 1
                act.wait_ge(y_ok, before("y_ok", l) + 2 * NQ[l])
                squares(2 * l + 1, xn2)
                modulate(l, 1)
                act.wait_ge(aff_sh, before("aff_sh", l) + 1)
                do(aff[:, q0:NT, :], aff[:, q0:NT, :], ACT.Exp).then_inc(aff_exp, 1)
                has_ctx = NSEG[l] - 1
                rows = CAPL + CAPC * has_ctx
                ns = 2 + has_ctx
                with act.Fori(0, E // GE) as g:
                    for dt in range(0, KD, 2):
                        act.wait_ge(xg_up, before("xg_up", l) + g * KD + (dt + 1))
                        for s in range(1 + has_ctx):
                            c = slice(0, CAPL) if s == 0 else slice(CAPL, rows)
                            b = slice(GE * c.start, GE * c.stop)
                            last = do(xg[:, dt, :, c], ps[4][:, b].rearrange("p (a b) -> p a b", a=GE), ACT.Identity,
                                      scale=scl[:, 1, dt, s:s + 1], bias=modT[:, 24 + dt, s:s + 1])
                        last.then_inc(xg_act, 1)
                    for p in range(2):
                        act.wait_ge(selT_up, before("selT_up", l) + g * ns + (p + 1))
                        do(selT_l[:, p, :], ps[6 + p][:, :], ACT.Copy).then_inc(selT_ok, 1)
                    if has_ctx:
                        act.wait_ge(selT_up, before("selT_up", l) + g * ns + 3)
                        do(selT_c, ps[0][:, 0:CTX], ACT.Copy).then_inc(selT_ok, 1)

                    def silu(j):
                        for half in range(2):
                            act.wait_ge(gu_up, before("gu_up", l) + g * 16 + (4 * j + 2 * half + 1))
                            if j:
                                act.wait_ge(hid_ok, before("hid_ok", l) + g * 8 + (2 * (j - 1) + half + 1))
                            do(g_act[0:rows, half, :], ps[2 * half][0:rows, :], ACT.Silu).then_inc(gu_silu, 1)

                    silu(0)
                    for j in range(GE):
                        if j + 1 < GE:
                            silu(j + 1)
                        act.wait_ge(hidT_up, before("hidT_up", l) + g * 8 + (2 * j + 1))
                        if j:
                            act.wait_ge(ye_up, before("ye_up", l) + g * 8 + 2 * j)
                        do(hidT[:, 0:4, 0:rows], ps[4][:, 0:4 * rows].rearrange("p (a b) -> p a b", a=4), ACT.Copy
                           ).then_inc(hidT_act, 1)
            act.wait_ge(x_ok, before("x_ok", DEPTH - 1) + moe_done(DEPTH - 1))
            squares(2 * DEPTH, fin)

        @block.vector
        def _(dve):
            v = nc.vector
            own = [0]

            def link(ins):
                own[0] += 1
                ins.then_inc(dve_own, 1)
                dve.wait_ge(dve_own, own[0])

            def copies(l, name):
                for i, (_, width, kind, where, dst, scale) in enumerate(projections(l)[name]):
                    n = first_job(l, name) + i
                    if n % 2:
                        dve.wait_ge(proj_up, before("proj_up", l) + n + 1)
                        m, size = (width, where.stop - where.start) if kind == "F" else (P, width)
                        v.tensor_scalar(dst, ps[n % 4][0:m, 0:size], scale, None, ALU.mult).then_inc(proj_dve, 1)

            def root(s):
                t0 = NT - NORMS[s]
                dve.wait_ge(nrm_ss, sum(NORMS[:s + 1]))
                v.tensor_scalar(st[:, 8 + t0:8 + NT], st[:, t0:NT], 1.0 / D, EPS, ALU.mult, ALU.add).then_inc(nrm_ms, 1)
                dve.wait_ge(nrm_root, s + 1)
                link(v.reciprocal(st[:, 24 + t0:24 + NT], st[:, 16 + t0:16 + NT]))
                return t0

            def scaled(s, xn):
                for t in range(root(s), NT):
                    v.tensor_scalar(xn[:, t, :], x_sb[:, t, :], st[:, 24 + t:25 + t], None, ALU.mult).then_inc(xn_ok, 1)

            def modulate(l, i):
                s = 2 * l + i
                if CTX_NORMS[s]:
                    for k in range(KD):
                        dve.wait_ge(hc_up, KD * sum(CTX_NORMS[:s]) + k + 1)
                        v.tensor_scalar(hT[:, k, CX], ps[4 + k % 2][:, 0:CTX], scl[:, i, k, 1:2], modT[:, 24 * i + k, 1:2],
                                        ALU.mult, ALU.add).then_inc(h_ctx, 1)

            def attention(l, i):
                idx = 2 * l + i
                us = units(l)
                n = len(us)

                def maxima(u):
                    h, t = us[u]
                    dve.wait_ge(s_up, before("s_up", idx) + u + 1)
                    if u >= 2:
                        dve.wait_ge(s_exp, before("s_exp", idx) + u - 1)
                    c = 32 + 8 * (u % 2)
                    lat, cx = ps[2 * (u % 2)], ps[2 * (u % 2) + 1]
                    if t < CT:
                        v.tensor_reduce(st[:, c + 2:c + 3], cx[:, 0:CTX], AX_X, ALU.max, negate=True).then_inc(s_max, 1)
                        return
                    if i == 0:
                        r = 6 - 2 * (t - CT)
                        v.tensor_tensor_reduce(s_bias[:, u % 2, :], lat[:, :], bias[:, h, r:r + 8, :].rearrange("p a b -> p (a b)"),
                                               1.0, NEG, ALU.add, ALU.max, st[:, c:c + 1])
                    else:
                        v.reduce_max(st[:, c:c + 1], lat[:, :], AX_X)
                    link(v.reduce_max(st[:, c + 1:c + 2], cx[:, 0:CTX], AX_X))
                    v.tensor_reduce(st[:, c + 2:c + 3], st[:, c:c + 2], AX_X, ALU.max, negate=True).then_inc(s_max, 1)

                def copy(u):
                    dve.wait_ge(p_up, before("p_up", idx) + u + 1)
                    if u >= 2:
                        dve.wait_ge(o_up, before("o_up", idx) + u - 1)
                    v.tensor_copy(probT[:, u % 2, 0:CT, :].rearrange("p a b -> p (a b)"), ps[5][:, 0:CTX]).then_inc(p_dve, 1)

                def normalise(u):
                    h, t = us[u]
                    c = 32 + 8 * (u % 2)
                    dve.wait_ge(o_up, before("o_up", idx) + u + 1)
                    if t >= CT:
                        link(v.tensor_tensor(st[:, c + 5:c + 6], st[:, c + 3:c + 4], st[:, c + 4:c + 5], ALU.add))
                        link(v.reciprocal(st[:, c + 6:c + 7], st[:, c + 5:c + 6]))
                    else:
                        link(v.reciprocal(st[:, c + 6:c + 7], st[:, c + 4:c + 5]))
                    v.tensor_scalar(o_tok[:, t, 64 * h:64 * h + 64], ps[6 + u % 2][:, 0:64], st[:, c + 6:c + 7], None, ALU.mult
                                    ).then_inc(o_ok, 1)

                for u in range(n + 2):
                    if u < n:
                        maxima(u)
                    if 1 <= u <= n:
                        copy(u - 1)
                    if u >= 2:
                        normalise(u - 2)
                for ti, t in enumerate(q_tiles(l)):
                    dve.wait_ge(oT_up, before("oT_up", idx) + ti + 1)
                    v.tensor_copy(oT[:, 2 * i:2 * i + 2, tile(t)], ps[4 + ti % 2][:, 0:256].rearrange("p (a b) -> p a b", a=2)
                                  ).then_inc(oT_ok, 1)

            def turned(l, ti):
                t = q_tiles(l)[ti]
                dve.wait_ge(goT_up, before("goT_up", l) + ti + 1)
                v.tensor_scalar(oT[:, 4:8, tile(t)], ps[6 + ti % 2][:, :].rearrange("p (h n) -> p h n", h=H), col(R_ON), None,
                                ALU.mult).then_inc(goT_ok, 1)

            dve.wait_ge(cst_in, 16)
            for l in range(DEPTH):
                q0 = q_tiles(l)[0]
                dve.wait_ge(vecs_up, before("vecs_up", l) + 1)
                v.tensor_copy(vT[:, :], ps[1][:, 0:R_ALL]).then_inc(vecs_ok, 1)
                dve.wait_ge(rpb_landed, before("rpb_landed", l) + 16)
                link(v.memset(rpb_pad[0:H * 15, :], 0.0))
                v.tensor_copy(rpb_pad[0:H * 15, 48:48 + WIN], rpb_in[0:H * 15, ::-1]).then_inc(rpb_padded, 1)
                dve.wait_ge(vecs_ok, before("vecs_ok", l) + 1)
                scaled(2 * l, xn1)
                dve.wait_ge(ada_used, 12 * (l + 1))
                link(v.tensor_tensor(modT[:, :, :], ps[0][:, 0:96].rearrange("p (a b) -> p a b", b=2),
                                     vT[:, R_AB:R_AB + 48].unsqueeze(2).to_broadcast([P, 48, 2]), ALU.add))
                for i in range(2):
                    last = v.scalar_tensor_tensor(scl[:, i, :, :], modT[:, 24 * i + 8:24 * i + 16, :], 1.0,
                                                  vT[:, R_N1 + 8 * i:R_N1 + 8 * i + 8].unsqueeze(2).to_broadcast([P, KD, 2]),
                                                  ALU.add, ALU.mult)
                last.then_inc(mod_ok, 1)
                dve.wait_ge(mod_ok, before("mod_ok", l) + 1)
                modulate(l, 0)
                for name in ("gqk", "ga", "gv"):
                    copies(l, name)
                link(v.memset(scan_keep, 1.0))
                link(v.memset(scan_keep[:, 0:TOK:C], 0.0))
                for u in range(4):
                    d, kt = u // 2, u % 2
                    for i, seg in enumerate((LAT, CX)):
                        dve.wait_ge(z_act, before("z_act", l) + 2 * u + i + 1)
                        v.tensor_scalar(g_log[:, seg], ps[4 + 2 * (u % 2) + i][:, 0:seg.stop - seg.start],
                                        col((R_BF, R_BB)[d] + kt), 0.0, ALU.add, ALU.min).then_inc(z_dve, 1)
                    dve.wait_ge(z_dve, before("z_dve", l) + 2 * u + 2)
                    dve.wait_ge(sp_ok, before("sp_ok", l) + u + 1)
                    link(v.tensor_tensor(g_log, g_log, softp, ALU.subtract))
                    if u:
                        dve.wait_ge(g_exp, before("g_exp", l) + 2 * u)
                    way = slice(None, None, -1 if d else 1)
                    v.tensor_tensor_scan(b_cum[:, way], scan_keep, g_log[:, way], 0.0, ALU.mult, ALU.add).then_inc(g_scan, 1)
                    dve.wait_ge(g_exp, before("g_exp", l) + 2 * u + 2)
                    v.tensor_copy(decay[:, d, kt, :], e_pos[:, (0 if d else C - 1):TOK:C])
                    qs = slice(q0 * P, TOK)
                    v.tensor_tensor(qd[:, d, kt, qs], g_raw[:, kt, qs], e_pos[:, qs], ALU.mult)
                    link(v.tensor_tensor(kd[:, d, kt, :], g_raw[:, 2 + kt, :], e_neg, ALU.mult))
                    if u:
                        dve.wait_ge(ke_up, before("ke_up", l) + 2 * u)
                    v.tensor_tensor(k_end.rearrange("p (c n) -> p c n", n=C), kd[:, d, kt, :].rearrange("p (c n) -> p c n", n=C),
                                    decay[:, d, kt, :].unsqueeze(2).to_broadcast([P, NCH, C]), ALU.mult).then_inc(ke_ok, 1)
                for d in range(2):
                    last = v.memset(states[:, d, order(d)[0], :, :], 0.0)
                link(last)
                for i in range(KV_STEPS):
                    for d in range(2):
                        c, nxt = order(d)[i], order(d)[i + 1]
                        dve.wait_ge(kv_up, before("kv_up", l) + 2 * i + d + 1)
                        if i:
                            dve.wait_ge(state_ok, before("state_ok", l) + 2 * (i - 1) + d + 1)
                        for kt in range(2):
                            last = v.scalar_tensor_tensor(states[:, d, nxt, kt, :], states[:, d, c, kt, :],
                                                          decay[:, d, kt, c:c + 1], ps[4 + 2 * d + i % 2][:, tile(kt)],
                                                          ALU.mult, ALU.add)
                        last.then_inc(state_ok, 1)
                dve.wait_ge(ke_ok, before("ke_ok", l) + 4)
                copies(l, "og")
                for ti, t in enumerate(q_tiles(l)):
                    for h in range(H):
                        u = H * ti + h
                        dve.wait_ge(a_up, before("a_up", l) + u + 1)
                        link(v.tensor_tensor(a_mask[:, u % 2, :], ps[u % 2][:, 0:256], tri, ALU.mult))
                        if u >= 2:
                            dve.wait_ge(go_up, before("go_up", l) + u - 1)
                        v.tensor_tensor(a_sum[:, u % 2, :], a_mask[:, u % 2, 0:P], a_mask[:, u % 2, P:2 * P], ALU.add
                                        ).then_inc(a_ok, 1)
                    dve.wait_ge(go_copied, before("go_copied", l) + 2 * ti + 2)
                    o = g_o[:, ti % 2, :, :]
                    link(v.tensor_tensor(g_sq, o, o, ALU.mult))
                    link(v.tensor_reduce(stm[:, 0, 0:H], g_sq, AX_X, ALU.add))
                    v.tensor_scalar(stm[:, 1, 0:H], stm[:, 0, 0:H], 1.0 / DV, EPS, ALU.mult, ALU.add).then_inc(go_ms, 1)
                    dve.wait_ge(go_root, before("go_root", l) + ti + 1)
                    link(v.reciprocal(stm[:, 3, 0:H], stm[:, 2, 0:H]))
                    link(v.tensor_tensor(o, o, stm[:, 3, 0:H].unsqueeze(2).to_broadcast([P, H, DV]), ALU.mult))
                    dve.wait_ge(og_silu, before("og_silu", l) + ti + 1)
                    v.tensor_tensor(o, o, g_og[:, t, :].rearrange("p (h n) -> p h n", h=H), ALU.mult).then_inc(go_ok, 1)
                    if ti:
                        turned(l, ti - 1)
                turned(l, NQ[l] - 1)
                for name in ("naqk", "navdq", "dkv"):
                    copies(l, name)
                dve.wait_ge(bias_in, before("bias_in", l) + 128)
                for h in range(H):
                    last = v.tensor_tensor(bias[:, h, :, :], bias_raw[:, h, :, ::-1],
                                           window.unsqueeze(1).to_broadcast([P, 14, 64]), ALU.add)
                link(last)
                attention(l, 0)
                dve.wait_ge(mla_ss, before("mla_ss", l) + 1)
                v.tensor_scalar(mst[:, 1, 0:6], mst[:, 0, 0:6], 1.0 / KVR, EPS, ALU.mult, ALU.add)
                v.tensor_scalar(mst[:, 1, 6:12], mst[:, 0, 6:12], 1.0 / QR, EPS, ALU.mult, ALU.add).then_inc(mla_ms, 1)
                dve.wait_ge(mla_root, before("mla_root", l) + 1)
                link(v.reciprocal(mst[:, 3, :], mst[:, 2, :]))
                cosr = cst[:, K_COS:K_COS + 128].rearrange("p (t r) -> p t r", r=ROPE)
                sinr = cst[:, K_SIN:K_SIN + 128].rearrange("p (t r) -> p t r", r=ROPE)
                for t in range(NT):
                    if t >= q0:
                        v.tensor_scalar(dqb[:, t, 0:QR], dqb[:, t, 0:QR], mst[:, 3, 6 + t:7 + t], None, ALU.mult)
                    if t >= CT:
                        kr = dqb[:, t, QR + KVR:DMLA]
                        v.tensor_tensor(rot[:, 0, 0, :], kr, cosr[:, t - CT, :], ALU.mult)
                        for pair in range(2):
                            last = v.tensor_tensor(rot[:, 1, 0, :].rearrange("p (f r e) -> p f r e", f=2, r=2)[:, :, pair, :],
                                                   kr.rearrange("p (f r e) -> p f r e", f=2, r=2)[:, :, 1 - pair, :],
                                                   sinr[:, t - CT, :].rearrange("p (f r e) -> p f r e", f=2, r=2)[:, :, pair, :],
                                                   ALU.mult)
                        link(last)
                        link(v.tensor_tensor(kr, rot[:, 0, 0, :], rot[:, 1, 0, :], ALU.add))
                    v.tensor_scalar(dqb[:, t, QR:QR + KVR], dqb[:, t, QR:QR + KVR], mst[:, 3, t:t + 1], None, ALU.mult
                                    ).then_inc(mla_n, 1)
                for t in range(NT):
                    dve.wait_ge(q_nope, before("q_nope", l) + t + 1)
                    if t:
                        dve.wait_ge(qkT_up, before("qkT_up", l) + t)
                    if t >= CT:
                        qr = ps[4 + 2 * (t % 2)][:, 0:H * DQK].rearrange("p (h d) -> p h d", h=H)[:, :, DH:DQK]
                        v.tensor_tensor(rot[:, 0, :, :], qr, cosr[:, t - CT, :].unsqueeze(1).to_broadcast([P, H, ROPE]), ALU.mult)
                        for piece in range(4):
                            to, fr = 8 * piece, 8 * (piece ^ 1)
                            last = v.tensor_tensor(rot[:, 1, :, to:to + 8], qr[:, :, fr:fr + 8],
                                                   sinr[:, t - CT, to:to + 8].unsqueeze(1).to_broadcast([P, H, 8]), ALU.mult)
                        link(last)
                        v.tensor_tensor(q_tok[:, :, DH:DQK], rot[:, 0, :, :], rot[:, 1, :, :], ALU.add)
                    v.tensor_copy(k_tok[:, :, DH:DQK], dqb[:, t, QR + KVR:DMLA].unsqueeze(1).to_broadcast([P, H, ROPE])
                                  ).then_inc(qk_tok, 1)
                    dve.wait_ge(qkT_up, before("qkT_up", l) + t + 1)
                    v.tensor_copy(kT[0:DQK, :, tile(t)], ps[1][0:DQK, :].rearrange("p (h d) -> p h d", h=H)).then_inc(qkT_dve, 1)
                attention(l, 1)
                q = 0
                for j in range(KD):
                    for seg in segments(l):
                        size = seg.stop - seg.start
                        for b in range(3):
                            dve.wait_ge(m_sig, before("m_sig", l) + q + 1)
                            br = ps[2 * (q % 4) + 1][:, 0:size]
                            if b == 0:
                                v.tensor_tensor(yT[:, j, seg], sig[q % 2][:, 0:size], br, ALU.mult).then_inc(m_ok, 1)
                            else:
                                link(v.tensor_tensor(part[:, 0:size], sig[q % 2][:, 0:size], br, ALU.mult))
                                v.tensor_tensor(yT[:, j, seg], yT[:, j, seg], part[:, 0:size], ALU.add).then_inc(m_ok, 1)
                                if b == 1:
                                    dve.wait_ge(m_ok, before("m_ok", l) + q + 1)
                            q += 1
                dve.wait_ge(m_ok, before("m_ok", l) + q)
                n = 0
                for i in range(2):
                    for s in range(NSEG[l]):
                        for half in range(2):
                            if n:
                                dve.wait_ge(grow_up, before("grow_up", l) + n)
                            m0 = 24 * i + 16 + 4 * half
                            v.tensor_tensor(diag, ident.unsqueeze(1).to_broadcast([P, 4, P]),
                                            modT[:, m0:m0 + 4, s:s + 1].to_broadcast([P, 4, P]), ALU.mult).then_inc(diag_ok, 1)
                            n += 1
                dve.wait_ge(grow_ok, before("grow_ok", l) + n)
                q = 0
                for t in q_tiles(l):
                    for half in range(2):
                        cols = slice(512 * half, 512 * half + 512)
                        dve.wait_ge(y_up, before("y_up", l) + q + 1)
                        if q:
                            dve.wait_ge(y_ok, before("y_ok", l) + q)
                        link(v.tensor_tensor(part, ps[2 + q % 4][:, :], gate_row[:, 0 if t >= CT else 1, cols], ALU.mult))
                        v.tensor_tensor(x_sb[:, t, cols], x_sb[:, t, cols], part, ALU.add).then_inc(y_ok, 1)
                        q += 1
                dve.wait_ge(y_ok, before("y_ok", l) + q)
                scaled(2 * l + 1, xn2)
                modulate(l, 1)
                dve.wait_ge(lg_up, before("lg_up", l) + 1)
                nt = NT - q0
                lg = ps[0][:, q0 * E:NT * E].rearrange("p (t e) -> p t e", e=E)
                link(v.tensor_reduce(st[:, 48 + q0:48 + NT], lg, AX_X, ALU.max))
                v.tensor_tensor(aff[:, q0:NT, :], lg, st[:, 48 + q0:48 + NT].unsqueeze(2).to_broadcast([P, nt, E]), ALU.subtract
                                ).then_inc(aff_sh, 1)
                dve.wait_ge(aff_exp, before("aff_exp", l) + 1)
                link(v.tensor_reduce(st[:, 48 + q0:48 + NT], aff[:, q0:NT, :], AX_X, ALU.add))
                link(v.reciprocal(st[:, 56 + q0:56 + NT], st[:, 48 + q0:48 + NT]))
                v.tensor_tensor(aff[:, q0:NT, :], aff[:, q0:NT, :], st[:, 56 + q0:56 + NT].unsqueeze(2).to_broadcast([P, nt, E]),
                                ALU.mult).then_inc(aff_ok, 1)
                dve.wait_ge(affT_up, before("affT_up", l) + 1)
                segs = segments(l)
                for i, seg in enumerate(segs):
                    last = v.tensor_copy(work[0:E, seg], ps[1 + i][0:E, 0:seg.stop - seg.start])
                link(last)
                for i, seg in enumerate(segs):
                    for _ in range((CAPL, CAPC)[i] // 8):
                        link(v.max(top8[0:E, i, :], work[0:E, seg]))
                        link(v.match_replace(work[0:E, seg], top8[0:E, i, :], work[0:E, seg], -1.0))
                cols = slice(q0 * P, TOK)
                link(v.tensor_scalar(chosen[0:E, cols], work[0:E, cols], 0.0, None, ALU.is_lt))
                for seg in segs:
                    last = v.tensor_tensor_scan(slotT[0:E, seg], ones[0:E, 0:1].to_broadcast([E, seg.stop - seg.start]),
                                                chosen[0:E, seg], 0.0, ALU.mult, ALU.add)
                link(last)
                link(v.tensor_tensor(slotT[0:E, cols], slotT[0:E, cols], chosen[0:E, cols], ALU.mult))
                v.tensor_scalar(slotT[0:E, cols], slotT[0:E, cols], 1.0, None, ALU.subtract).then_inc(top_ok, 1)
                dve.wait_ge(slot_up, before("slot_up", l) + 1)
                v.tensor_copy(slot[:, q0:NT, :], ps[3][:, q0 * E:NT * E].rearrange("p (t e) -> p t e", e=E)).then_inc(slot_ok, 1)
                dve.wait_ge(slot_ok, before("slot_ok", l) + 1)
                has_ctx = NSEG[l] - 1
                rows = CAPL + CAPC * has_ctx
                nq = 2 * NQ[l]
                with dve.Fori(0, E // GE) as g:
                    v.tensor_copy(turn_s[:, 0, q0:NT, :], slot[:, q0:NT, bass.ds(g * GE, GE)]).then_inc(turn_own, 1)
                    v.tensor_copy(turn_s[:, 1, q0:NT, :], aff[:, q0:NT, bass.ds(g * GE, GE)]).then_inc(turn_own, 1)
                    dve.wait_ge(turn_own, before("turn_own", l) + g * 3 + 2)
                    for t in range(q0, NT):
                        dst, i, cap = (sel_l, t - CT, CAPL) if t >= CT else (sel_c, t, CAPC)
                        last = v.tensor_tensor(dst[:, i, :, :], iota[:, 0:cap].unsqueeze(1).to_broadcast([P, GE, cap]),
                                               turn_s[:, 0, t, :].unsqueeze(2).to_broadcast([P, GE, cap]), ALU.is_equal)
                    last.then_inc(turn_own, 1)
                    dve.wait_ge(turn_own, before("turn_own", l) + g * 3 + 3)
                    for t in range(q0, NT):
                        src, dst, i, cap = (sel_l, selw_l, t - CT, CAPL) if t >= CT else (sel_c, selw_c, t, CAPC)
                        last = v.tensor_tensor(dst[:, i, :, :], src[:, i, :, :],
                                               turn_s[:, 1, t, :].unsqueeze(2).to_broadcast([P, GE, cap]), ALU.mult)
                    last.then_inc(sel_ok, 1)
                    for dt in range(1, KD, 2):
                        dve.wait_ge(xg_up, before("xg_up", l) + g * KD + (dt + 1))
                        for s in range(1 + has_ctx):
                            c = slice(0, CAPL) if s == 0 else slice(CAPL, rows)
                            b = slice(GE * c.start, GE * c.stop)
                            last = v.tensor_scalar(xg[:, dt, :, c], ps[5][:, b].rearrange("p (a b) -> p a b", a=GE),
                                                   scl[:, 1, dt, s:s + 1], modT[:, 24 + dt, s:s + 1], ALU.mult, ALU.add)
                        last.then_inc(xg_dve, 1)

                    def hidden(j):
                        for half in range(2):
                            dve.wait_ge(gu_up, before("gu_up", l) + g * 16 + (4 * j + 2 * half + 2))
                            dve.wait_ge(gu_silu, before("gu_silu", l) + g * 8 + (2 * j + half + 1))
                            if j:
                                dve.wait_ge(hidT_up, before("hidT_up", l) + g * 8 + 2 * j)
                            v.tensor_tensor(hid[0:rows, 512 * half:512 * half + 512], g_act[0:rows, half, :],
                                            ps[2 * half + 1][0:rows, :], ALU.mult).then_inc(hid_ok, 1)

                    hidden(0)
                    for j in range(GE):
                        dve.wait_ge(hidT_up, before("hidT_up", l) + g * 8 + (2 * j + 2))
                        if j:
                            dve.wait_ge(ye_up, before("ye_up", l) + g * 8 + 2 * j)
                        v.tensor_copy(hidT[:, 4:8, 0:rows], ps[5][:, 0:4 * rows].rearrange("p (a b) -> p a b", a=4)
                                      ).then_inc(hidT_dve, 1)
                        if j + 1 < GE:
                            hidden(j + 1)
                        for half in range(2):
                            cols = slice(512 * half, 512 * half + 512)
                            dve.wait_ge(ye_up, before("ye_up", l) + g * 8 + (2 * j + half + 1))
                            r = 64 * (j % 2)
                            last = v.tensor_tensor(ye_l[r:r + 64, j // 2, cols], ps[6 + half][0:64, :], gate5[0:64, cols], ALU.mult)
                            if has_ctx:
                                last = v.tensor_tensor(ye_c[32 * j:32 * j + 32, cols], ps[6 + half][64:96, :], gate5[64:96, cols],
                                                       ALU.mult)
                            last.then_inc(ye_ok, 1)
                    q = 0
                    for t in q_tiles(l):
                        for half in range(2):
                            cols = slice(512 * half, 512 * half + 512)
                            dve.wait_ge(sc_up, before("sc_up", l) + g * nq + (q + 1))
                            v.tensor_tensor(x_sb[:, t, cols], x_sb[:, t, cols], ps[q % 4][:, :], ALU.add).then_inc(x_ok, 1)
                            q += 1
            dve.wait_ge(fin_in, 16)
            for t in range(root(2 * DEPTH), NT):
                v.scalar_tensor_tensor(fin[:, t - CT, :], x_sb[:, t, :], st[:, 24 + t:25 + t], fin_row, ALU.mult, ALU.mult
                                       ).then_inc(fin_ok, 1)


NAMES = ["x", "c", "ctx", "c_ctx", "ada_w", "ada_b", "norm1", "norm2", "w_in", "na_rpb", "mla_q_norm", "mla_w_uq", "mla_kv_norm",
         "mla_w_ukv", "gla_w_af", "gla_b_af", "gla_w_ab", "gla_b_ab", "gla_o_norm", "w_br_a", "w_br_b", "w_br_c", "w_out",
         "moe_router", "moe_w_gate", "moe_w_up", "moe_w_down", "final_norm"]


def kernel(**inputs):
    import concourse.bacc as bacc
    from concourse.bass_utils import run_bass_kernel_spmd

    nc = bacc.Bacc("TRN2", target_bir_lowering=False, num_devices=1)
    arrays, aps = {}, {}
    for name in NAMES + ["constants"]:
        v = constants() if name == "constants" else np.ascontiguousarray(inputs[name])
        arrays["in_" + name] = v
        aps[name] = nc.dram_tensor("in_" + name, v.shape, mybir.dt.from_np(v.dtype), kind="ExternalInput").ap()
    out = nc.dram_tensor("out", (1, SEQ, D), F32, kind="ExternalOutput").ap()
    hybrid_kernel(nc, aps, out)
    r = run_bass_kernel_spmd(nc, [arrays], core_ids=[0])
    return r.results[0]["out"]
```

```python
from contextlib import ExitStack

import numpy as np

import concourse.bass as bass
from concourse import mybir

F32 = mybir.dt.float32
F32R = mybir.dt.float32r
ALU = mybir.AluOpType
ACT = mybir.ActivationFunctionType
AX_X = mybir.AxisListType.X

P = 128
D = 1024
KD = D // P
SEQ, CTX = 512, 256
TOK = SEQ + CTX
NT = TOK // P
CT = CTX // P
DEPTH = 2
EPS = 1e-6
GRID_W = 64
H = 4
DH = 64
ROPE = 32
QR, KVR = 256, 128
DQK = DH + ROPE
DV = 128
C = 64
NCH = TOK // C
RANK = 16
E = 16
CAPL, CAPC = 2 * SEQ // E, 2 * CTX // E
GE = 4
ROWS = CAPL + CAPC
GRAIN = 4
SLOTS, HI_SLOTS = 6, 3


def turn_loads():
    gate_up = [[(j, m, half, part) for half in range(2) for m in ("gate", "up") for part in range(2)] for j in range(GE)]
    down = [[(j, "down", half, part) for half in range(2) for part in range(2)] for j in range(GE)]
    out = list(gate_up[0])
    for j in range(GE):
        out += (gate_up[j + 1] if j + 1 < GE else []) + down[j]
    return out


LOADS = turn_loads()
PER_TURN = len(LOADS)


def used(j, matrix, half):
    return SLOTS + LOADS.index((j, matrix, half, 1)) + 1


def turned_after(i):
    j, rest = LOADS[i][0], LOADS[i][1:]
    return j - 1 if j and rest == ("gate", 0, 0) else j + 1 if j == GE - 2 and rest == ("down", 1, 1) else None


NEG = -1.0e30
WIN = 31
PADW = 2 * GRID_W - 1

O_NAQK, O_NAV, O_DQ, O_DKV = 0, 512, 768, 1024
O_GQK, O_GV, O_GA, O_OG, O_M = 1184, 1696, 2208, 2240, 2752
DMLA = QR + KVR + ROPE

K_ID, K_TRI, K_IOTA, K_WIN, K_COS, K_SIN, K_ONE = 0, 128, 384, 448, 512, 640, 768
K_ALL = 896

LAT, CX = slice(CTX, TOK), slice(0, CTX)

R_AB, R_N1, R_N2, R_C, R_CC, R_QN, R_KVN, R_ON, R_BF, R_BB, R_ALL = 0, 48, 56, 64, 72, 80, 82, 83, 84, 86, 88


def constants():
    k = np.zeros((P, K_ALL), np.float32)
    k[:, K_ID:K_ID + P] = np.eye(P)
    s, t = np.arange(P)[:, None], np.arange(P)[None, :]
    same = s // C == t // C
    k[:, K_TRI:K_TRI + P] = same & (s <= t)
    k[:, K_TRI + P:K_TRI + 2 * P] = same & (s >= t)
    k[:, K_IOTA:K_IOTA + 64] = np.arange(64)
    qc = np.arange(P) % GRID_W
    start = np.clip(qc - 8, 0, GRID_W - 16)[:, None]
    kc = np.arange(GRID_W)[None, :]
    k[:, K_WIN:K_WIN + 64] = np.where((kc >= start) & (kc < start + 16), 0.0, NEG)
    inv = np.float32(10000.0) ** (-np.arange(8, dtype=np.float32) / np.float32(8))
    for tile in range(SEQ // P):
        tok = tile * P + np.arange(P)
        for half, pos in enumerate((tok // GRID_W, tok % GRID_W)):
            ang = pos.astype(np.float32)[:, None] * inv
            at = tile * ROPE + half * 16
            for pair, sign in ((0, -1.0), (1, 1.0)):
                k[:, K_COS + at + 8 * pair:K_COS + at + 8 * pair + 8] = np.cos(ang)
                k[:, K_SIN + at + 8 * pair:K_SIN + at + 8 * pair + 8] = sign * np.sin(ang)
    k[:, K_ONE:K_ONE + P] = 1.0
    return k


def hybrid_kernel(nc, a, out):
    ctx = ExitStack()
    with ctx:
        def sb(name, shape):
            return ctx.enter_context(nc.sbuf_tensor(name, shape, F32))

        def sem(name):
            return ctx.enter_context(nc.semaphore(name))

        def sems(name):
            return [sem(f"{name}{l}") for l in range(DEPTH)]

        KB = 256
        x_sb = sb("x_sb", [P, NT, D])
        oT = sb("oT", [P, KD, TOK])
        ring = sb("ring", [P, 2, 16 * KB])
        with nc.sbuf_tensor("arena", [P, 96 * KB], F32) as arena, nc.sbuf_tensor("hT", [P, KD, TOK], F32) as hT:
            pass
        def sbr(name, shape):
            return ctx.enter_context(nc.sbuf_tensor(name, shape, F32R))

        w_hi, w_lo = sbr("w_hi", [P, HI_SLOTS, GRAIN, 512]), sbr("w_lo", [P, SLOTS, GRAIN, 512])
        hidT_hi, hidT_lo = sbr("hidT_hi", [P, KD, ROWS]), sbr("hidT_lo", [P, KD, ROWS])
        xg_hi, xg_lo = sbr("xg_hi", [P, KD, GE, ROWS]), sbr("xg_lo", [P, KD, GE, ROWS])
        sb("rest_of_hT", [P, 18 * KB])
        cst = sb("cst", [P, K_ALL])
        vT = sb("vT", [P, R_ALL])
        silc = sb("silc", [P, 2, KD])
        modT = [sb(f"modT{l}", [P, 48, 2]) for l in range(DEPTH)]
        ada_row = sb("ada_row", [2, 256])
        scl = sb("scl", [P, 2, KD, 2])
        router = sb("router", [P, KD, E])
        st = sb("st", [P, 64])
        stm = sb("stm", [P, 4, 8])
        mst = sb("mst", [P, 4, 12])
        top8 = sb("top8", [P, 2, 8])
        turn_s = sb("turn_s", [P, 2, NT, GE])
        hTf = hT[:, :, :].rearrange("p a b -> p (a b)")
        oTf = oT[:, :, :].rearrange("p a b -> p (a b)")
        ringf = ring[:, :, :].rearrange("p a b -> p (a b)")

        def carve(flat, kb, *dims):
            n = int(np.prod(dims))
            v = flat[:, int(kb * KB):int(kb * KB) + n]
            if len(dims) == 1:
                return v
            names = "abcd"[:len(dims)]
            return v.rearrange(f"p ({' '.join(names)}) -> p {' '.join(names)}",
                               **{c: d for c, d in zip(names, dims)})

        ar = arena[:, :]
        ident = cst[:, K_ID:K_ID + P]
        tri = cst[:, K_TRI:K_TRI + 2 * P]
        iota = cst[:, K_IOTA:K_IOTA + 64]
        window = cst[:, K_WIN:K_WIN + 64]
        ones = cst[:, K_ONE:K_ONE + P]

        xn1 = carve(ar, 0, NT, D)
        xn2 = carve(oTf, 0, NT, D)
        vecs = carve(hTf, 22, P)
        g_v = carve(ar, 0, NT, H * DV)
        g_raw = carve(ar, 12, 4, TOK)
        g_og = carve(ar, 12, NT, H * DV)
        qd = carve(ar, 24, 2, 2, TOK)
        kd = carve(ar, 36, 2, 2, TOK)
        ke_tok = carve(ar, 48, 2, NT, 256)
        states = carve(ar, 60, 2, NCH, 2, DV)
        w_decay = carve(ar, 84, 2, 256)
        a_mask = carve(ar, 86, 2, 256)
        a_sum = carve(ar, 88, 2, P)
        g_o = carve(ar, 89, 2, H, DV)
        g_sq = carve(ar, 93, H, DV)
        softp = carve(oTf, 0, TOK)
        g_log = carve(oTf, 3, TOK)
        b_cum = carve(oTf, 6, TOK)
        e_pos = carve(oTf, 9, TOK)
        e_neg = carve(oTf, 12, TOK)
        k_end = carve(oTf, 15, TOK)
        aT = carve(oTf, 18, 2, TOK)
        scan_keep = carve(ar, 89, TOK)
        decay = sb("decay", [P, 2, 2, NCH])
        naqT, nakT = carve(ar, 0, 2, TOK), carve(ar, 6, 2, TOK)
        nav = carve(ar, 12, NT, 256)
        bias = carve(ar, 18, H, 14, 64)
        bias_raw = carve(ar, 32, H, 14, 64)
        rpb_in, rpb_pad = carve(ar, 95.5, WIN), carve(ar, 95, PADW)
        dqb = carve(ar, 46, NT, DMLA)
        dqnT, dkvnT = carve(ar, 56, 2, TOK), carve(ar, 62, TOK)
        w_uq, w_ukv = carve(ar, 65, 2, H * DQK), carve(ar, 68, H * 128)
        q_tok, k_tok = carve(ar, 70, H, DQK), carve(ar, 71.5, H, DQK)
        rot = carve(ar, 73, 2, H, ROPE)
        s_bias = carve(ar, 74, 2, SEQ)
        qT, kT = carve(ar, 0, H, TOK), carve(ar, 32, H, TOK)
        mv = carve(ar, 12, NT, H, DH)
        prob = carve(ar, 78, 2, TOK)
        probT = carve(ar, 84, 2, NT, P)
        o_tok = carve(ar, 90, NT, 256)
        yT = carve(ar, 0, KD, TOK)
        w_br = carve(ar, 24, KD, D)
        w_out = carve(ar, 56, KD, D)
        gate_row = carve(ar, 88, 2, D)
        sig = [carve(ringf, 12, SEQ), carve(ringf, 14, SEQ)]
        branch = carve(ringf, 30, SEQ)
        diag = carve(ringf, 30, 4, P)
        w_raw = [carve(ar, 24 + 8 * i, GRAIN, 512) for i in range(SLOTS)]
        work, chosen, slotT = carve(hTf, 6, TOK), carve(hTf, 9, TOK), carve(hTf, 12, TOK)
        ye_l, ye_c = carve(hTf, 6, 2, D), carve(hTf, 14, D)
        xg_sum = carve(hTf, 18, 2, GE * ROWS)
        hid = carve(ringf, 0, D)
        g_act = carve(ringf, 7, 2, 512)
        sel_l, selw_l = carve(ringf, 11, 4, GE, CAPL), carve(ringf, 15, 4, GE, CAPL)
        sel_c, selw_c = carve(ringf, 19, CT, GE, CAPC), carve(ringf, 20, CT, GE, CAPC)
        selT_l, selT_c = carve(ringf, 21, 2, SEQ), carve(ringf, 25, CTX)
        gate5 = carve(ringf, 26, D)
        aff, slot = carve(hTf, 21, NT, E), carve(hTf, 21.5, NT, E)
        fin_row = carve(ar, 0, D)
        fin = carve(ar, 4, SEQ // P, D)

        ps = [ctx.enter_context(nc.psum_tensor(f"ps{i}", [P, 512], F32)) for i in range(8)]
        rpb_scratch = [nc.dram_tensor(f"rpb_scratch{l}", [H * 15, PADW], F32, kind="Internal").ap()
                       for l in range(DEPTH)]

        ADA = {"first": 4, "gates": 8, "na": 6, "mla": 6}

        def ada_first(stage):
            names = list(ADA)
            return sum(ADA[n] for n in names[:names.index(stage)])

        def ada_events(stage, point, points):
            h0, n, events = 2 * ada_first(stage), 2 * ADA[stage] * KD, []
            for i in range(n * point // points, n * (point + 1) // points):
                events.append((h0 + i // KD, i % KD))
                if i >= KD and i % KD == 3:
                    events.append((h0 + i // KD - 1, None))
            if point == points - 1:
                events.append((h0 + 2 * ADA[stage] - 1, None))
            return events

        def unit_events(stage, u, place):
            h = 2 * ada_first(stage) + u // 2
            if u // 2 >= 2 * ADA[stage]:
                return []
            return {(0, "later"): [(h, k) for k in range(5)], (1, "early"): [(h, k) for k in range(5, KD)],
                    (1, "last"): [(h, None)]}.get((u % 2, place), [])

        def ada_bank(h):
            return ps[7] if h >= 2 * ada_first("na") else ps[2 + h % 2]

        def ada_loads(stage):
            g0 = ada_first(stage)
            return [("ada", g, a["ada_w"][g // 12][:, 512 * (g % 12):512 * (g % 12) + 512]) for g in range(g0, g0 + ADA[stage])]

        def in_loads(l, *names):
            at = {"gqk": (O_GQK, 512), "ga": (O_GA, 32), "gv": (O_GV, 512), "og": (O_OG, 512),
                  "naqk": (O_NAQK, 512), "navdq": (O_NAV, 512), "dkv": (O_DKV, 160)}
            return [(name, l, a["w_in"][l][:, at[name][0]:at[name][0] + at[name][1]]) for name in names]

        ring_loads = ada_loads("first")
        for l in range(DEPTH):
            ring_loads += in_loads(l, "gqk", "ga", "gv") + (ada_loads("gates") if l == 0 else [])
            ring_loads += in_loads(l, "og")
            ring_loads += in_loads(l, "naqk", "navdq", "dkv") + (ada_loads("na") + ada_loads("mla") if l == 0 else [])
            ring_loads += [("m", (l, j), None) for j in range(KD)]
        ring_at = {load[0:2]: n for n, load in enumerate(ring_loads)}

        def ring_view(n, w):
            return carve(ringf, 16 * (n % 2), KD, w)

        def segments(l):
            return (LAT, CX) if l < DEPTH - 1 else (LAT,)

        def q_tiles(l):
            return list(range(NT)) if l < DEPTH - 1 else list(range(CT, NT))

        def projections(l):
            jobs = {"gqk": [], "ga": [], "gv": [], "og": [], "naqk": [], "navdq": [], "dkv": []}
            for c in range(4):
                for seg in (segments(l) if c < 2 else (LAT, CX)):
                    jobs["gqk"].append((c * P, P, "F", seg, g_raw[:, c, seg], DH ** -0.5 if c < 2 else 1.0))
                    jobs["naqk"].append((c * P, P, "F", seg, (naqT if c < 2 else nakT)[:, c % 2, seg],
                                         DH ** -0.5 if c < 2 else 1.0))
            for d in range(2):
                for seg in (LAT, CX):
                    jobs["ga"].append((RANK * d, RANK, "F", seg, aT[0:RANK, d, seg], 1.0))
            for t in range(NT):
                jobs["gv"].append((0, 512, "T", t, g_v[:, t, :], 1.0))
                if t in q_tiles(l):
                    jobs["og"].append((0, 512, "T", t, g_og[:, t, :], 1.0))
                jobs["navdq"].append((0, 256, "T", t, nav[:, t, :], 1.0))
                if t in q_tiles(l):
                    jobs["navdq"].append((256, 256, "T", t, dqb[:, t, 0:QR], 1.0))
                jobs["dkv"].append((0, 160, "T", t, dqb[:, t, QR:DMLA], 1.0))
            return jobs

        WIDTH = {"gqk": 512, "ga": 32, "gv": 512, "og": 512, "naqk": 512, "navdq": 512, "dkv": 160}
        ORDER = ("gqk", "ga", "gv", "og", "naqk", "navdq", "dkv")

        def first_job(l, name):
            js = projections(l)
            return sum(len(js[g]) for g in ORDER[:ORDER.index(name)])

        def last_job(l, name):
            return first_job(l, name) + len(projections(l)[name])

        cst_in, x_in = sem("cst_in"), sem("x_in")
        ring_in = [sem("ring_in0"), sem("ring_in1")]
        ada_up, ada_copied, ada_turned, ada_raw = sem("ada_up"), sem("ada_copied"), sem("ada_turned"), sem("ada_raw")
        vec_in, small_in, mla_in = sem("vec_in"), sem("small_in"), sem("mla_in")
        rpb_landed, rpb_flat, bias_in = sem("rpb_landed"), sem("rpb_flat"), sem("bias_in")
        rpb_padded, bias_ready = sem("rpb_padded"), sem("bias_ready")
        vecs_up, vecs_ok = sem("vecs_up"), sem("vecs_ok")
        silu_ok, mod_ok, mod_late = sem("silu_ok"), sem("mod_ok"), sem("mod_late")
        nrm_ss, nrm_ms, nrm_root = sem("nrm_ss"), sem("nrm_ms"), sem("nrm_root")
        xn_ok = sem("xn_ok")
        hl_up, hc_up, h_lat, h_ctx = sem("hl_up"), sem("hc_up"), sem("h_lat"), sem("h_ctx")
        proj_up, proj_act, proj_dve = sem("proj_up"), sem("proj_act"), sem("proj_dve")
        z_up, z_act, z_dve = sem("z_up"), sem("z_act"), sem("z_dve")
        sp_ok = sem("sp_ok")
        g_scan, g_exp, ke_ok, ke_up, ke_tok_ok = (sem("g_scan"), sem("g_exp"), sem("ke_ok"), sem("ke_up"),
                                                  sem("ke_tok_ok"))
        kv_up, state_ok = sem("kv_up"), sem("state_ok")
        a_up, a_ok, go_up, go_copied, go_ok, goT_up, goT_ok = (
            sem("a_up"), sem("a_ok"), sem("go_up"), sem("go_copied"), sem("go_ok"), sem("goT_up"),
            sem("goT_ok"))
        og_silu, go_ms, go_root = sem("og_silu"), sem("go_ms"), sem("go_root")
        s_up, s_max, s_exp = [sem(n) for n in ("s_up", "s_max", "s_exp")]
        p_up, p_act, p_dve = [sem(n) for n in ("p_up", "p_act", "p_dve")]
        o_up, o_ok, oT_up, oT_ok = [sem(n) for n in ("o_up", "o_ok", "oT_up", "oT_ok")]
        mla_ss, mla_ms, mla_root, mla_n = sem("mla_ss"), sem("mla_ms"), sem("mla_root"), sem("mla_n")
        mlaT_up, mlaT_ok = sem("mlaT_up"), sem("mlaT_ok")
        qkT_dve = sem("qkT_dve")
        qk_up, q_nope, qk_tok, qkT_up, qkT_act = (sem("qk_up"), sem("q_nope"), sem("qk_tok"), sem("qkT_up"),
                                                 sem("qkT_act"))
        wbr_in, wout_in = sem("wbr_in"), sem("wout_in")
        m_up, m_sig, m_ok = sem("m_up"), sem("m_sig"), sem("m_ok")
        diag_ok, grow_up, grow_ok = sem("diag_ok"), sem("grow_up"), sem("grow_ok")
        y_up, y_ok = sem("y_up"), sem("y_ok")
        lg_up, aff_exp, aff_sh, aff_ok, affT_up, top_ok, slot_up, slot_ok = (
            sem("lg_up"), sem("aff_exp"), sem("aff_sh"), sem("aff_ok"), sem("affT_up"), sem("top_ok"),
            sem("slot_up"), sem("slot_ok"))
        ex_in = [sem(f"ex_in{i}") for i in range(SLOTS)]
        w_hi_ok, w_lo_ok, w_used = sem("w_hi_ok"), sem("w_lo_ok"), sem("w_used")
        sel_ok, selT_up, selT_ok = sem("sel_ok"), sem("selT_up"), sem("selT_ok")
        xg_up, xg_sum_ok, xg_hi_ok, xg_lo_ok = sem("xg_up"), sem("xg_sum_ok"), sem("xg_hi_ok"), sem("xg_lo_ok")
        xg_zero = sem("xg_zero")
        gu_silu, hid_ok = sem("gu_silu"), sem("hid_ok")
        hidT_up, hidT_act, hidT_dve = sem("hidT_up"), sem("hidT_act"), sem("hidT_dve")
        ye_ok, sc_up, x_ok = sem("ye_ok"), sem("sc_up"), sem("x_ok")
        fin_in, fin_ok, stored = sem("fin_in"), sem("fin_ok"), sem("stored")
        dve_own, act_own = sem("dve_own"), sem("act_own")
        turn_own = sem("turn_own")
        started = sem("started")

        NJ = [sum(len(v) for v in projections(l).values()) for l in range(DEPTH)]
        NSEG = [len(segments(l)) for l in range(DEPTH)]
        O_BANKS = [1, 2]
        NQ = [len(q_tiles(l)) for l in range(DEPTH)]
        UNITS = [H * n for n in NQ]
        NORMS = [n for l in range(DEPTH) for n in (NT, NQ[l])] + [SEQ // P]
        CTX_NORMS = [n for l in range(DEPTH) for n in (1, NSEG[l] - 1)]

        def col(row):
            return vT[:, row:row + 1]

        def moe_done(l):
            return E // GE * 2 * NQ[l]

        def ring_count(n):
            return 16 * sum(3 if ring_loads[i][0] == "m" else 1 for i in range(n % 2, n + 1, 2))

        def tile(t):
            return slice(t * P, (t + 1) * P)

        def jobs_done(eng, l, name):
            n = last_job(l, name)
            eng.wait_ge(proj_act, before("proj_act", l) + (n + 1) // 2)
            eng.wait_ge(proj_dve, before("proj_dve", l) + n // 2)

        def units(l):
            return [(h, t) for h in range(H) for t in q_tiles(l)]

        def order(d):
            c = list(range(CTX // C)), list(range(CTX // C, NCH))
            return c[0] + c[1] if d == 0 else c[0][::-1] + c[1][::-1]

        KV_STEPS = NCH - 1

        def before(name, l):
            if name in ATTENTION:
                return sum(ATTENTION[name](i // 2) for i in range(l))
            return sum(COUNTS[name](i) if callable(COUNTS[name]) else COUNTS[name] for i in range(l))

        ATTENTION = {n: lambda l: UNITS[l] for n in ("s_up", "s_max", "s_exp", "p_up", "p_dve", "o_up", "o_ok")}
        ATTENTION |= {"p_act": lambda l: H * (NT - CT), "oT_up": lambda l: NQ[l], "oT_ok": lambda l: NQ[l]}
        TURNS = E // GE
        COUNTS = {
            "vec_in": 160, "small_in": 48, "mla_in": 32, "rpb_landed": 16, "rpb_flat": 16, "bias_in": 128,
            "wbr_in": 48, "wout_in": 16,
            "proj_up": lambda l: NJ[l], "proj_act": lambda l: (NJ[l] + 1) // 2, "proj_dve": lambda l: NJ[l] // 2,
            "z_up": 8, "z_act": 8, "z_dve": 8, "sp_ok": 4, "g_scan": 4, "g_exp": 8, "ke_ok": 4, "ke_up": 8, "ke_tok_ok": 8,
            "kv_up": 2 * KV_STEPS, "state_ok": 2 * KV_STEPS, "go_copied": lambda l: 2 * NQ[l],
            "mla_n": NT, "mlaT_up": lambda l: 2 * NSEG[l] + 2, "mlaT_ok": lambda l: 2 * NSEG[l] + 2,
            "qk_up": NT, "q_nope": NT, "qk_tok": NT, "qkT_up": NT, "qkT_act": lambda l: NQ[l], "qkT_dve": NT,
            "y_up": lambda l: 2 * NQ[l], "y_ok": lambda l: 2 * NQ[l],
            "sel_ok": TURNS, "selT_up": lambda l: TURNS * (1 + NSEG[l]), "selT_ok": lambda l: TURNS * (1 + NSEG[l]),
            "xg_up": KD * TURNS, "xg_sum_ok": KD * TURNS, "xg_hi_ok": KD * TURNS, "xg_lo_ok": KD * TURNS,
            "w_hi_ok": PER_TURN * TURNS, "w_lo_ok": PER_TURN * TURNS, "w_used": PER_TURN * TURNS,
            "gu_silu": 2 * E, "hid_ok": 2 * E, "hidT_up": 2 * E, "hidT_act": 2 * E, "hidT_dve": 2 * E, "ye_ok": 2 * E, "turn_own": 3 * TURNS,
            "sc_up": lambda l: 2 * TURNS * NQ[l], "x_ok": lambda l: 2 * TURNS * NQ[l],
        }
        COUNTS |= {n: 1 for n in ("rpb_padded", "vecs_up", "vecs_ok", "mod_ok", "mla_ss", "mla_ms",
                                  "mla_root", "lg_up", "aff_exp", "aff_sh", "aff_ok", "affT_up", "top_ok", "slot_up",
                                  "slot_ok")}
        COUNTS |= {n: lambda l: UNITS[l] for n in ("a_up", "a_ok", "go_up")}
        COUNTS |= {n: lambda l: NQ[l] for n in ("go_ok", "goT_up", "goT_ok", "og_silu", "go_ms", "go_root")}
        COUNTS |= {n: lambda l: 24 * NSEG[l] for n in ("m_up", "m_sig", "m_ok")}
        COUNTS |= {n: lambda l: 4 * NSEG[l] for n in ("diag_ok", "grow_up", "grow_ok")}

        block = ctx.enter_context(nc.Block())


        @block.sync
        def _(sp):
            sp.dma_start(cst[:, :], a["constants"]).then_inc(cst_in, 16)
            sp.dma_start(x_sb[:, 0:CT, :], a["ctx"][0].rearrange("(t p) d -> p t d", p=P)).then_inc(x_in, 16)
            sp.dma_start(x_sb[:, CT:NT, :], a["x"][0].rearrange("(t p) d -> p t d", p=P)).then_inc(x_in, 16)

            def slot_read(n):
                kind, which, _ = ring_loads[n]
                if kind == "ada":
                    sp.wait_ge(ada_up, 2 * which + 2)
                elif kind == "m":
                    l, j = which
                    sp.wait_ge(m_up, before("m_up", l) + 3 * NSEG[l] * (j + 1))
                else:
                    sp.wait_ge(proj_up, before("proj_up", which) + last_job(which, kind))

            def expert_loads(l, g):
                for i, (j, matrix, half, part) in enumerate(LOADS):
                    sp.wait_ge(w_used, before("w_used", l) + g * PER_TURN + (i + 1))
                    src = a["moe_w_" + matrix][l, bass.ds(g * GE + j, 1), part * 512:part * 512 + 512, 512 * half:512 * half + 512]
                    sp.dma_start(w_raw[i % SLOTS], src.rearrange("e (k p) n -> p (e k) n", p=P)
                                 ).then_inc(ex_in[i % SLOTS], 16)

            for n, (kind, which, src) in enumerate(ring_loads):
                if n >= 2:
                    slot_read(n - 2)
                if (kind, which) == ("gqk", 1):
                    sp.wait_ge(x_ok, before("x_ok", 0) + moe_done(0))
                if kind == "m":
                    l, j = which
                    for b in range(3):
                        c0 = O_M + b * D + j * P
                        sp.dma_start(ring_view(n, 3 * P)[:, :, b * P:(b + 1) * P],
                                     a["w_in"][l][:, c0:c0 + P].rearrange("(k p) n -> p k n", p=P)).then_inc(ring_in[n % 2], 16)
                else:
                    sp.dma_start(ring_view(n, src.shape[1]), src.rearrange("(k p) n -> p k n", p=P)
                                 ).then_inc(ring_in[n % 2], 16)
                if kind != "m" or j < KD - 1:
                    continue
                sp.wait_ge(y_ok, before("y_ok", l) + 2 * NQ[l])
                with sp.Fori(0, TURNS) as g:
                    expert_loads(l, g)
            sp.wait_ge(fin_ok, SEQ // P)
            sp.dma_start(out[0].rearrange("(t p) d -> p t d", p=P), fin).then_inc(stored, 16)
            sp.wait_ge(stored, 16)

        @block.gpsimd
        def _(pool):
            nc.gpsimd.memset(mst[:, 0:2, :], 1.0).then_inc(w_used, SLOTS)
            nc.gpsimd.memset(mst[:, 2:4, :], 1.0).then_inc(started, 1)
            for l in range(DEPTH):
                if l:
                    pool.wait_ge(lg_up, before("lg_up", l - 1) + 1)
                rows = ((R_AB, 48, a["ada_b"][l]), (R_N1, 8, a["norm1"][l]), (R_N2, 8, a["norm2"][l]), (R_C, 8, a["c"][0]),
                        (R_CC, 8, a["c_ctx"]), (R_QN, 2, a["mla_q_norm"][l]), (R_KVN, 1, a["mla_kv_norm"][l]),
                        (R_ON, 1, a["gla_o_norm"][l]), (R_BF, 2, a["gla_b_af"][l]), (R_BB, 2, a["gla_b_ab"][l]))
                for r, n, src in rows:
                    pool.dma_start(vecs[r:r + n, :], src.rearrange("(r c) -> r c", c=P)).then_inc(vec_in, 16)
                pool.dma_start(router[:, :, :], a["moe_router"][l].rearrange("(k p) e -> p k e", p=P)
                               ).then_inc(small_in, 16)
                if l:
                    pool.wait_ge(x_ok, before("x_ok", l - 1) + moe_done(l - 1))
                for d, name in enumerate(("gla_w_af", "gla_w_ab")):
                    pool.dma_start(w_decay[0:RANK, d, :], a[name][l]).then_inc(small_in, 16)
                pool.dma_start(rpb_in[0:H * 15, :], a["na_rpb"][l].rearrange("h r c -> (h r) c")).then_inc(rpb_landed, 16)
                pool.wait_ge(rpb_padded, before("rpb_padded", l) + 1)
                pool.dma_start(rpb_scratch[l], rpb_pad[0:H * 15, :]).then_inc(rpb_flat, 16)
                pool.wait_ge(rpb_flat, before("rpb_flat", l) + 16)
                pool.wait_ge(goT_ok, before("goT_ok", l) + NQ[l])
                for half in range(2):
                    for h in range(H):
                        src = bass.AP(rpb_scratch[l].tensor, (h * 15 + 1 - half) * PADW, [[1, 64], [PADW, 14], [1, 64]])
                        pool.dma_start(bias_raw[64 * half:64 * half + 64, h, :, :], src).then_inc(bias_in, 16)
                pool.dma_start(w_uq, a["mla_w_uq"][l].rearrange("(k p) n -> p k n", p=P)).then_inc(mla_in, 16)
                pool.dma_start(w_ukv, a["mla_w_ukv"][l]).then_inc(mla_in, 16)
                pool.wait_ge(oT_ok, before("oT_ok", 2 * l + 1) + NQ[l])
                at = 0
                for name, rows in (("w_br_a", 2), ("w_br_b", 2), ("w_br_c", 4)):
                    pool.dma_start(w_br[:, at:at + rows, :], a[name][l].rearrange("(k p) n -> p k n", p=P)
                                   ).then_inc(wbr_in, 16)
                    at += rows
                pool.dma_start(w_out, a["w_out"][l].rearrange("(k p) n -> p k n", p=P)).then_inc(wout_in, 16)
            pool.wait_ge(x_ok, before("x_ok", DEPTH - 1) + moe_done(DEPTH - 1))
            fn = a["final_norm"]
            pool.dma_start(fin_row, bass.AP(fn.tensor, fn.offset, [[0, P], [1, D]])).then_inc(fin_in, 16)

        @block.tensor
        def _(pe):
            mm, tr = nc.tensor.matmul, nc.tensor.transpose

            def ring_entry(kind, which, width):
                n = ring_at[(kind, which)]
                pe.wait_ge(ring_in[n % 2], ring_count(n))
                return ring_view(n, width)

            def modulation_products(events):
                for h, k in events:
                    alone = h >= 2 * ada_first("na")
                    if k is None:
                        pe.wait_ge(ada_copied, h + 1)
                        for c in range(2):
                            last = tr(ada_bank(h)[:, 256 + 2 * c:258 + 2 * c], ada_row[:, tile(c)], ident[0:2, 0:2])
                        last.then_inc(ada_turned, 1)
                        continue
                    if k == 0 and h >= 2:
                        pe.wait_ge(ada_raw, h if alone else h - 1)
                    w = ring_entry("ada", h // 2, 512) if (h % 2, k) == (0, 0) else ring_view(ring_at[("ada", h // 2)], 512)
                    last = mm(ada_bank(h)[0:2, 0:256], silc[:, :, k], w[:, k, 256 * (h % 2):256 * (h % 2) + 256],
                              start=k == 0, stop=k == KD - 1)
                    if k == KD - 1:
                        last.then_inc(ada_up, 1)

            def project(l, name):
                w = ring_entry(name, l, WIDTH[name])
                jobs = projections(l)[name]
                for i, (c0, width, kind, where, _, _) in enumerate(jobs):
                    n = first_job(l, name) + i
                    if n >= 4:
                        pe.wait_ge((proj_act, proj_dve)[n % 2], before(("proj_act", "proj_dve")[n % 2], l) + (n - 4) // 2 + 1)
                    for k in range(KD):
                        if kind == "F":
                            size = where.stop - where.start
                            last = mm(ps[n % 4][0:width, 0:size], w[:, k, c0:c0 + width], hT[:, k, where],
                                      start=k == 0, stop=k == KD - 1)
                        else:
                            last = mm(ps[n % 4][:, 0:width], hT[:, k, tile(where)], w[:, k, c0:c0 + width],
                                      start=k == 0, stop=k == KD - 1)
                    last.then_inc(proj_up, 1)

            def norm_transposes(l, i):
                s = 2 * l + i
                xn = (xn1, xn2)[i]
                pe.wait_ge(xn_ok, sum(NORMS[:s + 1]))
                for k in range(KD):
                    if k >= 2:
                        pe.wait_ge(h_lat, KD * s + k - 1)
                    for t in range(CT, NT):
                        last = tr(ps[2 + k % 2][:, tile(t - CT)], xn[:, t, tile(k)], ident)
                    last.then_inc(hl_up, 1)
                    if CTX_NORMS[s]:
                        if k >= 2:
                            pe.wait_ge(h_ctx, KD * sum(CTX_NORMS[:s]) + k - 1)
                        for t in range(CT):
                            last = tr(ps[4 + k % 2][:, tile(t)], xn[:, t, tile(k)], ident)
                        last.then_inc(hc_up, 1)
                pe.wait_ge(h_lat, KD * (s + 1))
                pe.wait_ge(h_ctx, KD * sum(CTX_NORMS[:s + 1]))

            def modulation(l):
                pe.wait_ge(cst_in, 16)
                pe.wait_ge(vec_in, before("vec_in", l) + 160)
                if l:
                    pe.wait_ge(x_ok, before("x_ok", l - 1) + moe_done(l - 1))
                tr(ps[1][:, 0:R_ALL], vecs[0:R_ALL, :], ident[0:R_ALL, 0:R_ALL]).then_inc(vecs_up, 1)
                if l == 0:
                    pe.wait_ge(silu_ok, 1)
                    modulation_products(ada_events("first", 0, 1))
                    pe.wait_ge(ada_raw, 2 * ADA["first"])

            def gates(l):
                jobs_done(pe, l, "gv")
                pe.wait_ge(small_in, before("small_in", l) + 48)
                for u in range(4):
                    d, kt = u // 2, u % 2
                    for i, seg in enumerate((LAT, CX)):
                        if u >= 2:
                            pe.wait_ge(z_dve, before("z_dve", l) + 2 * (u - 2) + i + 1)
                        mm(ps[4 + 2 * (u % 2) + i][:, 0:seg.stop - seg.start], w_decay[0:RANK, d, tile(kt)],
                           aT[0:RANK, d, seg], start=True, stop=True).then_inc(z_up, 1)
                    if u:
                        keys_end(l, u - 1)
                    if l == 0:
                        modulation_products(ada_events("gates", u, 4))
                keys_end(l, 3)
                pe.wait_ge(ada_raw, 2 * ada_first("na"))

            def keys_end(l, u):
                pe.wait_ge(ke_ok, before("ke_ok", l) + u + 1)
                if u:
                    pe.wait_ge(ke_tok_ok, before("ke_tok_ok", l) + 2 * u)
                for t in range(CT, NT):
                    last = tr(ps[0][:, tile(t - CT)], k_end[:, tile(t)], ident)
                last.then_inc(ke_up, 1)
                for t in range(CT):
                    last = tr(ps[1][:, tile(t)], k_end[:, tile(t)], ident)
                last.then_inc(ke_up, 1)

            def chunk_states(l):
                pe.wait_ge(ke_tok_ok, before("ke_tok_ok", l) + 8)
                pe.wait_ge(z_dve, before("z_dve", l) + 8)
                for i in range(KV_STEPS):
                    for d in range(2):
                        c = order(d)[i]
                        t, r = c // 2, C * (c % 2)
                        bank = ps[4 + 2 * d + i % 2]
                        if i >= 2:
                            pe.wait_ge(state_ok, before("state_ok", l) + 2 * (i - 2) + d + 1)
                        for h in range(H):
                            last = mm(bank[64 * (h % 2):64 * (h % 2) + 64, tile(h // 2)],
                                      ke_tok[r:r + C, d, t, 64 * h:64 * h + 64], g_v[r:r + C, t, h * DV:(h + 1) * DV],
                                      start=True, stop=True)
                        last.then_inc(kv_up, 1)

            def gla_outputs(l):
                tiles = q_tiles(l)
                jobs_done(pe, l, "og")
                pe.wait_ge(state_ok, before("state_ok", l) + 2 * KV_STEPS)

                def scores(u):
                    t, h = tiles[u // H], u % H
                    r = 64 * (h % 2)
                    if u >= 2:
                        pe.wait_ge(a_ok, before("a_ok", l) + u - 1)
                    for d in range(2):
                        last = mm(ps[u % 2][:, tile(d)], kd[r:r + 64, d, h // 2, tile(t)], qd[r:r + 64, d, h // 2, tile(t)],
                                  start=True, stop=True)
                    last.then_inc(a_up, 1)

                def values(u):
                    ti, h = u // H, u % H
                    t, r = tiles[ti], 64 * (h % 2)
                    o = ps[2 + 2 * (ti % 2) + h % 2]
                    if h == 0 and ti >= 2:
                        pe.wait_ge(go_copied, before("go_copied", l) + 2 * (ti - 1))
                    pe.wait_ge(a_ok, before("a_ok", l) + u + 1)
                    mm(o[:, tile(h // 2)], a_sum[:, u % 2, :], g_v[:, t, h * DV:(h + 1) * DV], start=True, stop=False,
                       skip_group_check=True)
                    for c in range(2):
                        for d in range(2):
                            last = mm(o[C * c:C * c + C, tile(h // 2)], qd[r:r + 64, d, h // 2, t * P + C * c:t * P + C * c + C],
                                      states[r:r + 64, d, 2 * t + c, h // 2, :], start=False, stop=True, skip_group_check=True)
                    last.then_inc(go_up, 1)

                def turn(ti):
                    pe.wait_ge(go_ok, before("go_ok", l) + ti + 1)
                    if ti >= 2:
                        pe.wait_ge(goT_ok, before("goT_ok", l) + ti - 1)
                    for h in range(H):
                        last = tr(ps[6 + ti % 2][:, tile(h)], g_o[:, ti % 2, h, :], ident)
                    last.then_inc(goT_up, 1)

                n = H * len(tiles)
                for u in range(n + 1):
                    if u < n:
                        scores(u)
                    if u >= 1:
                        values(u - 1)
                    if u > H and u % H == 3:
                        turn(u // H - 1)
                turn(len(tiles) - 1)
                pe.wait_ge(goT_ok, before("goT_ok", l) + len(tiles))

            def attention(l, i):
                idx = 2 * l + i
                us = units(l)
                n = len(us)
                lats = [sum(1 for h, t in us[:u + 1] if t >= CT) for u in range(n)]

                def scores(u):
                    h, t = us[u]
                    if i == 0:
                        r = 64 * (h % 2)
                        q, kk = naqT[r:r + 64, h // 2, tile(t)], nakT[r:r + 64, h // 2, :]
                    else:
                        q, kk = qT[0:DQK, h, tile(t)], kT[0:DQK, h, :]
                    if u >= 2:
                        pe.wait_ge(s_exp, before("s_exp", idx) + u - 1)
                    if t >= CT:
                        mm(ps[2 * (u % 2)][:, :], q, kk[:, LAT], start=True, stop=True)
                    mm(ps[2 * (u % 2) + 1][:, 0:CTX], q, kk[:, CX], start=True, stop=True).then_inc(s_up, 1)

                def turn(u):
                    pe.wait_ge(s_exp, before("s_exp", idx) + u + 1)
                    if us[u][1] >= CT:
                        if lats[u] >= 2:
                            pe.wait_ge(p_act, before("p_act", idx) + lats[u] - 1)
                        for t in range(CT, NT):
                            tr(ps[4][:, tile(t - CT)], prob[:, u % 2, tile(t)], ident)
                    if u:
                        pe.wait_ge(p_dve, before("p_dve", idx) + u)
                    for t in range(CT):
                        last = tr(ps[5][:, tile(t)], prob[:, u % 2, tile(t)], ident)
                    last.then_inc(p_up, 1)

                def values(u):
                    h, t = us[u]
                    if t >= CT:
                        pe.wait_ge(p_act, before("p_act", idx) + lats[u])
                    pe.wait_ge(p_dve, before("p_dve", idx) + u + 1)
                    if u >= O_BANKS[l]:
                        pe.wait_ge(o_ok, before("o_ok", idx) + u + 1 - O_BANKS[l])
                    keys = range(NT if t >= CT else CT)
                    for kt in keys:
                        v = nav[:, kt, 64 * h:64 * h + 64] if i == 0 else mv[:, kt, h, :]
                        last = mm(ps[6 + u % O_BANKS[l]][:, 0:64], probT[:, u % 2, kt, :], v, start=kt == 0, stop=kt == keys[-1])
                    last.then_inc(o_up, 1)

                for u in range(n + 2):
                    if u < n:
                        scores(u)
                    if l == 0:
                        modulation_products(unit_events(("na", "mla")[i], u, "early"))
                    if 1 <= u <= n:
                        turn(u - 1)
                    if l == 0:
                        modulation_products(unit_events(("na", "mla")[i], u, "later"))
                    if u >= 2:
                        values(u - 2)
                    if l == 0:
                        modulation_products(unit_events(("na", "mla")[i], u, "last"))
                pe.wait_ge(o_ok, before("o_ok", idx) + n)
                for ti, t in enumerate(q_tiles(l)):
                    if ti >= 2:
                        pe.wait_ge(oT_ok, before("oT_ok", idx) + ti - 1)
                    for k in range(2):
                        last = tr(ps[4 + ti % 2][:, tile(k)], o_tok[:, t, tile(k)], ident)
                    last.then_inc(oT_up, 1)
                pe.wait_ge(oT_ok, before("oT_ok", idx) + NQ[l])

            def latent_heads(l):
                pe.wait_ge(mla_n, before("mla_n", l) + NT)
                n = 0
                for f in range(3):
                    for seg in ((LAT, CX) if f == 2 else segments(l)):
                        if n >= 4:
                            pe.wait_ge(mlaT_ok, before("mlaT_ok", l) + n - 3)
                        tiles = range(CT, NT) if seg is LAT else range(CT)
                        for t in tiles:
                            last = tr(ps[n % 4][:, tile(t - tiles[0])], dqb[:, t, tile(f)], ident)
                        last.then_inc(mlaT_up, 1)
                        n += 1
                pe.wait_ge(mlaT_ok, before("mlaT_ok", l) + n)
                pe.wait_ge(mla_in, before("mla_in", l) + 32)

                def up(t):
                    if t >= 2:
                        pe.wait_ge(qk_tok, before("qk_tok", l) + t - 1)
                    if t in q_tiles(l):
                        for k in range(2):
                            mm(ps[4 + 2 * (t % 2)][:, 0:H * DQK], dqnT[:, k, tile(t)], w_uq[:, k, :], start=k == 0, stop=k == 1)
                    mm(ps[5 + 2 * (t % 2)][:, :], dkvnT[:, tile(t)], w_ukv, start=True, stop=True).then_inc(qk_up, 1)

                def turn(t):
                    pe.wait_ge(qk_tok, before("qk_tok", l) + t + 1)
                    if t in q_tiles(l):
                        if t > q_tiles(l)[0]:
                            pe.wait_ge(qkT_act, before("qkT_act", l) + t - q_tiles(l)[0])
                        for h in range(H):
                            tr(ps[0][0:DQK, tile(h)], q_tok[:, h, :], ident)
                    if t:
                        pe.wait_ge(qkT_dve, before("qkT_dve", l) + t)
                    for h in range(H):
                        last = tr(ps[1][0:DQK, tile(h)], k_tok[:, h, :], ident)
                    last.then_inc(qkT_up, 1)

                up(0)
                for t in range(NT):
                    if t + 1 < NT:
                        up(t + 1)
                    turn(t)
                pe.wait_ge(qkT_act, before("qkT_act", l) + NQ[l])
                pe.wait_ge(qkT_dve, before("qkT_dve", l) + NT)

            def merge(l):
                pe.wait_ge(wbr_in, before("wbr_in", l) + 48)
                q = 0
                for j in range(KD):
                    w = ring_entry("m", (l, j), 3 * P)
                    for seg in segments(l):
                        size = seg.stop - seg.start
                        for b, kts in enumerate(((0, 1), (2, 3), (4, 5, 6, 7))):
                            if q >= 4:
                                pe.wait_ge(m_ok, before("m_ok", l) + q - 3)
                            for k in range(KD):
                                mm(ps[2 * (q % 4)][:, 0:size], w[:, k, tile(b)], hT[:, k, seg], start=k == 0, stop=k == KD - 1)
                            for k in kts:
                                last = mm(ps[2 * (q % 4) + 1][:, 0:size], w_br[:, k, tile(j)], oT[:, k, seg],
                                          start=k == kts[0], stop=k == kts[-1])
                            last.then_inc(m_up, 1)
                            q += 1
                pe.wait_ge(m_ok, before("m_ok", l) + q)
                for n in range(4 * NSEG[l]):
                    pe.wait_ge(diag_ok, before("diag_ok", l) + n + 1)
                    if n >= 2:
                        pe.wait_ge(grow_ok, before("grow_ok", l) + n - 1)
                    mm(ps[n % 2][:, :], ones, diag.rearrange("p a b -> p (a b)"), start=True, stop=True).then_inc(grow_up, 1)
                pe.wait_ge(wout_in, before("wout_in", l) + 16)
                q = 0
                for t in q_tiles(l):
                    for half in range(2):
                        if q >= 4:
                            pe.wait_ge(y_ok, before("y_ok", l) + q - 3)
                        for k in range(KD):
                            last = mm(ps[2 + q % 4][:, :], yT[:, k, tile(t)], w_out[:, k, 512 * half:512 * half + 512],
                                      start=k == 0, stop=k == KD - 1)
                        last.then_inc(y_up, 1)
                        q += 1
                pe.wait_ge(y_ok, before("y_ok", l) + q)
                pe.wait_ge(grow_ok, before("grow_ok", l) + 4 * NSEG[l])

            def route(l):
                for t in q_tiles(l):
                    for k in range(KD):
                        last = mm(ps[0][:, t * E:(t + 1) * E], hT[:, k, tile(t)], router[:, k, :], start=k == 0, stop=k == KD - 1)
                last.then_inc(lg_up, 1)
                pe.wait_ge(aff_ok, before("aff_ok", l) + 1)
                for t in q_tiles(l):
                    bank, at = (ps[1], t - CT) if t >= CT else (ps[2], t)
                    last = tr(bank[0:E, tile(at)], aff[:, t, :], ident)
                last.then_inc(affT_up, 1)
                pe.wait_ge(top_ok, before("top_ok", l) + 1)
                for t in q_tiles(l):
                    last = tr(ps[3][:, t * E:(t + 1) * E], slotT[0:E, tile(t)], ident[0:E, 0:E])
                last.then_inc(slot_up, 1)

            def experts(l):
                has_ctx = NSEG[l] - 1
                ns = 2 + has_ctx
                nq = 2 * NQ[l]

                def product(g, i, bank, x_hi, x_lo, k0, part):
                    pe.wait_ge(w_lo_ok, before("w_lo_ok", l) + g * PER_TURN + (i + 1))
                    for k in range(GRAIN):
                        hi, lo = w_hi[:, i % HI_SLOTS, k, :], w_lo[:, i % SLOTS, k, :]
                        for n, (x, w) in enumerate(((x_hi, hi), (x_lo, hi), (x_hi, lo))):
                            last = mm(bank[0:ROWS, :], x(k0 + k), w, start=part == 0 and k == 0 and n == 0,
                                      stop=part == 1 and k == GRAIN - 1 and n == 2)
                    last.then_inc(w_used, 1)

                def hidden_turned(g, j):
                    pe.wait_ge(hid_ok, before("hid_ok", l) + g * 8 + (2 * j + 2))
                    if j:
                        pe.wait_ge(hidT_dve, before("hidT_dve", l) + g * 8 + 2 * j)
                    for b in range(2):
                        for k in range(4):
                            last = tr(ps[4 + b][:, k * ROWS:(k + 1) * ROWS], hid[0:ROWS, tile(4 * b + k)], ident[0:ROWS, 0:ROWS])
                        last.then_inc(hidT_up, 1)

                if not has_ctx:
                    pe.wait_ge(xg_zero, 2)
                with pe.Fori(0, TURNS) as g:
                    pe.wait_ge(sel_ok, before("sel_ok", l) + g + 1)
                    for dt in range(KD):
                        if dt >= 2:
                            pe.wait_ge(xg_sum_ok, before("xg_sum_ok", l) + g * KD + (dt - 1))
                        bank = ps[4 + dt % 2]
                        for t in range(4):
                            last = mm(bank[:, 0:GE * CAPL], xn2[:, CT + t, tile(dt)], sel_l[:, t, :, :].rearrange("p a b -> p (a b)"),
                                      start=t == 0, stop=t == 3)
                        for t in range(CT * has_ctx):
                            last = mm(bank[:, GE * CAPL:GE * ROWS], xn2[:, t, tile(dt)],
                                      sel_c[:, t, :, :].rearrange("p a b -> p (a b)"), start=t == 0, stop=t == CT - 1)
                        last.then_inc(xg_up, 1)
                    for p in range(2):
                        for t in range(4):
                            last = tr(ps[6 + p][:, tile(t)], selw_l[:, t, 2 * p:2 * p + 2, :].rearrange("p a b -> p (a b)"), ident)
                        last.then_inc(selT_up, 1)
                    if has_ctx:
                        for t in range(CT):
                            last = tr(ps[0][:, tile(t)], selw_c[:, t, :, :].rearrange("p a b -> p (a b)"), ident)
                        last.then_inc(selT_up, 1)
                    pe.wait_ge(xg_lo_ok, before("xg_lo_ok", l) + g * KD + KD)
                    pe.wait_ge(selT_ok, before("selT_ok", l) + g * ns + ns)
                    for i, (j, matrix, half, part) in enumerate(LOADS):
                        if matrix != "down":
                            if j and matrix == "gate" and part == 0:
                                pe.wait_ge(hid_ok, before("hid_ok", l) + g * 8 + (2 * (j - 1) + half + 1))
                            product(g, i, ps[2 * half + (matrix == "up")], lambda k: xg_hi[:, k, j, :], lambda k: xg_lo[:, k, j, :],
                                    GRAIN * part, part)
                            if turned_after(i) is not None:
                                hidden_turned(g, turned_after(i))
                            continue
                        if half == 0 and part == 0:
                            pe.wait_ge(hidT_dve, before("hidT_dve", l) + g * 8 + (2 * j + 2))
                        if j and part == 0:
                            pe.wait_ge(ye_ok, before("ye_ok", l) + g * 8 + (2 * (j - 1) + half + 1))
                        product(g, i, ps[6 + half], lambda k: hidT_hi[:, k, :], lambda k: hidT_lo[:, k, :], GRAIN * part, part)
                        if turned_after(i) is not None:
                            hidden_turned(g, turned_after(i))
                    pe.wait_ge(ye_ok, before("ye_ok", l) + g * 8 + 8)
                    q = 0
                    for t in q_tiles(l):
                        for half in range(2):
                            if q >= 4:
                                pe.wait_ge(x_ok, before("x_ok", l) + g * nq + (q - 3))
                            cols = slice(512 * half, 512 * half + 512)
                            if t >= CT:
                                for p in range(2):
                                    last = mm(ps[q % 4][:, :], selT_l[:, p, tile(t - CT)], ye_l[:, p, cols], start=p == 0, stop=p == 1)
                            else:
                                last = mm(ps[q % 4][:, :], selT_c[:, tile(t)], ye_c[:, cols], start=True, stop=True)
                            last.then_inc(sc_up, 1)
                            q += 1

            for l in range(DEPTH):
                modulation(l)
                norm_transposes(l, 0)
                project(l, "gqk")
                project(l, "ga")
                project(l, "gv")
                gates(l)
                chunk_states(l)
                project(l, "og")
                gla_outputs(l)
                project(l, "naqk")
                project(l, "navdq")
                project(l, "dkv")
                jobs_done(pe, l, "dkv")
                attention(l, 0)
                latent_heads(l)
                attention(l, 1)
                merge(l)
                norm_transposes(l, 1)
                route(l)
                experts(l)

        @block.scalar
        def _(act):
            do = nc.scalar.activation
            own = [0]

            def link(ins):
                own[0] += 1
                ins.then_inc(act_own, 1)
                act.wait_ge(act_own, own[0])

            def copies(l, name):
                for i, (_, width, kind, where, dst, scale) in enumerate(projections(l)[name]):
                    n = first_job(l, name) + i
                    if n % 2 == 0:
                        act.wait_ge(proj_up, before("proj_up", l) + n + 1)
                        m, size = (width, where.stop - where.start) if kind == "F" else (P, width)
                        do(dst, ps[n % 4][0:m, 0:size], ACT.Copy, scale=scale).then_inc(proj_act, 1)

            def squares(s, junk):
                t0 = NT - NORMS[s]
                for t in range(t0, NT):
                    do(junk[:, t - (CT if s == 2 * DEPTH else 0), :], x_sb[:, t, :], ACT.Square, accum_out=st[:, t:t + 1]
                       ).then_inc(nrm_ss, 1)
                act.wait_ge(nrm_ms, s + 1)
                do(st[:, 16 + t0:16 + NT], st[:, 8 + t0:8 + NT], ACT.Sqrt).then_inc(nrm_root, 1)

            def modulate(l, i):
                s = 2 * l + i
                for k in range(KD):
                    act.wait_ge(hl_up, KD * s + k + 1)
                    do(hT[:, k, LAT], ps[2 + k % 2][:, :], ACT.Identity, scale=scl[:, i, k, 0:1],
                       bias=modT[l][:, 24 * i + k, 0:1]).then_inc(h_lat, 1)

            def attention(l, i):
                idx = 2 * l + i
                us = units(l)
                n = len(us)

                def exps(u):
                    t = us[u][1]
                    act.wait_ge(s_max, before("s_max", idx) + u + 1)
                    if u >= 2:
                        act.wait_ge(p_up, before("p_up", idx) + u - 1)
                        act.wait_ge(o_ok, before("o_ok", idx) + u - 1)
                    c = 32 + 8 * (u % 2)
                    if t >= CT:
                        src = s_bias[:, u % 2, :] if i == 0 else ps[2 * (u % 2)][:, :]
                        do(prob[:, u % 2, LAT], src, ACT.Exp, bias=st[:, c + 2:c + 3], accum_out=st[:, c + 3:c + 4])
                    do(prob[:, u % 2, CX], ps[2 * (u % 2) + 1][:, 0:CTX], ACT.Exp, bias=st[:, c + 2:c + 3],
                       accum_out=st[:, c + 4:c + 5]).then_inc(s_exp, 1)

                def copy(u):
                    if us[u][1] < CT:
                        return
                    act.wait_ge(p_up, before("p_up", idx) + u + 1)
                    if u >= 2:
                        act.wait_ge(o_up, before("o_up", idx) + u - 1)
                    do(probT[:, u % 2, CT:NT, :].rearrange("p a b -> p (a b)"), ps[4][:, :], ACT.Copy).then_inc(p_act, 1)

                for u in range(n + 1):
                    if u < n:
                        exps(u)
                    if u >= 1:
                        copy(u - 1)

            for l in range(DEPTH):
                if l == 0:
                    act.wait_ge(vecs_ok, 1)
                    do(silc[:, :, :], vT[:, R_C:R_C + 16].rearrange("p (a b) -> p a b", a=2), ACT.Silu).then_inc(silu_ok, 1)
                    act.wait_ge(x_in, 32)
                    act.wait_ge(started, 1)
                else:
                    act.wait_ge(x_ok, before("x_ok", l - 1) + moe_done(l - 1))
                squares(2 * l, xn1)
                act.wait_ge(mod_ok, before("mod_ok", l) + 1)
                modulate(l, 0)
                for name in ("gqk", "ga", "gv"):
                    copies(l, name)
                for u in range(4):
                    d, kt = u // 2, u % 2
                    if u:
                        act.wait_ge(g_scan, before("g_scan", l) + u)
                    for i, seg in enumerate((LAT, CX)):
                        act.wait_ge(z_up, before("z_up", l) + 2 * u + i + 1)
                        do(softp[:, seg], ps[4 + 2 * (u % 2) + i][:, 0:seg.stop - seg.start], ACT.Abs,
                           bias=col((R_BF, R_BB)[d] + kt)).then_inc(z_act, 1)
                    act.wait_ge(z_act, before("z_act", l) + 2 * u + 2)
                    link(do(softp, softp, ACT.Exp, scale=-1.0))
                    do(softp, softp, ACT.Ln, bias=1.0).then_inc(sp_ok, 1)
                    act.wait_ge(g_scan, before("g_scan", l) + u + 1)
                    if u:
                        act.wait_ge(ke_ok, before("ke_ok", l) + u)
                    do(e_pos, b_cum, ACT.Exp, scale=1.0 / 16).then_inc(g_exp, 1)
                    do(e_neg, b_cum, ACT.Exp, scale=-1.0 / 16).then_inc(g_exp, 1)
                    for i in range(2):
                        act.wait_ge(ke_up, before("ke_up", l) + 2 * u + i + 1)
                        ts = slice(CT, NT) if i == 0 else slice(0, CT)
                        m = ts.stop - ts.start
                        do(ke_tok[:, d, ts, tile(kt)], ps[i][:, 0:m * P].rearrange("p (a b) -> p a b", a=m), ACT.Copy
                           ).then_inc(ke_tok_ok, 1)
                act.wait_ge(ke_ok, before("ke_ok", l) + 4)
                copies(l, "og")
                jobs_done(act, l, "og")
                for ti, t in enumerate(q_tiles(l)):
                    do(g_og[:, t, :], g_og[:, t, :], ACT.Silu).then_inc(og_silu, 1)
                for ti, t in enumerate(q_tiles(l)):
                    act.wait_ge(go_up, before("go_up", l) + H * ti + H)
                    if ti >= 2:
                        act.wait_ge(goT_up, before("goT_up", l) + ti - 1)
                    for odd in range(2):
                        do(g_o[:, ti % 2, odd:H:2, :], ps[2 + 2 * (ti % 2) + odd][:, 0:2 * P].rearrange("p (a b) -> p a b", a=2),
                           ACT.Copy).then_inc(go_copied, 1)
                    act.wait_ge(go_ms, before("go_ms", l) + ti + 1)
                    do(stm[:, 2, 0:H], stm[:, 1, 0:H], ACT.Sqrt).then_inc(go_root, 1)
                for name in ("naqk", "navdq", "dkv"):
                    copies(l, name)
                attention(l, 0)
                jobs_done(act, l, "dkv")
                for t in range(NT):
                    if t in q_tiles(l):
                        do(s_bias[:, t % 2, 0:QR], dqb[:, t, 0:QR], ACT.Square, accum_out=mst[:, 0, 6 + t:7 + t])
                    last = do(s_bias[:, t % 2, QR:QR + KVR], dqb[:, t, QR:QR + KVR], ACT.Square, accum_out=mst[:, 0, t:t + 1])
                    if t % 2 and t < NT - 1:
                        link(last)
                last.then_inc(mla_ss, 1)
                act.wait_ge(mla_ms, before("mla_ms", l) + 1)
                do(mst[:, 2, :], mst[:, 1, :], ACT.Sqrt).then_inc(mla_root, 1)
                n = 0
                for f in range(3):
                    for seg in ((LAT, CX) if f == 2 else segments(l)):
                        act.wait_ge(mlaT_up, before("mlaT_up", l) + n + 1)
                        dst = dkvnT[:, seg] if f == 2 else dqnT[:, f, seg]
                        do(dst, ps[n % 4][:, 0:seg.stop - seg.start], ACT.Copy, scale=col(R_QN + f)).then_inc(mlaT_ok, 1)
                        n += 1
                q0 = q_tiles(l)[0]
                for t in range(NT):
                    act.wait_ge(qk_up, before("qk_up", l) + t + 1)
                    if t:
                        act.wait_ge(qkT_up, before("qkT_up", l) + t)
                    qs = ps[4 + 2 * (t % 2)][:, 0:H * DQK].rearrange("p (h d) -> p h d", h=H)
                    kv = ps[5 + 2 * (t % 2)][:, :].rearrange("p (h d) -> p h d", h=H)
                    if t >= q0:
                        w = DH if t >= CT else DQK
                        do(q_tok[:, :, 0:w], qs[:, :, 0:w], ACT.Copy)
                    do(k_tok[:, :, 0:DH], kv[:, :, 0:DH], ACT.Copy)
                    do(mv[:, t, :, :], kv[:, :, DH:128], ACT.Copy).then_inc(q_nope, 1)
                    if t >= q0:
                        act.wait_ge(qkT_up, before("qkT_up", l) + t + 1)
                        do(qT[0:DQK, :, tile(t)], ps[0][0:DQK, :].rearrange("p (h d) -> p h d", h=H), ACT.Copy,
                           scale=DQK ** -0.5).then_inc(qkT_act, 1)
                attention(l, 1)
                q = 0
                for j in range(KD):
                    for seg in segments(l):
                        size = seg.stop - seg.start
                        for b in range(3):
                            act.wait_ge(m_up, before("m_up", l) + q + 1)
                            if q >= 2:
                                act.wait_ge(m_ok, before("m_ok", l) + q - 1)
                            do(sig[q % 2][:, 0:size], ps[2 * (q % 4)][:, 0:size], ACT.Sigmoid).then_inc(m_sig, 1)
                            q += 1
                n = 0
                for i in range(2):
                    for s in range(NSEG[l]):
                        for half in range(2):
                            act.wait_ge(grow_up, before("grow_up", l) + n + 1)
                            cols = slice(512 * half, 512 * half + 512)
                            if i == 0:
                                do(gate_row[:, s, cols], ps[n % 2][:, :], ACT.Copy).then_inc(grow_ok, 1)
                            else:
                                r = slice(0, CAPL) if s == 0 else slice(CAPL, CAPL + CAPC)
                                do(gate5[r, cols], ps[n % 2][r, :], ACT.Copy).then_inc(grow_ok, 1)
                            n += 1
                act.wait_ge(y_ok, before("y_ok", l) + 2 * NQ[l])
                squares(2 * l + 1, xn2)
                modulate(l, 1)
                act.wait_ge(aff_sh, before("aff_sh", l) + 1)
                do(aff[:, q0:NT, :], aff[:, q0:NT, :], ACT.Exp).then_inc(aff_exp, 1)
                has_ctx = NSEG[l] - 1
                ns = 2 + has_ctx
                with act.Fori(0, TURNS) as g:
                    def high(i):
                        act.wait_ge(ex_in[i % SLOTS], 16 * TURNS * PER_TURN // SLOTS * l + g * (16 * PER_TURN // SLOTS)
                                    + 16 * (i // SLOTS + 1))
                        act.wait_ge(w_used, before("w_used", l) + g * PER_TURN + (i + 1 + SLOTS - HI_SLOTS))
                        do(w_hi[:, i % HI_SLOTS, :, :], w_raw[i % SLOTS], ACT.Copy).then_inc(w_hi_ok, 1)

                    def silu(j, half):
                        act.wait_ge(w_used, before("w_used", l) + g * PER_TURN + used(j, "gate", half))
                        if j:
                            act.wait_ge(hid_ok, before("hid_ok", l) + g * 8 + (2 * (j - 1) + half + 1))
                        do(g_act[0:ROWS, half, :], ps[2 * half][0:ROWS, :], ACT.Silu).then_inc(gu_silu, 1)

                    def hidden_high(j):
                        if j:
                            act.wait_ge(w_used, before("w_used", l) + g * PER_TURN + used(j - 1, "down", 1))
                        for b in range(2):
                            act.wait_ge(hidT_up, before("hidT_up", l) + g * 8 + (2 * j + b + 1))
                            do(hidT_hi[:, 4 * b:4 * b + 4, :], ps[4 + b][:, 0:4 * ROWS].rearrange("p (a b) -> p a b", a=4), ACT.Copy
                               ).then_inc(hidT_act, 1)

                    for i in range(HI_SLOTS):
                        high(i)
                    for dt in range(KD):
                        act.wait_ge(xg_up, before("xg_up", l) + g * KD + (dt + 1))
                        if dt >= 2:
                            act.wait_ge(xg_lo_ok, before("xg_lo_ok", l) + g * KD + (dt - 1))
                        for s in range(1 + has_ctx):
                            c, n = ((0, CAPL), (CAPL, CAPC))[s]
                            last = do(xg_sum[:, dt % 2, GE * c:GE * (c + n)], ps[4 + dt % 2][:, GE * c:GE * (c + n)], ACT.Identity,
                                      scale=scl[:, 1, dt, s:s + 1], bias=modT[l][:, 24 + dt, s:s + 1])
                        last.then_inc(xg_sum_ok, 1)
                        act.wait_ge(xg_sum_ok, before("xg_sum_ok", l) + g * KD + (dt + 1))
                        for s in range(1 + has_ctx):
                            c, n = ((0, CAPL), (CAPL, CAPC))[s]
                            last = do(xg_hi[:, dt, :, c:c + n], xg_sum[:, dt % 2, GE * c:GE * (c + n)].rearrange("p (a b) -> p a b", a=GE),
                                      ACT.Copy)
                        last.then_inc(xg_hi_ok, 1)
                    for p in range(2):
                        act.wait_ge(selT_up, before("selT_up", l) + g * ns + (p + 1))
                        do(selT_l[:, p, :], ps[6 + p][:, :], ACT.Copy).then_inc(selT_ok, 1)
                    if has_ctx:
                        act.wait_ge(selT_up, before("selT_up", l) + g * ns + 3)
                        do(selT_c, ps[0][:, 0:CTX], ACT.Copy).then_inc(selT_ok, 1)
                    for i in range(HI_SLOTS, PER_TURN + HI_SLOTS):
                        j, matrix, half, part = LOADS[i - HI_SLOTS]
                        if part == 1 and matrix == "gate":
                            silu(j, half)
                        if i < PER_TURN:
                            high(i)
                        if turned_after(i - HI_SLOTS) is not None:
                            hidden_high(turned_after(i - HI_SLOTS))
            act.wait_ge(x_ok, before("x_ok", DEPTH - 1) + moe_done(DEPTH - 1))
            squares(2 * DEPTH, fin)

        @block.vector
        def _(dve):
            v = nc.vector
            own = [0]

            def link(ins):
                own[0] += 1
                ins.then_inc(dve_own, 1)
                dve.wait_ge(dve_own, own[0])

            def copies(l, name):
                for i, (_, width, kind, where, dst, scale) in enumerate(projections(l)[name]):
                    n = first_job(l, name) + i
                    if n % 2:
                        dve.wait_ge(proj_up, before("proj_up", l) + n + 1)
                        m, size = (width, where.stop - where.start) if kind == "F" else (P, width)
                        v.tensor_scalar(dst, ps[n % 4][0:m, 0:size], scale, None, ALU.mult).then_inc(proj_dve, 1)

            def root(s):
                t0 = NT - NORMS[s]
                dve.wait_ge(nrm_ss, sum(NORMS[:s + 1]))
                v.tensor_scalar(st[:, 8 + t0:8 + NT], st[:, t0:NT], 1.0 / D, EPS, ALU.mult, ALU.add).then_inc(nrm_ms, 1)
                dve.wait_ge(nrm_root, s + 1)
                link(v.reciprocal(st[:, 24 + t0:24 + NT], st[:, 16 + t0:16 + NT]))
                return t0

            def scaled(s, xn):
                for t in range(root(s), NT):
                    v.tensor_scalar(xn[:, t, :], x_sb[:, t, :], st[:, 24 + t:25 + t], None, ALU.mult).then_inc(xn_ok, 1)

            def modulation_rows(events):
                for h, k in events:
                    if k == KD - 1:
                        dve.wait_ge(ada_up, h + 1)
                        if h:
                            dve.wait_ge(ada_turned, h)
                        v.tensor_copy(ada_row[:, :], ada_bank(h)[0:2, 0:256]).then_inc(ada_copied, 1)
                    if k is None:
                        dve.wait_ge(ada_turned, h + 1)
                        m = 2 * (h % 24)
                        v.tensor_copy(modT[h // 24][:, m:m + 2, :], ada_bank(h)[:, 256:260].rearrange("p (a b) -> p a b", b=2)
                                      ).then_inc(ada_raw, 1)

            def biased(l, ms):
                link(v.tensor_tensor(modT[l][:, ms, :], modT[l][:, ms, :],
                                     vT[:, R_AB + ms.start:R_AB + ms.stop].unsqueeze(2).to_broadcast([P, ms.stop - ms.start, 2]),
                                     ALU.add))

            def gains(l, i):
                return v.scalar_tensor_tensor(scl[:, i, :, :], modT[l][:, 24 * i + 8:24 * i + 16, :], 1.0,
                                              vT[:, R_N1 + 8 * i:R_N1 + 8 * i + 8].unsqueeze(2).to_broadcast([P, KD, 2]),
                                              ALU.add, ALU.mult)

            def modulate(l, i):
                s = 2 * l + i
                if CTX_NORMS[s]:
                    for k in range(KD):
                        dve.wait_ge(hc_up, KD * sum(CTX_NORMS[:s]) + k + 1)
                        v.tensor_scalar(hT[:, k, CX], ps[4 + k % 2][:, 0:CTX], scl[:, i, k, 1:2], modT[l][:, 24 * i + k, 1:2],
                                        ALU.mult, ALU.add).then_inc(h_ctx, 1)

            def attention(l, i):
                idx = 2 * l + i
                us = units(l)
                n = len(us)

                def maxima(u):
                    h, t = us[u]
                    dve.wait_ge(s_up, before("s_up", idx) + u + 1)
                    if u >= 2:
                        dve.wait_ge(s_exp, before("s_exp", idx) + u - 1)
                    c = 32 + 8 * (u % 2)
                    lat, cx = ps[2 * (u % 2)], ps[2 * (u % 2) + 1]
                    if t < CT:
                        v.tensor_reduce(st[:, c + 2:c + 3], cx[:, 0:CTX], AX_X, ALU.max, negate=True).then_inc(s_max, 1)
                        return
                    if i == 0:
                        r = 6 - 2 * (t - CT)
                        v.tensor_tensor_reduce(s_bias[:, u % 2, :], lat[:, :], bias[:, h, r:r + 8, :].rearrange("p a b -> p (a b)"),
                                               1.0, NEG, ALU.add, ALU.max, st[:, c:c + 1])
                    else:
                        v.reduce_max(st[:, c:c + 1], lat[:, :], AX_X)
                    link(v.reduce_max(st[:, c + 1:c + 2], cx[:, 0:CTX], AX_X))
                    v.tensor_reduce(st[:, c + 2:c + 3], st[:, c:c + 2], AX_X, ALU.max, negate=True).then_inc(s_max, 1)

                def copy(u):
                    dve.wait_ge(p_up, before("p_up", idx) + u + 1)
                    if u >= 2:
                        dve.wait_ge(o_up, before("o_up", idx) + u - 1)
                    v.tensor_copy(probT[:, u % 2, 0:CT, :].rearrange("p a b -> p (a b)"), ps[5][:, 0:CTX]).then_inc(p_dve, 1)

                def normalise(u):
                    h, t = us[u]
                    c = 32 + 8 * (u % 2)
                    dve.wait_ge(o_up, before("o_up", idx) + u + 1)
                    if t >= CT:
                        link(v.tensor_tensor(st[:, c + 5:c + 6], st[:, c + 3:c + 4], st[:, c + 4:c + 5], ALU.add))
                        link(v.reciprocal(st[:, c + 6:c + 7], st[:, c + 5:c + 6]))
                    else:
                        link(v.reciprocal(st[:, c + 6:c + 7], st[:, c + 4:c + 5]))
                    v.tensor_scalar(o_tok[:, t, 64 * h:64 * h + 64], ps[6 + u % O_BANKS[l]][:, 0:64], st[:, c + 6:c + 7], None, ALU.mult
                                    ).then_inc(o_ok, 1)

                for u in range(n + 2):
                    if u < n:
                        maxima(u)
                    if l == 0:
                        modulation_rows(unit_events(("na", "mla")[i], u, "early"))
                    if 1 <= u <= n:
                        copy(u - 1)
                    if u >= 2:
                        normalise(u - 2)
                    if l == 0:
                        modulation_rows(unit_events(("na", "mla")[i], u, "last"))
                for ti, t in enumerate(q_tiles(l)):
                    dve.wait_ge(oT_up, before("oT_up", idx) + ti + 1)
                    v.tensor_copy(oT[:, 2 * i:2 * i + 2, tile(t)], ps[4 + ti % 2][:, 0:256].rearrange("p (a b) -> p a b", a=2)
                                  ).then_inc(oT_ok, 1)

            def turned(l, ti):
                t = q_tiles(l)[ti]
                dve.wait_ge(goT_up, before("goT_up", l) + ti + 1)
                v.tensor_scalar(oT[:, 4:8, tile(t)], ps[6 + ti % 2][:, :].rearrange("p (h n) -> p h n", h=H), col(R_ON), None,
                                ALU.mult).then_inc(goT_ok, 1)

            dve.wait_ge(cst_in, 16)
            for l in range(DEPTH):
                q0 = q_tiles(l)[0]
                dve.wait_ge(vecs_up, before("vecs_up", l) + 1)
                v.tensor_copy(vT[:, :], ps[1][:, 0:R_ALL]).then_inc(vecs_ok, 1)
                dve.wait_ge(rpb_landed, before("rpb_landed", l) + 16)
                link(v.memset(rpb_pad[0:H * 15, :], 0.0))
                v.tensor_copy(rpb_pad[0:H * 15, 48:48 + WIN], rpb_in[0:H * 15, ::-1]).then_inc(rpb_padded, 1)
                dve.wait_ge(vecs_ok, before("vecs_ok", l) + 1)
                scaled(2 * l, xn1)
                if l == 0:
                    modulation_rows(ada_events("first", 0, 1))
                dve.wait_ge(ada_raw, (8, 48)[l])
                biased(l, slice(0, (16, 48)[l]))
                for i in range(1 + l):
                    last = gains(l, i)
                last.then_inc(mod_ok, 1)
                dve.wait_ge(mod_ok, before("mod_ok", l) + 1)
                modulate(l, 0)
                for name in ("gqk", "ga", "gv"):
                    copies(l, name)
                link(v.memset(scan_keep, 1.0))
                link(v.memset(scan_keep[:, 0:TOK:C], 0.0))
                for u in range(4):
                    d, kt = u // 2, u % 2
                    for i, seg in enumerate((LAT, CX)):
                        dve.wait_ge(z_act, before("z_act", l) + 2 * u + i + 1)
                        v.tensor_scalar(g_log[:, seg], ps[4 + 2 * (u % 2) + i][:, 0:seg.stop - seg.start],
                                        col((R_BF, R_BB)[d] + kt), 0.0, ALU.add, ALU.min).then_inc(z_dve, 1)
                    dve.wait_ge(z_dve, before("z_dve", l) + 2 * u + 2)
                    dve.wait_ge(sp_ok, before("sp_ok", l) + u + 1)
                    link(v.tensor_tensor(g_log, g_log, softp, ALU.subtract))
                    if u:
                        dve.wait_ge(g_exp, before("g_exp", l) + 2 * u)
                    way = slice(None, None, -1 if d else 1)
                    v.tensor_tensor_scan(b_cum[:, way], scan_keep, g_log[:, way], 0.0, ALU.mult, ALU.add).then_inc(g_scan, 1)
                    dve.wait_ge(g_exp, before("g_exp", l) + 2 * u + 2)
                    v.tensor_copy(decay[:, d, kt, :], e_pos[:, (0 if d else C - 1):TOK:C])
                    qs = slice(q0 * P, TOK)
                    v.tensor_tensor(qd[:, d, kt, qs], g_raw[:, kt, qs], e_pos[:, qs], ALU.mult)
                    link(v.tensor_tensor(kd[:, d, kt, :], g_raw[:, 2 + kt, :], e_neg, ALU.mult))
                    if l == 0:
                        modulation_rows(ada_events("gates", u, 4))
                    if u:
                        dve.wait_ge(ke_up, before("ke_up", l) + 2 * u)
                    v.tensor_tensor(k_end.rearrange("p (c n) -> p c n", n=C), kd[:, d, kt, :].rearrange("p (c n) -> p c n", n=C),
                                    decay[:, d, kt, :].unsqueeze(2).to_broadcast([P, NCH, C]), ALU.mult).then_inc(ke_ok, 1)
                for d in range(2):
                    last = v.memset(states[:, d, order(d)[0], :, :], 0.0)
                link(last)
                for i in range(KV_STEPS):
                    for d in range(2):
                        c, nxt = order(d)[i], order(d)[i + 1]
                        dve.wait_ge(kv_up, before("kv_up", l) + 2 * i + d + 1)
                        if i:
                            dve.wait_ge(state_ok, before("state_ok", l) + 2 * (i - 1) + d + 1)
                        for kt in range(2):
                            last = v.scalar_tensor_tensor(states[:, d, nxt, kt, :], states[:, d, c, kt, :],
                                                          decay[:, d, kt, c:c + 1], ps[4 + 2 * d + i % 2][:, tile(kt)],
                                                          ALU.mult, ALU.add)
                        last.then_inc(state_ok, 1)
                dve.wait_ge(ke_ok, before("ke_ok", l) + 4)
                copies(l, "og")
                for ti, t in enumerate(q_tiles(l)):
                    for h in range(H):
                        u = H * ti + h
                        dve.wait_ge(a_up, before("a_up", l) + u + 1)
                        link(v.tensor_tensor(a_mask[:, u % 2, :], ps[u % 2][:, 0:256], tri, ALU.mult))
                        if u >= 2:
                            dve.wait_ge(go_up, before("go_up", l) + u - 1)
                        v.tensor_tensor(a_sum[:, u % 2, :], a_mask[:, u % 2, 0:P], a_mask[:, u % 2, P:2 * P], ALU.add
                                        ).then_inc(a_ok, 1)
                    dve.wait_ge(go_copied, before("go_copied", l) + 2 * ti + 2)
                    o = g_o[:, ti % 2, :, :]
                    link(v.tensor_tensor(g_sq, o, o, ALU.mult))
                    link(v.tensor_reduce(stm[:, 0, 0:H], g_sq, AX_X, ALU.add))
                    v.tensor_scalar(stm[:, 1, 0:H], stm[:, 0, 0:H], 1.0 / DV, EPS, ALU.mult, ALU.add).then_inc(go_ms, 1)
                    dve.wait_ge(go_root, before("go_root", l) + ti + 1)
                    link(v.reciprocal(stm[:, 3, 0:H], stm[:, 2, 0:H]))
                    link(v.tensor_tensor(o, o, stm[:, 3, 0:H].unsqueeze(2).to_broadcast([P, H, DV]), ALU.mult))
                    dve.wait_ge(og_silu, before("og_silu", l) + ti + 1)
                    v.tensor_tensor(o, o, g_og[:, t, :].rearrange("p (h n) -> p h n", h=H), ALU.mult).then_inc(go_ok, 1)
                    if ti:
                        turned(l, ti - 1)
                turned(l, NQ[l] - 1)
                for name in ("naqk", "navdq", "dkv"):
                    copies(l, name)
                dve.wait_ge(bias_in, before("bias_in", l) + 128)
                for h in range(H):
                    last = v.tensor_tensor(bias[:, h, :, :], bias_raw[:, h, :, ::-1],
                                           window.unsqueeze(1).to_broadcast([P, 14, 64]), ALU.add)
                link(last)
                attention(l, 0)
                dve.wait_ge(mla_ss, before("mla_ss", l) + 1)
                v.tensor_scalar(mst[:, 1, 0:6], mst[:, 0, 0:6], 1.0 / KVR, EPS, ALU.mult, ALU.add)
                v.tensor_scalar(mst[:, 1, 6:12], mst[:, 0, 6:12], 1.0 / QR, EPS, ALU.mult, ALU.add).then_inc(mla_ms, 1)
                dve.wait_ge(mla_root, before("mla_root", l) + 1)
                link(v.reciprocal(mst[:, 3, :], mst[:, 2, :]))
                cosr = cst[:, K_COS:K_COS + 128].rearrange("p (t r) -> p t r", r=ROPE)
                sinr = cst[:, K_SIN:K_SIN + 128].rearrange("p (t r) -> p t r", r=ROPE)
                for t in range(NT):
                    if t >= q0:
                        v.tensor_scalar(dqb[:, t, 0:QR], dqb[:, t, 0:QR], mst[:, 3, 6 + t:7 + t], None, ALU.mult)
                    if t >= CT:
                        kr = dqb[:, t, QR + KVR:DMLA]
                        v.tensor_tensor(rot[:, 0, 0, :], kr, cosr[:, t - CT, :], ALU.mult)
                        for pair in range(2):
                            last = v.tensor_tensor(rot[:, 1, 0, :].rearrange("p (f r e) -> p f r e", f=2, r=2)[:, :, pair, :],
                                                   kr.rearrange("p (f r e) -> p f r e", f=2, r=2)[:, :, 1 - pair, :],
                                                   sinr[:, t - CT, :].rearrange("p (f r e) -> p f r e", f=2, r=2)[:, :, pair, :],
                                                   ALU.mult)
                        link(last)
                        link(v.tensor_tensor(kr, rot[:, 0, 0, :], rot[:, 1, 0, :], ALU.add))
                    v.tensor_scalar(dqb[:, t, QR:QR + KVR], dqb[:, t, QR:QR + KVR], mst[:, 3, t:t + 1], None, ALU.mult
                                    ).then_inc(mla_n, 1)
                for t in range(NT):
                    dve.wait_ge(q_nope, before("q_nope", l) + t + 1)
                    if t:
                        dve.wait_ge(qkT_up, before("qkT_up", l) + t)
                    if t >= CT:
                        qr = ps[4 + 2 * (t % 2)][:, 0:H * DQK].rearrange("p (h d) -> p h d", h=H)[:, :, DH:DQK]
                        v.tensor_tensor(rot[:, 0, :, :], qr, cosr[:, t - CT, :].unsqueeze(1).to_broadcast([P, H, ROPE]), ALU.mult)
                        for piece in range(4):
                            to, fr = 8 * piece, 8 * (piece ^ 1)
                            last = v.tensor_tensor(rot[:, 1, :, to:to + 8], qr[:, :, fr:fr + 8],
                                                   sinr[:, t - CT, to:to + 8].unsqueeze(1).to_broadcast([P, H, 8]), ALU.mult)
                        link(last)
                        v.tensor_tensor(q_tok[:, :, DH:DQK], rot[:, 0, :, :], rot[:, 1, :, :], ALU.add)
                    v.tensor_copy(k_tok[:, :, DH:DQK], dqb[:, t, QR + KVR:DMLA].unsqueeze(1).to_broadcast([P, H, ROPE])
                                  ).then_inc(qk_tok, 1)
                    dve.wait_ge(qkT_up, before("qkT_up", l) + t + 1)
                    v.tensor_copy(kT[0:DQK, :, tile(t)], ps[1][0:DQK, :].rearrange("p (h d) -> p h d", h=H)).then_inc(qkT_dve, 1)
                attention(l, 1)
                if l == 0:
                    dve.wait_ge(ada_raw, 48)
                    biased(l, slice(16, 48))
                    gains(l, 1).then_inc(mod_late, 1)
                    dve.wait_ge(mod_late, 1)
                q = 0
                for j in range(KD):
                    for seg in segments(l):
                        size = seg.stop - seg.start
                        for b in range(3):
                            dve.wait_ge(m_sig, before("m_sig", l) + q + 1)
                            br = ps[2 * (q % 4) + 1][:, 0:size]
                            if b == 0:
                                v.tensor_tensor(yT[:, j, seg], sig[q % 2][:, 0:size], br, ALU.mult).then_inc(m_ok, 1)
                            else:
                                link(v.tensor_tensor(branch[:, 0:size], sig[q % 2][:, 0:size], br, ALU.mult))
                                v.tensor_tensor(yT[:, j, seg], yT[:, j, seg], branch[:, 0:size], ALU.add).then_inc(m_ok, 1)
                                if b == 1:
                                    dve.wait_ge(m_ok, before("m_ok", l) + q + 1)
                            q += 1
                dve.wait_ge(m_ok, before("m_ok", l) + q)
                n = 0
                for i in range(2):
                    for s in range(NSEG[l]):
                        for half in range(2):
                            if n:
                                dve.wait_ge(grow_up, before("grow_up", l) + n)
                            m0 = 24 * i + 16 + 4 * half
                            v.tensor_tensor(diag, ident.unsqueeze(1).to_broadcast([P, 4, P]),
                                            modT[l][:, m0:m0 + 4, s:s + 1].to_broadcast([P, 4, P]), ALU.mult).then_inc(diag_ok, 1)
                            n += 1
                dve.wait_ge(grow_ok, before("grow_ok", l) + n)
                q = 0
                for t in q_tiles(l):
                    for half in range(2):
                        cols = slice(512 * half, 512 * half + 512)
                        dve.wait_ge(y_up, before("y_up", l) + q + 1)
                        if q:
                            dve.wait_ge(y_ok, before("y_ok", l) + q)
                        link(v.tensor_tensor(branch, ps[2 + q % 4][:, :], gate_row[:, 0 if t >= CT else 1, cols], ALU.mult))
                        v.tensor_tensor(x_sb[:, t, cols], x_sb[:, t, cols], branch, ALU.add).then_inc(y_ok, 1)
                        q += 1
                dve.wait_ge(y_ok, before("y_ok", l) + q)
                scaled(2 * l + 1, xn2)
                modulate(l, 1)
                dve.wait_ge(lg_up, before("lg_up", l) + 1)
                nt = NT - q0
                lg = ps[0][:, q0 * E:NT * E].rearrange("p (t e) -> p t e", e=E)
                link(v.tensor_reduce(st[:, 48 + q0:48 + NT], lg, AX_X, ALU.max))
                v.tensor_tensor(aff[:, q0:NT, :], lg, st[:, 48 + q0:48 + NT].unsqueeze(2).to_broadcast([P, nt, E]), ALU.subtract
                                ).then_inc(aff_sh, 1)
                dve.wait_ge(aff_exp, before("aff_exp", l) + 1)
                link(v.tensor_reduce(st[:, 48 + q0:48 + NT], aff[:, q0:NT, :], AX_X, ALU.add))
                link(v.reciprocal(st[:, 56 + q0:56 + NT], st[:, 48 + q0:48 + NT]))
                v.tensor_tensor(aff[:, q0:NT, :], aff[:, q0:NT, :], st[:, 56 + q0:56 + NT].unsqueeze(2).to_broadcast([P, nt, E]),
                                ALU.mult).then_inc(aff_ok, 1)
                dve.wait_ge(affT_up, before("affT_up", l) + 1)
                segs = segments(l)
                for i, seg in enumerate(segs):
                    last = v.tensor_copy(work[0:E, seg], ps[1 + i][0:E, 0:seg.stop - seg.start])
                link(last)
                for i, seg in enumerate(segs):
                    for _ in range((CAPL, CAPC)[i] // 8):
                        link(v.max(top8[0:E, i, :], work[0:E, seg]))
                        link(v.match_replace(work[0:E, seg], top8[0:E, i, :], work[0:E, seg], -1.0))
                cols = slice(q0 * P, TOK)
                link(v.tensor_scalar(chosen[0:E, cols], work[0:E, cols], 0.0, None, ALU.is_lt))
                for seg in segs:
                    last = v.tensor_tensor_scan(slotT[0:E, seg], ones[0:E, 0:1].to_broadcast([E, seg.stop - seg.start]),
                                                chosen[0:E, seg], 0.0, ALU.mult, ALU.add)
                link(last)
                link(v.tensor_tensor(slotT[0:E, cols], slotT[0:E, cols], chosen[0:E, cols], ALU.mult))
                v.tensor_scalar(slotT[0:E, cols], slotT[0:E, cols], 1.0, None, ALU.subtract).then_inc(top_ok, 1)
                dve.wait_ge(slot_up, before("slot_up", l) + 1)
                v.tensor_copy(slot[:, q0:NT, :], ps[3][:, q0 * E:NT * E].rearrange("p (t e) -> p t e", e=E)).then_inc(slot_ok, 1)
                dve.wait_ge(slot_ok, before("slot_ok", l) + 1)
                has_ctx = NSEG[l] - 1
                nq = 2 * NQ[l]
                if not has_ctx:
                    for buf in (xg_hi, xg_lo):
                        v.tensor_scalar(buf[:, :, :, CAPL:ROWS].rearrange("p a b c -> p (a b) c"),
                                        ones[:, 0:CAPC].unsqueeze(1).to_broadcast([P, KD * GE, CAPC]), 0.0, None, ALU.mult
                                        ).then_inc(xg_zero, 1)
                with dve.Fori(0, TURNS) as g:
                    def low(i):
                        dve.wait_ge(w_hi_ok, before("w_hi_ok", l) + g * PER_TURN + (i + 1))
                        v.tensor_tensor(w_lo[:, i % SLOTS, :, :], w_raw[i % SLOTS], w_hi[:, i % HI_SLOTS, :, :].bitcast(F32),
                                        ALU.subtract).then_inc(w_lo_ok, 1)

                    def hidden(j, half):
                        dve.wait_ge(w_used, before("w_used", l) + g * PER_TURN + used(j, "up", half))
                        dve.wait_ge(gu_silu, before("gu_silu", l) + g * 8 + (2 * j + half + 1))
                        if j:
                            dve.wait_ge(hidT_up, before("hidT_up", l) + g * 8 + 2 * j)
                        v.tensor_tensor(hid[0:ROWS, 512 * half:512 * half + 512], g_act[0:ROWS, half, :],
                                        ps[2 * half + 1][0:ROWS, :], ALU.mult).then_inc(hid_ok, 1)

                    def hidden_low(j):
                        if j:
                            dve.wait_ge(w_used, before("w_used", l) + g * PER_TURN + used(j - 1, "down", 1))
                        for b in range(2):
                            dve.wait_ge(hidT_act, before("hidT_act", l) + g * 8 + (2 * j + b + 1))
                            v.tensor_tensor(hidT_lo[:, 4 * b:4 * b + 4, :], ps[4 + b][:, 0:4 * ROWS].rearrange("p (a b) -> p a b", a=4),
                                            hidT_hi[:, 4 * b:4 * b + 4, :].bitcast(F32), ALU.subtract).then_inc(hidT_dve, 1)

                    def results(j, half):
                        cols = slice(512 * half, 512 * half + 512)
                        dve.wait_ge(w_used, before("w_used", l) + g * PER_TURN + used(j, "down", half))
                        r = 64 * (j % 2)
                        last = v.tensor_tensor(ye_l[r:r + 64, j // 2, cols], ps[6 + half][0:64, :], gate5[0:64, cols], ALU.mult)
                        if has_ctx:
                            last = v.tensor_tensor(ye_c[32 * j:32 * j + 32, cols], ps[6 + half][64:96, :], gate5[64:96, cols], ALU.mult)
                        last.then_inc(ye_ok, 1)

                    v.tensor_copy(turn_s[:, 0, q0:NT, :], slot[:, q0:NT, bass.ds(g * GE, GE)]).then_inc(turn_own, 1)
                    v.tensor_copy(turn_s[:, 1, q0:NT, :], aff[:, q0:NT, bass.ds(g * GE, GE)]).then_inc(turn_own, 1)
                    dve.wait_ge(turn_own, before("turn_own", l) + g * 3 + 2)
                    for t in range(q0, NT):
                        dst, i, cap = (sel_l, t - CT, CAPL) if t >= CT else (sel_c, t, CAPC)
                        last = v.tensor_tensor(dst[:, i, :, :], iota[:, 0:cap].unsqueeze(1).to_broadcast([P, GE, cap]),
                                               turn_s[:, 0, t, :].unsqueeze(2).to_broadcast([P, GE, cap]), ALU.is_equal)
                    last.then_inc(turn_own, 1)
                    dve.wait_ge(turn_own, before("turn_own", l) + g * 3 + 3)
                    for t in range(q0, NT):
                        src, dst, i, cap = (sel_l, selw_l, t - CT, CAPL) if t >= CT else (sel_c, selw_c, t, CAPC)
                        last = v.tensor_tensor(dst[:, i, :, :], src[:, i, :, :],
                                               turn_s[:, 1, t, :].unsqueeze(2).to_broadcast([P, GE, cap]), ALU.mult)
                    last.then_inc(sel_ok, 1)
                    for i in range(HI_SLOTS):
                        low(i)
                    for dt in range(KD):
                        dve.wait_ge(xg_hi_ok, before("xg_hi_ok", l) + g * KD + (dt + 1))
                        for s in range(1 + has_ctx):
                            c, n = ((0, CAPL), (CAPL, CAPC))[s]
                            last = v.tensor_tensor(xg_lo[:, dt, :, c:c + n],
                                                   xg_sum[:, dt % 2, GE * c:GE * (c + n)].rearrange("p (a b) -> p a b", a=GE),
                                                   xg_hi[:, dt, :, c:c + n].bitcast(F32), ALU.subtract)
                        last.then_inc(xg_lo_ok, 1)
                    for i in range(HI_SLOTS, PER_TURN + HI_SLOTS):
                        j, matrix, half, part = LOADS[i - HI_SLOTS]
                        if part == 1 and matrix == "up":
                            hidden(j, half)
                        if part == 1 and matrix == "down":
                            results(j, half)
                        if i < PER_TURN:
                            low(i)
                        if turned_after(i - HI_SLOTS) is not None:
                            hidden_low(turned_after(i - HI_SLOTS))
                    q = 0
                    for t in q_tiles(l):
                        for half in range(2):
                            cols = slice(512 * half, 512 * half + 512)
                            dve.wait_ge(sc_up, before("sc_up", l) + g * nq + (q + 1))
                            v.tensor_tensor(x_sb[:, t, cols], x_sb[:, t, cols], ps[q % 4][:, :], ALU.add).then_inc(x_ok, 1)
                            q += 1
            dve.wait_ge(fin_in, 16)
            for t in range(root(2 * DEPTH), NT):
                v.scalar_tensor_tensor(fin[:, t - CT, :], x_sb[:, t, :], st[:, 24 + t:25 + t], fin_row, ALU.mult, ALU.mult
                                       ).then_inc(fin_ok, 1)


NAMES = ["x", "c", "ctx", "c_ctx", "ada_w", "ada_b", "norm1", "norm2", "w_in", "na_rpb", "mla_q_norm", "mla_w_uq", "mla_kv_norm",
         "mla_w_ukv", "gla_w_af", "gla_b_af", "gla_w_ab", "gla_b_ab", "gla_o_norm", "w_br_a", "w_br_b", "w_br_c", "w_out",
         "moe_router", "moe_w_gate", "moe_w_up", "moe_w_down", "final_norm"]


def kernel(**inputs):
    import concourse.bacc as bacc
    from concourse.bass_utils import run_bass_kernel_spmd

    nc = bacc.Bacc("TRN2", target_bir_lowering=False, num_devices=1)
    arrays, aps = {}, {}
    for name in NAMES + ["constants"]:
        v = constants() if name == "constants" else np.ascontiguousarray(inputs[name])
        arrays["in_" + name] = v
        aps[name] = nc.dram_tensor("in_" + name, v.shape, mybir.dt.from_np(v.dtype), kind="ExternalInput").ap()
    out = nc.dram_tensor("out", (1, SEQ, D), F32, kind="ExternalOutput").ap()
    hybrid_kernel(nc, aps, out)
    r = run_bass_kernel_spmd(nc, [arrays], core_ids=[0])
    return r.results[0]["out"]
```

```python
from contextlib import ExitStack

import numpy as np

import concourse.bass as bass
from concourse import mybir

F32 = mybir.dt.float32
F32R = mybir.dt.float32r
ALU = mybir.AluOpType
ACT = mybir.ActivationFunctionType
AX_X = mybir.AxisListType.X

P = 128
D = 1024
KD = D // P
SEQ, CTX = 512, 256
TOK = SEQ + CTX
NT = TOK // P
CT = CTX // P
DEPTH = 2
EPS = 1e-6
GRID_W = 64
H = 4
DH = 64
ROPE = 32
QR, KVR = 256, 128
DQK = DH + ROPE
DV = 128
C = 64
NCH = TOK // C
RANK = 16
E = 16
CAPL, CAPC = 2 * SEQ // E, 2 * CTX // E
GE = 4
ROWS = CAPL + CAPC
GRAIN = 4
SLOTS, HI_SLOTS = 6, 3


def turn_loads():
    gate_up = [[(j, m, half, part) for half in range(2) for m in ("gate", "up") for part in range(2)] for j in range(GE)]
    down = [[(j, "down", half, part) for half in range(2) for part in range(2)] for j in range(GE)]
    out = list(gate_up[0])
    for j in range(GE):
        out += (gate_up[j + 1] if j + 1 < GE else []) + down[j]
    return out


BRANCH_TILES = ((0, 1), (2, 3), (4, 5, 6, 7))
M_AT = (0, KD + 2, 2 * KD + 4)
MT = 4 * KD
SPLITS = ([("w", 0)] + [("h", k) for k in range(KD)] + [("o", 0), ("o", 1), ("w", 1), ("o", 2), ("o", 3), ("w", 2)]
          + [("o", k) for k in range(4, KD)])

LOADS = turn_loads()
PER_TURN = len(LOADS)
TURN_SEL, NEXT_SEL, NEXT_GATHER = 13, 20, PER_TURN - D // P


def used(j, matrix, half):
    return SLOTS + LOADS.index((j, matrix, half, 1)) + 1


def turned_after(i):
    j, rest = LOADS[i][0], LOADS[i][1:]
    return j - 1 if j and rest == ("gate", 0, 0) else j + 1 if j == GE - 2 and rest == ("down", 1, 1) else None


NEG = -1.0e30
WIN = 31
PADW = 2 * GRID_W - 1

O_NAQK, O_NAV, O_DQ, O_DKV = 0, 512, 768, 1024
O_GQK, O_GV, O_GA, O_OG, O_M = 1184, 1696, 2208, 2240, 2752
DMLA = QR + KVR + ROPE

K_ID, K_TRI, K_IOTA, K_WIN, K_COS, K_SIN, K_ONE = 0, 128, 384, 448, 512, 640, 768
K_ALL = 896

LAT, CX = slice(CTX, TOK), slice(0, CTX)

R_AB, R_N1, R_N2, R_C, R_CC, R_QN, R_KVN, R_ON, R_BF, R_BB, R_ALL = 0, 48, 56, 64, 72, 80, 82, 83, 84, 86, 88


def constants():
    k = np.zeros((P, K_ALL), np.float32)
    k[:, K_ID:K_ID + P] = np.eye(P)
    s, t = np.arange(P)[:, None], np.arange(P)[None, :]
    same = s // C == t // C
    k[:, K_TRI:K_TRI + P] = same & (s <= t)
    k[:, K_TRI + P:K_TRI + 2 * P] = same & (s >= t)
    k[:, K_IOTA:K_IOTA + 64] = np.arange(64)
    qc = np.arange(P) % GRID_W
    start = np.clip(qc - 8, 0, GRID_W - 16)[:, None]
    kc = np.arange(GRID_W)[None, :]
    k[:, K_WIN:K_WIN + 64] = np.where((kc >= start) & (kc < start + 16), 0.0, NEG)
    inv = np.float32(10000.0) ** (-np.arange(8, dtype=np.float32) / np.float32(8))
    for tile in range(SEQ // P):
        tok = tile * P + np.arange(P)
        for half, pos in enumerate((tok // GRID_W, tok % GRID_W)):
            ang = pos.astype(np.float32)[:, None] * inv
            at = tile * ROPE + half * 16
            for pair, sign in ((0, -1.0), (1, 1.0)):
                k[:, K_COS + at + 8 * pair:K_COS + at + 8 * pair + 8] = np.cos(ang)
                k[:, K_SIN + at + 8 * pair:K_SIN + at + 8 * pair + 8] = sign * np.sin(ang)
    k[:, K_ONE:K_ONE + P] = 1.0
    return k


def hybrid_kernel(nc, a, out):
    ctx = ExitStack()
    with ctx:
        def sb(name, shape):
            return ctx.enter_context(nc.sbuf_tensor(name, shape, F32))

        def sem(name):
            return ctx.enter_context(nc.semaphore(name))

        def sems(name):
            return [sem(f"{name}{l}") for l in range(DEPTH)]

        KB = 256
        x_sb = sb("x_sb", [P, NT, D])
        with (nc.sbuf_tensor("oT", [P, KD, TOK], F32) as oT, nc.sbuf_tensor("ring", [P, 2, 16 * KB], F32) as ring,
              nc.sbuf_tensor("arena", [P, 96 * KB], F32) as arena, nc.sbuf_tensor("hT", [P, KD, TOK], F32) as hT):
            pass
        with (nc.sbuf_tensor("oT_lo", [P, KD, TOK], F32R) as oT_lo, nc.sbuf_tensor("m_lo", [P, 2, MT, P], F32R) as m_lo,
              nc.sbuf_tensor("hT_hi", [P, KD, TOK], F32R) as hT_hi, nc.sbuf_tensor("oT_hi", [P, KD, TOK], F32R) as oT_hi,
              nc.sbuf_tensor("yT_lo", [P, KD, TOK], F32R) as yT_lo, nc.sbuf_tensor("m_hi", [P, MT, P], F32R) as m_hi,
              nc.sbuf_tensor("arena_88_96", [P, 8 * KB], F32), nc.sbuf_tensor("hT_lo", [P, KD, TOK], F32R) as hT_lo):
            pass

        def sbr(name, shape):
            return ctx.enter_context(nc.sbuf_tensor(name, shape, F32R))

        sb("oT_and_ring", [P, 56 * KB])
        w_hi, w_lo = sbr("w_hi", [P, HI_SLOTS, GRAIN, 512]), sbr("w_lo", [P, SLOTS, GRAIN, 512])
        hidT_hi, hidT_lo = sbr("hidT_hi", [P, KD, ROWS]), sbr("hidT_lo", [P, KD, ROWS])
        xg_hi, xg_lo = sbr("xg_hi", [P, KD, GE, ROWS]), sbr("xg_lo", [P, KD, GE, ROWS])
        sb("rest_of_hT", [P, 18 * KB])
        cst = sb("cst", [P, K_ALL])
        vT = sb("vT", [P, R_ALL])
        silc = sb("silc", [P, 2, KD])
        modT = [sb(f"modT{l}", [P, 48, 2]) for l in range(DEPTH)]
        ada_row = sb("ada_row", [2, 256])
        scl = sb("scl", [P, 2, KD, 2])
        router = sb("router", [P, KD, E])
        st = sb("st", [P, 64])
        stm = sb("stm", [P, 4, 8])
        mst = sb("mst", [P, 4, 12])
        top8 = sb("top8", [P, 2, 8])
        turn_s = sb("turn_s", [P, 2, NT, GE])
        hTf = hT[:, :, :].rearrange("p a b -> p (a b)")
        oTf = oT[:, :, :].rearrange("p a b -> p (a b)")
        ringf = ring[:, :, :].rearrange("p a b -> p (a b)")

        def carve(flat, kb, *dims):
            n = int(np.prod(dims))
            v = flat[:, int(kb * KB):int(kb * KB) + n]
            if len(dims) == 1:
                return v
            names = "abcd"[:len(dims)]
            return v.rearrange(f"p ({' '.join(names)}) -> p {' '.join(names)}",
                               **{c: d for c, d in zip(names, dims)})

        ar = arena[:, :]
        ident = cst[:, K_ID:K_ID + P]
        tri = cst[:, K_TRI:K_TRI + 2 * P]
        iota = cst[:, K_IOTA:K_IOTA + 64]
        window = cst[:, K_WIN:K_WIN + 64]
        ones = cst[:, K_ONE:K_ONE + P]

        xn1 = carve(ar, 0, NT, D)
        xn2 = carve(oTf, 0, NT, D)
        vecs = carve(hTf, 22, P)
        g_v = carve(ar, 0, NT, H * DV)
        g_raw = carve(ar, 12, 4, TOK)
        g_og = carve(ar, 12, NT, H * DV)
        qd = carve(ar, 24, 2, 2, TOK)
        kd = carve(ar, 36, 2, 2, TOK)
        ke_tok = carve(ar, 48, 2, NT, 256)
        states = carve(ar, 60, 2, NCH, 2, DV)
        w_decay = carve(ar, 84, 2, 256)
        a_mask = carve(ar, 86, 2, 256)
        a_sum = carve(ar, 88, 2, P)
        g_o = carve(ar, 89, 2, H, DV)
        g_sq = carve(ar, 93, H, DV)
        softp = [carve(oTf, 0, TOK), carve(ar, 60, TOK)]
        g_log = [carve(oTf, 3, TOK), carve(ar, 63, TOK)]
        b_cum = [carve(oTf, 6, TOK), carve(ar, 66, TOK)]
        e_pos = [carve(oTf, 9, TOK), carve(ar, 69, TOK)]
        e_neg = [carve(oTf, 12, TOK), carve(ar, 72, TOK)]
        k_end = [carve(oTf, 15, TOK), carve(ar, 75, TOK)]
        aT = carve(oTf, 18, 2, TOK)
        scan_keep = carve(ar, 89, TOK)
        decay = sb("decay", [P, 2, 2, NCH])
        naqT, nakT = carve(ar, 0, 2, TOK), carve(ar, 6, 2, TOK)
        nav = carve(ar, 12, NT, 256)
        bias = carve(ar, 18, H, 14, 64)
        bias_raw = carve(ar, 32, H, 14, 64)
        rpb_in, rpb_pad = carve(ar, 95.5, WIN), carve(ar, 95, PADW)
        dqb = carve(ar, 46, NT, DMLA)
        dqnT, dkvnT = carve(ar, 56, 2, TOK), carve(ar, 62, TOK)
        w_uq, w_ukv = carve(ar, 65, 2, H * DQK), carve(ar, 68, H * 128)
        q_tok, k_tok = carve(ar, 70, H, DQK), carve(ar, 71.5, H, DQK)
        rot = carve(ar, 73, 2, H, ROPE)
        s_bias = carve(ar, 74, 2, SEQ)
        qT, kT = carve(ar, 0, H, TOK), carve(ar, 32, H, TOK)
        mv = carve(ar, 12, NT, H, DH)
        prob = carve(ar, 78, 2, TOK)
        probT = carve(ar, 84, 2, NT, P)
        o_tok = carve(ar, 90, NT, 256)
        yT = carve(ar, 48, KD, TOK)
        sig, branch = [carve(ar, 88, SEQ), carve(ar, 90, SEQ)], carve(ar, 92, SEQ)
        gate_row = carve(ar, 88, 2, D)
        diag, gated = carve(oTf, 0, 4, P), carve(ar, 24, SEQ)
        out_hi_at = [t.rearrange("p (k n) -> p k n", n=512)
                     for t in (m_hi[:, :, :].rearrange("p a b -> p (a b)"), oT_hi[:, :, :].rearrange("p a b -> p (a b)")[:, 8 * KB:24 * KB])]
        w_raw = [carve(ar, 24 + 8 * i, GRAIN, 512) for i in range(SLOTS)]
        work, chosen, slotT = carve(hTf, 6, TOK), carve(hTf, 9, TOK), carve(hTf, 12, TOK)
        ye_l, ye_c = carve(hTf, 6, 2, D), carve(hTf, 14, D)
        xg_sum = carve(hTf, 18, 2, GE * ROWS)
        hid = carve(ringf, 0, D)
        g_act = carve(ringf, 7, 2, 512)
        sel_l, selw_l = carve(ringf, 11, 4, GE, CAPL), carve(ringf, 15, 4, GE, CAPL)
        sel_c, selw_c = carve(ringf, 19, CT, GE, CAPC), carve(ringf, 20, CT, GE, CAPC)
        selT_l, selT_c = carve(ringf, 21, 2, SEQ), carve(ringf, 25, CTX)
        gate5 = carve(ringf, 26, D)
        aff, slot = carve(hTf, 21, NT, E), carve(hTf, 21.5, NT, E)
        fin_row = carve(ar, 0, D)
        fin = carve(ar, 4, SEQ // P, D)

        ps = [ctx.enter_context(nc.psum_tensor(f"ps{i}", [P, 512], F32)) for i in range(8)]
        rpb_scratch = [nc.dram_tensor(f"rpb_scratch{l}", [H * 15, PADW], F32, kind="Internal").ap()
                       for l in range(DEPTH)]

        ADA = {"first": 4, "gates": 8, "na": 6, "mla": 6}

        def ada_first(stage):
            names = list(ADA)
            return sum(ADA[n] for n in names[:names.index(stage)])

        def ada_events(stage, point, points):
            h0, n, events = 2 * ada_first(stage), 2 * ADA[stage] * KD, []
            for i in range(n * point // points, n * (point + 1) // points):
                events.append((h0 + i // KD, i % KD))
                if i >= KD and i % KD == 3:
                    events.append((h0 + i // KD - 1, None))
            if point == points - 1:
                events.append((h0 + 2 * ADA[stage] - 1, None))
            return events

        def unit_events(stage, u, place):
            h = 2 * ada_first(stage) + u // 2
            if u // 2 >= 2 * ADA[stage]:
                return []
            return {(0, "later"): [(h, k) for k in range(5)], (1, "early"): [(h, k) for k in range(5, KD)],
                    (1, "last"): [(h, None)]}.get((u % 2, place), [])

        def ada_bank(h):
            return ps[7] if h >= 2 * ada_first("na") else ps[2 + h % 2]

        def ada_loads(stage):
            g0 = ada_first(stage)
            return [("ada", g, a["ada_w"][g // 12][:, 512 * (g % 12):512 * (g % 12) + 512]) for g in range(g0, g0 + ADA[stage])]

        def in_loads(l, *names):
            at = {"gqk": (O_GQK, 512), "ga": (O_GA, 32), "gv": (O_GV, 512), "og": (O_OG, 512),
                  "naqk": (O_NAQK, 512), "navdq": (O_NAV, 512), "dkv": (O_DKV, 160)}
            return [(name, l, a["w_in"][l][:, at[name][0]:at[name][0] + at[name][1]]) for name in names]

        ring_loads = ada_loads("first")
        for l in range(DEPTH):
            ring_loads += in_loads(l, "gqk", "ga", "gv") + (ada_loads("gates") if l == 0 else [])
            ring_loads += in_loads(l, "og")
            ring_loads += in_loads(l, "naqk", "navdq", "dkv") + (ada_loads("na") + ada_loads("mla") if l == 0 else [])
            ring_loads += [("m", (l, j), None) for j in range(KD)]
            ring_loads += [("out", (l, half), a["w_out"][l][:, 512 * half:512 * half + 512]) for half in range(2)]
        ring_at = {load[0:2]: n for n, load in enumerate(ring_loads)}

        def ring_view(n, w, rows=KD):
            return carve(ringf, 16 * (n % 2), rows, w)

        def segments(l):
            return (LAT, CX) if l < DEPTH - 1 else (LAT,)

        def q_tiles(l):
            return list(range(NT)) if l < DEPTH - 1 else list(range(CT, NT))

        def projections(l):
            jobs = {"gqk": [], "ga": [], "gv": [], "og": [], "naqk": [], "navdq": [], "dkv": []}
            for c in range(4):
                for seg in (segments(l) if c < 2 else (LAT, CX)):
                    jobs["gqk"].append((c * P, P, "F", seg, g_raw[:, c, seg], DH ** -0.5 if c < 2 else 1.0))
                    jobs["naqk"].append((c * P, P, "F", seg, (naqT if c < 2 else nakT)[:, c % 2, seg],
                                         DH ** -0.5 if c < 2 else 1.0))
            for d in range(2):
                for seg in (LAT, CX):
                    jobs["ga"].append((RANK * d, RANK, "F", seg, aT[0:RANK, d, seg], 1.0))
            for t in range(NT):
                jobs["gv"].append((0, 512, "T", t, g_v[:, t, :], 1.0))
                if t in q_tiles(l):
                    jobs["og"].append((0, 512, "T", t, g_og[:, t, :], 1.0))
                jobs["navdq"].append((0, 256, "T", t, nav[:, t, :], 1.0))
                if t in q_tiles(l):
                    jobs["navdq"].append((256, 256, "T", t, dqb[:, t, 0:QR], 1.0))
                jobs["dkv"].append((0, 160, "T", t, dqb[:, t, QR:DMLA], 1.0))
            return jobs

        WIDTH = {"gqk": 512, "ga": 32, "gv": 512, "og": 512, "naqk": 512, "navdq": 512, "dkv": 160}
        ORDER = ("gqk", "ga", "gv", "og", "naqk", "navdq", "dkv")

        def first_job(l, name):
            js = projections(l)
            return sum(len(js[g]) for g in ORDER[:ORDER.index(name)])

        def last_job(l, name):
            return first_job(l, name) + len(projections(l)[name])

        cst_in, x_in = sem("cst_in"), sem("x_in")
        ring_in = [sem("ring_in0"), sem("ring_in1")]
        ada_up, ada_copied, ada_turned, ada_raw = sem("ada_up"), sem("ada_copied"), sem("ada_turned"), sem("ada_raw")
        vec_in, small_in, mla_in = sem("vec_in"), sem("small_in"), sem("mla_in")
        rpb_landed, rpb_flat, bias_in = sem("rpb_landed"), sem("rpb_flat"), sem("bias_in")
        rpb_padded, bias_ready = sem("rpb_padded"), sem("bias_ready")
        vecs_up, vecs_ok = sem("vecs_up"), sem("vecs_ok")
        silu_ok, mod_ok, mod_late = sem("silu_ok"), sem("mod_ok"), sem("mod_late")
        nrm_ss, nrm_ms, nrm_root = sem("nrm_ss"), sem("nrm_ms"), sem("nrm_root")
        xn_ok = sem("xn_ok")
        hl_up, hc_up, h_lat, h_ctx = sem("hl_up"), sem("hc_up"), sem("h_lat"), sem("h_ctx")
        proj_up, proj_act, proj_dve = sem("proj_up"), sem("proj_act"), sem("proj_dve")
        z_up, z_act, z_dve = sem("z_up"), sem("z_act"), sem("z_dve")
        sp_ok = sem("sp_ok")
        g_scan, g_exp, ke_ok, ke_up, ke_tok_ok = (sem("g_scan"), sem("g_exp"), sem("ke_ok"), sem("ke_up"),
                                                  sem("ke_tok_ok"))
        kv_up, state_ok = sem("kv_up"), sem("state_ok")
        a_up, a_ok, go_up, go_copied, go_ok, goT_up, goT_ok = (
            sem("a_up"), sem("a_ok"), sem("go_up"), sem("go_copied"), sem("go_ok"), sem("goT_up"),
            sem("goT_ok"))
        og_silu, go_ms, go_root = sem("og_silu"), sem("go_ms"), sem("go_root")
        s_up, s_max, s_exp = [sem(n) for n in ("s_up", "s_max", "s_exp")]
        p_up, p_act, p_dve = [sem(n) for n in ("p_up", "p_act", "p_dve")]
        o_up, o_ok, oT_up, oT_ok = [sem(n) for n in ("o_up", "o_ok", "oT_up", "oT_ok")]
        mla_ss, mla_ms, mla_root, mla_n = sem("mla_ss"), sem("mla_ms"), sem("mla_root"), sem("mla_n")
        mlaT_up, mlaT_ok = sem("mlaT_up"), sem("mlaT_ok")
        qkT_dve = sem("qkT_dve")
        qk_up, q_nope, qk_tok, qkT_up, qkT_act = (sem("qk_up"), sem("q_nope"), sem("qk_tok"), sem("qkT_up"),
                                                 sem("qkT_act"))
        part_hi, part_lo, out_hi, out_lo = sem("part_hi"), sem("part_lo"), sem("out_hi"), sem("out_lo")
        m_up, m_sig, m_ok = sem("m_up"), sem("m_sig"), sem("m_ok")
        diag_ok, grow_up, grow_ok = sem("diag_ok"), sem("grow_up"), sem("grow_ok")
        y_up, y_ok = sem("y_up"), sem("y_ok")
        lg_up, aff_exp, aff_sh, aff_ok, affT_up, top_ok, slot_up, slot_ok = (
            sem("lg_up"), sem("aff_exp"), sem("aff_sh"), sem("aff_ok"), sem("affT_up"), sem("top_ok"),
            sem("slot_up"), sem("slot_ok"))
        ex_in = [sem(f"ex_in{i}") for i in range(SLOTS)]
        w_hi_ok, w_lo_ok, w_used = sem("w_hi_ok"), sem("w_lo_ok"), sem("w_used")
        sel_ok, selT_up, selT_ok = sem("sel_ok"), sem("selT_up"), sem("selT_ok")
        xg_up, xg_sum_ok, xg_hi_ok, xg_lo_ok = sem("xg_up"), sem("xg_sum_ok"), sem("xg_hi_ok"), sem("xg_lo_ok")
        xg_zero = sem("xg_zero")
        gu_silu, hid_ok = sem("gu_silu"), sem("hid_ok")
        hidT_up, hidT_act, hidT_dve = sem("hidT_up"), sem("hidT_act"), sem("hidT_dve")
        ye_ok, sc_up, x_ok = sem("ye_ok"), sem("sc_up"), sem("x_ok")
        fin_in, fin_ok, stored = sem("fin_in"), sem("fin_ok"), sem("stored")
        dve_own, act_own = sem("dve_own"), sem("act_own")
        turn_own = sem("turn_own")
        started = sem("started")

        NJ = [sum(len(v) for v in projections(l).values()) for l in range(DEPTH)]
        NSEG = [len(segments(l)) for l in range(DEPTH)]
        O_BANKS = [1, 2]
        NQ = [len(q_tiles(l)) for l in range(DEPTH)]
        UNITS = [H * n for n in NQ]
        NORMS = [n for l in range(DEPTH) for n in (NT, NQ[l])] + [SEQ // P]
        CTX_NORMS = [n for l in range(DEPTH) for n in (1, NSEG[l] - 1)]

        def col(row):
            return vT[:, row:row + 1]

        def moe_done(l):
            return E // GE * 2 * NQ[l]

        def ring_count(n):
            return 16 * sum(6 if ring_loads[i][0] == "m" else 1 for i in range(n % 2, n + 1, 2))

        def tile(t):
            return slice(t * P, (t + 1) * P)

        def jobs_done(eng, l, name):
            n = last_job(l, name)
            eng.wait_ge(proj_act, before("proj_act", l) + (n + 1) // 2)
            eng.wait_ge(proj_dve, before("proj_dve", l) + n // 2)

        def units(l):
            return [(h, t) for h in range(H) for t in q_tiles(l)]

        def order(d):
            c = list(range(CTX // C)), list(range(CTX // C, NCH))
            return c[0] + c[1] if d == 0 else c[0][::-1] + c[1][::-1]

        KV_STEPS = NCH - 1

        def before(name, l):
            if name in ATTENTION:
                return sum(ATTENTION[name](i // 2) for i in range(l))
            return sum(COUNTS[name](i) if callable(COUNTS[name]) else COUNTS[name] for i in range(l))

        ATTENTION = {n: lambda l: UNITS[l] for n in ("s_up", "s_max", "s_exp", "p_up", "p_dve", "o_up", "o_ok")}
        ATTENTION |= {"p_act": lambda l: H * (NT - CT), "oT_up": lambda l: NQ[l], "oT_ok": lambda l: NQ[l]}
        TURNS = E // GE
        SPLIT = len(SPLITS) + 3 * (KD - 1)

        def split_count(l, kind, k, j=0):
            return before("part_lo", l) + (SPLITS.index((kind, k)) + 1 if j == 0 else len(SPLITS) + 3 * (j - 1) + k + 1)

        def w_tiles(b):
            return slice(M_AT[b], M_AT[b] + KD + len(BRANCH_TILES[b]))

        def out_operands(l, half):
            n, cols = ring_at[("out", (l, half))], slice(q_tiles(l)[0] * P, TOK)
            out = []
            for k in range(KD):
                if half == 0:
                    out.append((yT[:, k, cols], hT_hi[:, k, cols], yT_lo[:, k, cols]))
                out.append((ring_view(n, 512)[:, k, :], out_hi_at[half][:, k, :], out_low(n)[:, k, :]))
            return out

        def out_low(n):
            return m_lo[:, n % 2, :, :].rearrange("p a b -> p (a b)").rearrange("p (k n) -> p k n", n=512)

        def operand(l, n, kind, k):
            if kind == "w":
                return ring_view(n, P, MT)[:, w_tiles(k), :], m_hi[:, w_tiles(k), :], m_lo[:, n % 2, w_tiles(k), :]
            cols = slice(q_tiles(l)[0] * P, TOK)
            return [t[:, k, cols] for t in ((hT, hT_hi, hT_lo) if kind == "h" else (oT, oT_hi, oT_lo))]

        COUNTS = {
            "vec_in": 160, "small_in": 48, "mla_in": 32, "rpb_landed": 16, "rpb_flat": 16, "bias_in": 128,
            "part_hi": SPLIT, "part_lo": SPLIT, "out_hi": 3 * KD, "out_lo": 3 * KD,
            "proj_up": lambda l: NJ[l], "proj_act": lambda l: (NJ[l] + 1) // 2, "proj_dve": lambda l: NJ[l] // 2,
            "z_up": 8, "z_act": 8, "z_dve": 8, "sp_ok": 4, "g_scan": 4, "g_exp": 8, "ke_ok": 4, "ke_up": 8, "ke_tok_ok": 8,
            "kv_up": 2 * KV_STEPS, "state_ok": 2 * KV_STEPS, "go_copied": lambda l: 2 * NQ[l],
            "mla_n": NT, "mlaT_up": lambda l: 2 * NSEG[l] + 2, "mlaT_ok": lambda l: 2 * NSEG[l] + 2,
            "qk_up": NT, "q_nope": NT, "qk_tok": NT, "qkT_up": NT, "qkT_act": lambda l: NQ[l], "qkT_dve": NT,
            "y_up": lambda l: 2 * NQ[l], "y_ok": lambda l: 2 * NQ[l],
            "sel_ok": TURNS, "selT_up": lambda l: TURNS * (1 + NSEG[l]), "selT_ok": lambda l: TURNS * (1 + NSEG[l]),
            "xg_up": KD * TURNS, "xg_sum_ok": KD * TURNS, "xg_hi_ok": KD * TURNS, "xg_lo_ok": KD * TURNS,
            "w_hi_ok": PER_TURN * TURNS, "w_lo_ok": PER_TURN * TURNS, "w_used": PER_TURN * TURNS,
            "gu_silu": 2 * E, "hid_ok": 2 * E, "hidT_up": 2 * E, "hidT_act": 2 * E, "hidT_dve": 2 * E, "ye_ok": 2 * E, "turn_own": 3 * TURNS,
            "sc_up": lambda l: 2 * TURNS * NQ[l], "x_ok": lambda l: 2 * TURNS * NQ[l],
        }
        COUNTS |= {n: 1 for n in ("rpb_padded", "vecs_up", "vecs_ok", "mod_ok", "mla_ss", "mla_ms",
                                  "mla_root", "lg_up", "aff_exp", "aff_sh", "aff_ok", "affT_up", "top_ok", "slot_up",
                                  "slot_ok")}
        COUNTS |= {n: lambda l: UNITS[l] for n in ("a_up", "a_ok", "go_up")}
        COUNTS |= {n: lambda l: NQ[l] for n in ("go_ok", "goT_up", "goT_ok", "og_silu", "go_ms", "go_root")}
        COUNTS |= {n: lambda l: 24 * NSEG[l] for n in ("m_up", "m_sig", "m_ok")}
        COUNTS |= {n: lambda l: 4 * NSEG[l] for n in ("diag_ok", "grow_up", "grow_ok")}

        block = ctx.enter_context(nc.Block())


        @block.sync
        def _(sp):
            sp.dma_start(cst[:, :], a["constants"]).then_inc(cst_in, 16)

            def slot_read(n):
                kind, which, _ = ring_loads[n]
                if kind == "ada":
                    sp.wait_ge(ada_up, 2 * which + 2)
                elif kind == "m":
                    l, j = which
                    sp.wait_ge(m_up, before("m_up", l) + 3 * NSEG[l] * (j + 1))
                elif kind == "out":
                    l, half = which
                    sp.wait_ge(y_up, before("y_up", l) + NQ[l] * (half + 1))
                else:
                    sp.wait_ge(proj_up, before("proj_up", which) + last_job(which, kind))

            def expert_loads(l, g):
                for i, (j, matrix, half, part) in enumerate(LOADS):
                    sp.wait_ge(w_used, before("w_used", l) + g * PER_TURN + (i + 1))
                    src = a["moe_w_" + matrix][l, bass.ds(g * GE + j, 1), part * 512:part * 512 + 512, 512 * half:512 * half + 512]
                    sp.dma_start(w_raw[i % SLOTS], src.rearrange("e (k p) n -> p (e k) n", p=P)
                                 ).then_inc(ex_in[i % SLOTS], 16)

            for n, (kind, which, src) in enumerate(ring_loads):
                if n == 2:
                    sp.dma_start(x_sb[:, 0:CT, :], a["ctx"][0].rearrange("(t p) d -> p t d", p=P)).then_inc(x_in, 16)
                    sp.dma_start(x_sb[:, CT:NT, :], a["x"][0].rearrange("(t p) d -> p t d", p=P)).then_inc(x_in, 16)
                if n >= 2:
                    slot_read(n - 2)
                if (kind, which) == ("gqk", 1):
                    sp.wait_ge(x_ok, before("x_ok", 0) + moe_done(0))
                if kind == "m":
                    l, j = which
                    for b in range(3):
                        c0 = O_M + b * D + j * P
                        at = M_AT[b]
                        sp.dma_start(ring_view(n, P, MT)[:, at:at + KD, :],
                                     a["w_in"][l][:, c0:c0 + P].rearrange("(k p) n -> p k n", p=P)).then_inc(ring_in[n % 2], 16)
                        sp.dma_start(ring_view(n, P, MT)[:, at + KD:w_tiles(b).stop, :],
                                     a[("w_br_a", "w_br_b", "w_br_c")[b]][l][:, j * P:(j + 1) * P].rearrange("(k p) n -> p k n", p=P)
                                     ).then_inc(ring_in[n % 2], 16)
                else:
                    sp.dma_start(ring_view(n, src.shape[1]), src.rearrange("(k p) n -> p k n", p=P)
                                 ).then_inc(ring_in[n % 2], 16)
                if kind != "out" or which[1] == 0:
                    continue
                sp.wait_ge(y_ok, before("y_ok", l) + 2 * NQ[l])
                with sp.Fori(0, TURNS) as g:
                    expert_loads(l, g)
            sp.wait_ge(fin_ok, SEQ // P)
            sp.dma_start(out[0].rearrange("(t p) d -> p t d", p=P), fin).then_inc(stored, 16)
            sp.wait_ge(stored, 16)

        @block.gpsimd
        def _(pool):
            nc.gpsimd.memset(mst[:, 0:2, :], 1.0).then_inc(w_used, SLOTS)
            nc.gpsimd.memset(mst[:, 2:4, :], 1.0).then_inc(started, 1)
            for l in range(DEPTH):
                if l:
                    pool.wait_ge(lg_up, before("lg_up", l - 1) + 1)
                rows = ((R_AB, 48, a["ada_b"][l]), (R_N1, 8, a["norm1"][l]), (R_N2, 8, a["norm2"][l]), (R_C, 8, a["c"][0]),
                        (R_CC, 8, a["c_ctx"]), (R_QN, 2, a["mla_q_norm"][l]), (R_KVN, 1, a["mla_kv_norm"][l]),
                        (R_ON, 1, a["gla_o_norm"][l]), (R_BF, 2, a["gla_b_af"][l]), (R_BB, 2, a["gla_b_ab"][l]))
                for r, n, src in rows:
                    pool.dma_start(vecs[r:r + n, :], src.rearrange("(r c) -> r c", c=P)).then_inc(vec_in, 16)
                pool.dma_start(router[:, :, :], a["moe_router"][l].rearrange("(k p) e -> p k e", p=P)
                               ).then_inc(small_in, 16)
                if l:
                    pool.wait_ge(x_ok, before("x_ok", l - 1) + moe_done(l - 1))
                for d, name in enumerate(("gla_w_af", "gla_w_ab")):
                    pool.dma_start(w_decay[0:RANK, d, :], a[name][l]).then_inc(small_in, 16)
                pool.dma_start(rpb_in[0:H * 15, :], a["na_rpb"][l].rearrange("h r c -> (h r) c")).then_inc(rpb_landed, 16)
                pool.wait_ge(rpb_padded, before("rpb_padded", l) + 1)
                pool.dma_start(rpb_scratch[l], rpb_pad[0:H * 15, :]).then_inc(rpb_flat, 16)
                pool.wait_ge(rpb_flat, before("rpb_flat", l) + 16)
                pool.wait_ge(goT_ok, before("goT_ok", l) + NQ[l])
                for half in range(2):
                    for h in range(H):
                        src = bass.AP(rpb_scratch[l].tensor, (h * 15 + 1 - half) * PADW, [[1, 64], [PADW, 14], [1, 64]])
                        pool.dma_start(bias_raw[64 * half:64 * half + 64, h, :, :], src).then_inc(bias_in, 16)
                pool.dma_start(w_uq, a["mla_w_uq"][l].rearrange("(k p) n -> p k n", p=P)).then_inc(mla_in, 16)
                pool.dma_start(w_ukv, a["mla_w_ukv"][l]).then_inc(mla_in, 16)
            pool.wait_ge(x_ok, before("x_ok", DEPTH - 1) + moe_done(DEPTH - 1))
            fn = a["final_norm"]
            pool.dma_start(fin_row, bass.AP(fn.tensor, fn.offset, [[0, P], [1, D]])).then_inc(fin_in, 16)

        @block.tensor
        def _(pe):
            mm, tr = nc.tensor.matmul, nc.tensor.transpose

            def ring_entry(kind, which, width):
                n = ring_at[(kind, which)]
                pe.wait_ge(ring_in[n % 2], ring_count(n))
                return ring_view(n, width)

            def modulation_products(events):
                for h, k in events:
                    alone = h >= 2 * ada_first("na")
                    if k is None:
                        pe.wait_ge(ada_copied, h + 1)
                        for c in range(2):
                            last = tr(ada_bank(h)[:, 256 + 2 * c:258 + 2 * c], ada_row[:, tile(c)], ident[0:2, 0:2])
                        last.then_inc(ada_turned, 1)
                        continue
                    if k == 0 and h >= 2:
                        pe.wait_ge(ada_raw, h if alone else h - 1)
                    w = ring_entry("ada", h // 2, 512) if (h % 2, k) == (0, 0) else ring_view(ring_at[("ada", h // 2)], 512)
                    last = mm(ada_bank(h)[0:2, 0:256], silc[:, :, k], w[:, k, 256 * (h % 2):256 * (h % 2) + 256],
                              start=k == 0, stop=k == KD - 1)
                    if k == KD - 1:
                        last.then_inc(ada_up, 1)

            def project(l, name):
                w = ring_entry(name, l, WIDTH[name])
                jobs = projections(l)[name]
                for i, (c0, width, kind, where, _, _) in enumerate(jobs):
                    n = first_job(l, name) + i
                    if n >= 4:
                        pe.wait_ge((proj_act, proj_dve)[n % 2], before(("proj_act", "proj_dve")[n % 2], l) + (n - 4) // 2 + 1)
                    for k in range(KD):
                        if kind == "F":
                            size = where.stop - where.start
                            last = mm(ps[n % 4][0:width, 0:size], w[:, k, c0:c0 + width], hT[:, k, where],
                                      start=k == 0, stop=k == KD - 1)
                        else:
                            last = mm(ps[n % 4][:, 0:width], hT[:, k, tile(where)], w[:, k, c0:c0 + width],
                                      start=k == 0, stop=k == KD - 1)
                    last.then_inc(proj_up, 1)

            def norm_transposes(l, i):
                s = 2 * l + i
                xn = (xn1, xn2)[i]
                pe.wait_ge(xn_ok, sum(NORMS[:s + 1]))
                for k in range(KD):
                    if k >= 2:
                        pe.wait_ge(h_lat, KD * s + k - 1)
                    for t in range(CT, NT):
                        last = tr(ps[2 + k % 2][:, tile(t - CT)], xn[:, t, tile(k)], ident)
                    last.then_inc(hl_up, 1)
                    if CTX_NORMS[s]:
                        if k >= 2:
                            pe.wait_ge(h_ctx, KD * sum(CTX_NORMS[:s]) + k - 1)
                        for t in range(CT):
                            last = tr(ps[4 + k % 2][:, tile(t)], xn[:, t, tile(k)], ident)
                        last.then_inc(hc_up, 1)
                pe.wait_ge(h_lat, KD * (s + 1))
                pe.wait_ge(h_ctx, KD * sum(CTX_NORMS[:s + 1]))

            def modulation(l):
                pe.wait_ge(cst_in, 16)
                pe.wait_ge(vec_in, before("vec_in", l) + 160)
                if l:
                    pe.wait_ge(x_ok, before("x_ok", l - 1) + moe_done(l - 1))
                tr(ps[1][:, 0:R_ALL], vecs[0:R_ALL, :], ident[0:R_ALL, 0:R_ALL]).then_inc(vecs_up, 1)
                if l == 0:
                    pe.wait_ge(silu_ok, 1)
                    modulation_products(ada_events("first", 0, 1))
                    pe.wait_ge(ada_raw, 2 * ADA["first"])

            def gates(l):
                jobs_done(pe, l, "gv")
                pe.wait_ge(small_in, before("small_in", l) + 48)
                decay_logits(l, 0)
                for u in range(4):
                    if u < 3:
                        decay_logits(l, u + 1)
                    if u:
                        keys_end(l, u - 1)
                    if l == 0:
                        modulation_products(ada_events("gates", u, 4))
                keys_end(l, 3)
                pe.wait_ge(ada_raw, 2 * ada_first("na"))

            def decay_logits(l, u):
                d, kt = u // 2, u % 2
                for i, seg in enumerate((LAT, CX)):
                    if u >= 2:
                        pe.wait_ge(z_dve, before("z_dve", l) + 2 * (u - 2) + i + 1)
                    mm(ps[4 + 2 * (u % 2) + i][:, 0:seg.stop - seg.start], w_decay[0:RANK, d, tile(kt)],
                       aT[0:RANK, d, seg], start=True, stop=True).then_inc(z_up, 1)

            def keys_end(l, u):
                pe.wait_ge(ke_ok, before("ke_ok", l) + u + 1)
                if u:
                    pe.wait_ge(ke_tok_ok, before("ke_tok_ok", l) + 2 * u)
                for t in range(CT, NT):
                    last = tr(ps[0][:, tile(t - CT)], k_end[u % 2][:, tile(t)], ident)
                last.then_inc(ke_up, 1)
                for t in range(CT):
                    last = tr(ps[1][:, tile(t)], k_end[u % 2][:, tile(t)], ident)
                last.then_inc(ke_up, 1)

            def chunk_states(l):
                pe.wait_ge(ke_tok_ok, before("ke_tok_ok", l) + 8)
                pe.wait_ge(z_dve, before("z_dve", l) + 8)
                for i in range(KV_STEPS):
                    for d in range(2):
                        c = order(d)[i]
                        t, r = c // 2, C * (c % 2)
                        bank = ps[4 + 2 * d + i % 2]
                        if i >= 2:
                            pe.wait_ge(state_ok, before("state_ok", l) + 2 * (i - 2) + d + 1)
                        for h in range(H):
                            last = mm(bank[64 * (h % 2):64 * (h % 2) + 64, tile(h // 2)],
                                      ke_tok[r:r + C, d, t, 64 * h:64 * h + 64], g_v[r:r + C, t, h * DV:(h + 1) * DV],
                                      start=True, stop=True)
                        last.then_inc(kv_up, 1)

            def gla_outputs(l):
                tiles = q_tiles(l)
                jobs_done(pe, l, "og")
                pe.wait_ge(state_ok, before("state_ok", l) + 2 * KV_STEPS)

                def scores(u):
                    t, h = tiles[u // H], u % H
                    r = 64 * (h % 2)
                    if u >= 2:
                        pe.wait_ge(a_ok, before("a_ok", l) + u - 1)
                    for d in range(2):
                        last = mm(ps[u % 2][:, tile(d)], kd[r:r + 64, d, h // 2, tile(t)], qd[r:r + 64, d, h // 2, tile(t)],
                                  start=True, stop=True)
                    last.then_inc(a_up, 1)

                def values(u):
                    ti, h = u // H, u % H
                    t, r = tiles[ti], 64 * (h % 2)
                    o = ps[2 + 2 * (ti % 2) + h % 2]
                    if h == 0 and ti >= 2:
                        pe.wait_ge(go_copied, before("go_copied", l) + 2 * (ti - 1))
                    pe.wait_ge(a_ok, before("a_ok", l) + u + 1)
                    mm(o[:, tile(h // 2)], a_sum[:, u % 2, :], g_v[:, t, h * DV:(h + 1) * DV], start=True, stop=False,
                       skip_group_check=True)
                    for c in range(2):
                        for d in range(2):
                            last = mm(o[C * c:C * c + C, tile(h // 2)], qd[r:r + 64, d, h // 2, t * P + C * c:t * P + C * c + C],
                                      states[r:r + 64, d, 2 * t + c, h // 2, :], start=False, stop=True, skip_group_check=True)
                    last.then_inc(go_up, 1)

                def turn(ti):
                    pe.wait_ge(go_ok, before("go_ok", l) + ti + 1)
                    if ti >= 2:
                        pe.wait_ge(goT_ok, before("goT_ok", l) + ti - 1)
                    for h in range(H):
                        last = tr(ps[6 + ti % 2][:, tile(h)], g_o[:, ti % 2, h, :], ident)
                    last.then_inc(goT_up, 1)

                n = H * len(tiles)
                for u in range(n + 1):
                    if u < n:
                        scores(u)
                    if u >= 1:
                        values(u - 1)
                    if u > H and u % H == 3:
                        turn(u // H - 1)
                turn(len(tiles) - 1)
                pe.wait_ge(goT_ok, before("goT_ok", l) + len(tiles))

            def attention(l, i):
                idx = 2 * l + i
                us = units(l)
                n = len(us)
                lats = [sum(1 for h, t in us[:u + 1] if t >= CT) for u in range(n)]

                def scores(u):
                    h, t = us[u]
                    if i == 0:
                        r = 64 * (h % 2)
                        q, kk = naqT[r:r + 64, h // 2, tile(t)], nakT[r:r + 64, h // 2, :]
                    else:
                        q, kk = qT[0:DQK, h, tile(t)], kT[0:DQK, h, :]
                    if u >= 2:
                        pe.wait_ge(s_exp, before("s_exp", idx) + u - 1)
                    if t >= CT:
                        mm(ps[2 * (u % 2)][:, :], q, kk[:, LAT], start=True, stop=True)
                    mm(ps[2 * (u % 2) + 1][:, 0:CTX], q, kk[:, CX], start=True, stop=True).then_inc(s_up, 1)

                def turn(u):
                    pe.wait_ge(s_exp, before("s_exp", idx) + u + 1)
                    if us[u][1] >= CT:
                        if lats[u] >= 2:
                            pe.wait_ge(p_act, before("p_act", idx) + lats[u] - 1)
                        for t in range(CT, NT):
                            tr(ps[4][:, tile(t - CT)], prob[:, u % 2, tile(t)], ident)
                    if u:
                        pe.wait_ge(p_dve, before("p_dve", idx) + u)
                    for t in range(CT):
                        last = tr(ps[5][:, tile(t)], prob[:, u % 2, tile(t)], ident)
                    last.then_inc(p_up, 1)

                def values(u):
                    h, t = us[u]
                    if t >= CT:
                        pe.wait_ge(p_act, before("p_act", idx) + lats[u])
                    pe.wait_ge(p_dve, before("p_dve", idx) + u + 1)
                    if u >= O_BANKS[l]:
                        pe.wait_ge(o_ok, before("o_ok", idx) + u + 1 - O_BANKS[l])
                    keys = range(NT if t >= CT else CT)
                    for kt in keys:
                        v = nav[:, kt, 64 * h:64 * h + 64] if i == 0 else mv[:, kt, h, :]
                        last = mm(ps[6 + u % O_BANKS[l]][:, 0:64], probT[:, u % 2, kt, :], v, start=kt == 0, stop=kt == keys[-1])
                    last.then_inc(o_up, 1)

                for u in range(n + 2):
                    if u < n:
                        scores(u)
                    if l == 0:
                        modulation_products(unit_events(("na", "mla")[i], u, "early"))
                    if 1 <= u <= n:
                        turn(u - 1)
                    if l == 0:
                        modulation_products(unit_events(("na", "mla")[i], u, "later"))
                    if u >= 2:
                        values(u - 2)
                    if l == 0:
                        modulation_products(unit_events(("na", "mla")[i], u, "last"))
                pe.wait_ge(o_ok, before("o_ok", idx) + n)
                for ti, t in enumerate(q_tiles(l)):
                    if ti >= 2:
                        pe.wait_ge(oT_ok, before("oT_ok", idx) + ti - 1)
                    for k in range(2):
                        last = tr(ps[4 + ti % 2][:, tile(k)], o_tok[:, t, tile(k)], ident)
                    last.then_inc(oT_up, 1)
                pe.wait_ge(oT_ok, before("oT_ok", idx) + NQ[l])

            def latent_heads(l):
                pe.wait_ge(mla_n, before("mla_n", l) + NT)
                n = 0
                for f in range(3):
                    for seg in ((LAT, CX) if f == 2 else segments(l)):
                        if n >= 4:
                            pe.wait_ge(mlaT_ok, before("mlaT_ok", l) + n - 3)
                        tiles = range(CT, NT) if seg is LAT else range(CT)
                        for t in tiles:
                            last = tr(ps[n % 4][:, tile(t - tiles[0])], dqb[:, t, tile(f)], ident)
                        last.then_inc(mlaT_up, 1)
                        n += 1
                pe.wait_ge(mlaT_ok, before("mlaT_ok", l) + n)
                pe.wait_ge(mla_in, before("mla_in", l) + 32)

                def up(t):
                    if t >= 2:
                        pe.wait_ge(qk_tok, before("qk_tok", l) + t - 1)
                    if t in q_tiles(l):
                        for k in range(2):
                            mm(ps[4 + 2 * (t % 2)][:, 0:H * DQK], dqnT[:, k, tile(t)], w_uq[:, k, :], start=k == 0, stop=k == 1)
                    mm(ps[5 + 2 * (t % 2)][:, :], dkvnT[:, tile(t)], w_ukv, start=True, stop=True).then_inc(qk_up, 1)

                def turn(t):
                    pe.wait_ge(qk_tok, before("qk_tok", l) + t + 1)
                    if t in q_tiles(l):
                        if t > q_tiles(l)[0]:
                            pe.wait_ge(qkT_act, before("qkT_act", l) + t - q_tiles(l)[0])
                        for h in range(H):
                            tr(ps[0][0:DQK, tile(h)], q_tok[:, h, :], ident)
                    if t:
                        pe.wait_ge(qkT_dve, before("qkT_dve", l) + t)
                    for h in range(H):
                        last = tr(ps[1][0:DQK, tile(h)], k_tok[:, h, :], ident)
                    last.then_inc(qkT_up, 1)

                up(0)
                for t in range(NT):
                    if t + 1 < NT:
                        up(t + 1)
                    turn(t)
                pe.wait_ge(qkT_act, before("qkT_act", l) + NQ[l])
                pe.wait_ge(qkT_dve, before("qkT_dve", l) + NT)

            def merge(l):
                q = 0
                for j in range(KD):
                    n = ring_at[("m", (l, j))]
                    for si, seg in enumerate(segments(l)):
                        size = seg.stop - seg.start
                        for b, kts in enumerate(BRANCH_TILES):
                            if q >= 4:
                                pe.wait_ge(m_ok, before("m_ok", l) + q - 3)
                            if si == 0:
                                pe.wait_ge(part_lo, split_count(l, "w", b, j))
                            steps = ([(0, M_AT[b] + k, "h", k) for k in range(KD)]
                                     + [(1, M_AT[b] + KD + i, "o", k) for i, k in enumerate(kts)])
                            for bank, at, kind, k in steps:
                                if j == 0 and si == 0 and (kind == "o" or b == 0):
                                    pe.wait_ge(part_lo, split_count(l, kind, k))
                                x_hi, x_lo = (hT_hi, hT_lo) if kind == "h" else (oT_hi, oT_lo)
                                hi, lo = m_hi[:, at, :], m_lo[:, n % 2, at, :]
                                for i, (w, x) in enumerate(((hi, x_hi), (hi, x_lo), (lo, x_hi))):
                                    last = mm(ps[2 * (q % 4) + bank][:, 0:size], w, x[:, k, seg],
                                              start=i == 0 and k == (0, kts[0])[bank],
                                              stop=i == 2 and k == (KD - 1, kts[-1])[bank])
                            last.then_inc(m_up, 1)
                            q += 1
                pe.wait_ge(m_ok, before("m_ok", l) + q)
                q = 0
                for half in range(2):
                    hi, lo = out_hi_at[half], out_low(ring_at[("out", (l, half))])
                    for t in q_tiles(l):
                        if q == 2:
                            gate_rows(l, 0)
                        if q >= 4:
                            pe.wait_ge(y_ok, before("y_ok", l) + q - 3)
                        for k in range(KD):
                            if t == q_tiles(l)[0]:
                                pe.wait_ge(out_lo, before("out_lo", l) + (2 * KD + k + 1 if half else 2 * k + 2))
                            for i, (y, w) in enumerate(((hT_hi, hi), (yT_lo, hi), (hT_hi, lo))):
                                last = mm(ps[2 + q % 4][:, :], y[:, k, tile(t)], w[:, k, :], start=i == 0 and k == 0,
                                          stop=i == 2 and k == KD - 1)
                        last.then_inc(y_up, 1)
                        q += 1
                gate_rows(l, 1)
                pe.wait_ge(y_ok, before("y_ok", l) + q)
                pe.wait_ge(grow_ok, before("grow_ok", l) + 4 * NSEG[l])

            def gate_rows(l, i):
                for n in range(2 * NSEG[l] * i, 2 * NSEG[l] * (i + 1)):
                    pe.wait_ge(diag_ok, before("diag_ok", l) + n + 1)
                    if n >= 2:
                        pe.wait_ge(grow_ok, before("grow_ok", l) + n - 1)
                    mm(ps[n % 2][:, :], ones, diag.rearrange("p a b -> p (a b)"), start=True, stop=True).then_inc(grow_up, 1)

            def route(l):
                for t in q_tiles(l):
                    for k in range(KD):
                        last = mm(ps[0][:, t * E:(t + 1) * E], hT[:, k, tile(t)], router[:, k, :], start=k == 0, stop=k == KD - 1)
                last.then_inc(lg_up, 1)
                pe.wait_ge(aff_ok, before("aff_ok", l) + 1)
                for t in q_tiles(l):
                    bank, at = (ps[1], t - CT) if t >= CT else (ps[2], t)
                    last = tr(bank[0:E, tile(at)], aff[:, t, :], ident)
                last.then_inc(affT_up, 1)
                pe.wait_ge(top_ok, before("top_ok", l) + 1)
                for t in q_tiles(l):
                    last = tr(ps[3][:, t * E:(t + 1) * E], slotT[0:E, tile(t)], ident[0:E, 0:E])
                last.then_inc(slot_up, 1)

            def experts(l):
                has_ctx = NSEG[l] - 1
                ns = 2 + has_ctx
                nq = 2 * NQ[l]

                def product(g, i, bank, x_hi, x_lo, k0, part):
                    pe.wait_ge(w_lo_ok, before("w_lo_ok", l) + g * PER_TURN + (i + 1))
                    for k in range(GRAIN):
                        hi, lo = w_hi[:, i % HI_SLOTS, k, :], w_lo[:, i % SLOTS, k, :]
                        for n, (x, w) in enumerate(((x_hi, hi), (x_lo, hi), (x_hi, lo))):
                            last = mm(bank[0:ROWS, :], x(k0 + k), w, start=part == 0 and k == 0 and n == 0,
                                      stop=part == 1 and k == GRAIN - 1 and n == 2)
                    last.then_inc(w_used, 1)

                def hidden_turned(g, j):
                    pe.wait_ge(hid_ok, before("hid_ok", l) + g * 8 + (2 * j + 2))
                    if j:
                        pe.wait_ge(hidT_dve, before("hidT_dve", l) + g * 8 + 2 * j)
                    for b in range(2):
                        for k in range(4):
                            last = tr(ps[4 + b][:, k * ROWS:(k + 1) * ROWS], hid[0:ROWS, tile(4 * b + k)], ident[0:ROWS, 0:ROWS])
                        last.then_inc(hidT_up, 1)

                def gather(g, dt):
                    if dt == 0:
                        pe.wait_ge(sel_ok, before("sel_ok", l) + g + 1)
                    if dt >= 4:
                        pe.wait_ge(xg_sum_ok, before("xg_sum_ok", l) + g * KD + (dt - 3))
                    bank = ps[dt % 4]
                    for t in range(4):
                        last = mm(bank[:, 0:GE * CAPL], xn2[:, CT + t, tile(dt)], sel_l[:, t, :, :].rearrange("p a b -> p (a b)"),
                                  start=t == 0, stop=t == 3)
                    for t in range(CT * has_ctx):
                        last = mm(bank[:, GE * CAPL:GE * ROWS], xn2[:, t, tile(dt)],
                                  sel_c[:, t, :, :].rearrange("p a b -> p (a b)"), start=t == 0, stop=t == CT - 1)
                    last.then_inc(xg_up, 1)

                def selection_turned(g, first):
                    if not first:
                        pe.wait_ge(x_ok, before("x_ok", l) + g * nq)
                    for p in range(2):
                        for t in range(4):
                            last = tr(ps[6 + p][:, tile(t)], selw_l[:, t, 2 * p:2 * p + 2, :].rearrange("p a b -> p (a b)"), ident)
                        last.then_inc(selT_up, 1)
                    if has_ctx:
                        pe.wait_ge(hidT_dve, before("hidT_dve", l) + g * 8 + 2)
                        for t in range(CT):
                            last = tr(ps[5][:, tile(t)], selw_c[:, t, :, :].rearrange("p a b -> p (a b)"), ident)
                        last.then_inc(selT_up, 1)

                def scatter(g, q):
                    if q == 0:
                        pe.wait_ge(ye_ok, before("ye_ok", l) + g * 8 + 8)
                        pe.wait_ge(selT_ok, before("selT_ok", l) + g * ns + ns)
                    if q >= 2:
                        pe.wait_ge(x_ok, before("x_ok", l) + g * nq + (q - 1))
                    t, cols = q_tiles(l)[q // 2], slice(512 * (q % 2), 512 * (q % 2) + 512)
                    if t >= CT:
                        for p in range(2):
                            last = mm(ps[6 + q % 2][:, :], selT_l[:, p, tile(t - CT)], ye_l[:, p, cols], start=p == 0, stop=p == 1)
                    else:
                        last = mm(ps[6 + q % 2][:, :], selT_c[:, tile(t)], ye_c[:, cols], start=True, stop=True)
                    last.then_inc(sc_up, 1)

                def turn(g, first, final):
                    pe.wait_ge(xg_lo_ok, before("xg_lo_ok", l) + g * KD + KD)
                    for i, (j, matrix, half, part) in enumerate(LOADS):
                        if matrix != "down":
                            if j and matrix == "gate" and part == 0:
                                pe.wait_ge(hid_ok, before("hid_ok", l) + g * 8 + (2 * (j - 1) + half + 1))
                            product(g, i, ps[2 * half + (matrix == "up")], lambda k: xg_hi[:, k, j, :], lambda k: xg_lo[:, k, j, :],
                                    GRAIN * part, part)
                        else:
                            if half == 0 and part == 0:
                                pe.wait_ge(hidT_dve, before("hidT_dve", l) + g * 8 + (2 * j + 2))
                                if j == 0:
                                    pe.wait_ge(selT_ok, before("selT_ok", l) + g * ns + ns)
                            if j and part == 0:
                                pe.wait_ge(ye_ok, before("ye_ok", l) + g * 8 + (2 * (j - 1) + half + 1))
                            product(g, i, ps[6 + half], lambda k: hidT_hi[:, k, :], lambda k: hidT_lo[:, k, :], GRAIN * part, part)
                        if turned_after(i) is not None:
                            hidden_turned(g, turned_after(i))
                        if not first and i < nq:
                            scatter(g - 1, i)
                        if i == TURN_SEL:
                            selection_turned(g, first)
                        if not final and i >= NEXT_GATHER:
                            if i == NEXT_GATHER:
                                pe.wait_ge(hid_ok, before("hid_ok", l) + g * 8 + 8)
                            gather(g + 1, i - NEXT_GATHER)

                if not has_ctx:
                    pe.wait_ge(xg_zero, 2)
                for dt in range(KD):
                    gather(0, dt)
                turn(0, True, False)
                with pe.Fori(1, TURNS - 1) as g:
                    turn(g, False, False)
                turn(TURNS - 1, False, True)
                for q in range(nq):
                    scatter(TURNS - 1, q)

            for l in range(DEPTH):
                modulation(l)
                norm_transposes(l, 0)
                project(l, "gqk")
                project(l, "ga")
                project(l, "gv")
                gates(l)
                chunk_states(l)
                project(l, "og")
                gla_outputs(l)
                project(l, "naqk")
                project(l, "navdq")
                project(l, "dkv")
                jobs_done(pe, l, "dkv")
                attention(l, 0)
                latent_heads(l)
                attention(l, 1)
                merge(l)
                norm_transposes(l, 1)
                route(l)
                experts(l)

        @block.scalar
        def _(act):
            do = nc.scalar.activation
            own = [0]

            def link(ins):
                own[0] += 1
                ins.then_inc(act_own, 1)
                act.wait_ge(act_own, own[0])

            def copies(l, name):
                for i, (_, width, kind, where, dst, scale) in enumerate(projections(l)[name]):
                    n = first_job(l, name) + i
                    if n % 2 == 0:
                        act.wait_ge(proj_up, before("proj_up", l) + n + 1)
                        m, size = (width, where.stop - where.start) if kind == "F" else (P, width)
                        do(dst, ps[n % 4][0:m, 0:size], ACT.Copy, scale=scale).then_inc(proj_act, 1)

            def squares(s, junk):
                t0 = NT - NORMS[s]
                for t in range(t0, NT):
                    do(junk[:, t - (CT if s == 2 * DEPTH else 0), :], x_sb[:, t, :], ACT.Square, accum_out=st[:, t:t + 1]
                       ).then_inc(nrm_ss, 1)
                act.wait_ge(nrm_ms, s + 1)
                do(st[:, 16 + t0:16 + NT], st[:, 8 + t0:8 + NT], ACT.Sqrt).then_inc(nrm_root, 1)

            def modulate(l, i):
                s = 2 * l + i
                for k in range(KD):
                    act.wait_ge(hl_up, KD * s + k + 1)
                    do(hT[:, k, LAT], ps[2 + k % 2][:, :], ACT.Identity, scale=scl[:, i, k, 0:1],
                       bias=modT[l][:, 24 * i + k, 0:1]).then_inc(h_lat, 1)

            def attention(l, i):
                idx = 2 * l + i
                us = units(l)
                n = len(us)

                def exps(u):
                    t = us[u][1]
                    act.wait_ge(s_max, before("s_max", idx) + u + 1)
                    if u >= 2:
                        act.wait_ge(p_up, before("p_up", idx) + u - 1)
                        act.wait_ge(o_ok, before("o_ok", idx) + u - 1)
                    c = 32 + 8 * (u % 2)
                    if t >= CT:
                        src = s_bias[:, u % 2, :] if i == 0 else ps[2 * (u % 2)][:, :]
                        do(prob[:, u % 2, LAT], src, ACT.Exp, bias=st[:, c + 2:c + 3], accum_out=st[:, c + 3:c + 4])
                    do(prob[:, u % 2, CX], ps[2 * (u % 2) + 1][:, 0:CTX], ACT.Exp, bias=st[:, c + 2:c + 3],
                       accum_out=st[:, c + 4:c + 5]).then_inc(s_exp, 1)

                def copy(u):
                    if us[u][1] < CT:
                        return
                    act.wait_ge(p_up, before("p_up", idx) + u + 1)
                    if u >= 2:
                        act.wait_ge(o_up, before("o_up", idx) + u - 1)
                    do(probT[:, u % 2, CT:NT, :].rearrange("p a b -> p (a b)"), ps[4][:, :], ACT.Copy).then_inc(p_act, 1)

                for u in range(n + 1):
                    if u < n:
                        exps(u)
                    if u >= 1:
                        copy(u - 1)

            for l in range(DEPTH):
                if l == 0:
                    act.wait_ge(vecs_ok, 1)
                    do(silc[:, :, :], vT[:, R_C:R_C + 16].rearrange("p (a b) -> p a b", a=2), ACT.Silu).then_inc(silu_ok, 1)
                    act.wait_ge(x_in, 32)
                    act.wait_ge(started, 1)
                else:
                    act.wait_ge(x_ok, before("x_ok", l - 1) + moe_done(l - 1))
                squares(2 * l, xn1)
                act.wait_ge(mod_ok, before("mod_ok", l) + 1)
                modulate(l, 0)
                for name in ("gqk", "ga", "gv"):
                    copies(l, name)
                def softplus(u):
                    d, kt, sp = u // 2, u % 2, softp[u % 2]
                    if u >= 2:
                        act.wait_ge(g_scan, before("g_scan", l) + u - 1)
                    for i, seg in enumerate((LAT, CX)):
                        act.wait_ge(z_up, before("z_up", l) + 2 * u + i + 1)
                        do(sp[:, seg], ps[4 + 2 * (u % 2) + i][:, 0:seg.stop - seg.start], ACT.Abs,
                           bias=col((R_BF, R_BB)[d] + kt)).then_inc(z_act, 1)
                    act.wait_ge(z_act, before("z_act", l) + 2 * u + 2)
                    link(do(sp, sp, ACT.Exp, scale=-1.0))
                    do(sp, sp, ACT.Ln, bias=1.0).then_inc(sp_ok, 1)

                def decays(u):
                    act.wait_ge(g_scan, before("g_scan", l) + u + 1)
                    if u >= 2:
                        act.wait_ge(ke_ok, before("ke_ok", l) + u - 1)
                    do(e_pos[u % 2], b_cum[u % 2], ACT.Exp, scale=1.0 / 16).then_inc(g_exp, 1)
                    do(e_neg[u % 2], b_cum[u % 2], ACT.Exp, scale=-1.0 / 16).then_inc(g_exp, 1)

                def keys_end(u):
                    d, kt = u // 2, u % 2
                    for i in range(2):
                        act.wait_ge(ke_up, before("ke_up", l) + 2 * u + i + 1)
                        ts = slice(CT, NT) if i == 0 else slice(0, CT)
                        m = ts.stop - ts.start
                        do(ke_tok[:, d, ts, tile(kt)], ps[i][:, 0:m * P].rearrange("p (a b) -> p a b", a=m), ACT.Copy
                           ).then_inc(ke_tok_ok, 1)

                softplus(0)
                for u in range(4):
                    if u < 3:
                        softplus(u + 1)
                    decays(u)
                    if u:
                        keys_end(u - 1)
                keys_end(3)
                act.wait_ge(ke_ok, before("ke_ok", l) + 4)
                copies(l, "og")
                jobs_done(act, l, "og")
                for ti, t in enumerate(q_tiles(l)):
                    do(g_og[:, t, :], g_og[:, t, :], ACT.Silu).then_inc(og_silu, 1)
                for ti, t in enumerate(q_tiles(l)):
                    act.wait_ge(go_up, before("go_up", l) + H * ti + H)
                    if ti >= 2:
                        act.wait_ge(goT_up, before("goT_up", l) + ti - 1)
                    for odd in range(2):
                        do(g_o[:, ti % 2, odd:H:2, :], ps[2 + 2 * (ti % 2) + odd][:, 0:2 * P].rearrange("p (a b) -> p a b", a=2),
                           ACT.Copy).then_inc(go_copied, 1)
                    act.wait_ge(go_ms, before("go_ms", l) + ti + 1)
                    do(stm[:, 2, 0:H], stm[:, 1, 0:H], ACT.Sqrt).then_inc(go_root, 1)
                for name in ("naqk", "navdq", "dkv"):
                    copies(l, name)
                attention(l, 0)
                jobs_done(act, l, "dkv")
                for t in range(NT):
                    if t in q_tiles(l):
                        do(s_bias[:, t % 2, 0:QR], dqb[:, t, 0:QR], ACT.Square, accum_out=mst[:, 0, 6 + t:7 + t])
                    last = do(s_bias[:, t % 2, QR:QR + KVR], dqb[:, t, QR:QR + KVR], ACT.Square, accum_out=mst[:, 0, t:t + 1])
                    if t % 2 and t < NT - 1:
                        link(last)
                last.then_inc(mla_ss, 1)
                act.wait_ge(mla_ms, before("mla_ms", l) + 1)
                do(mst[:, 2, :], mst[:, 1, :], ACT.Sqrt).then_inc(mla_root, 1)
                n = 0
                for f in range(3):
                    for seg in ((LAT, CX) if f == 2 else segments(l)):
                        act.wait_ge(mlaT_up, before("mlaT_up", l) + n + 1)
                        dst = dkvnT[:, seg] if f == 2 else dqnT[:, f, seg]
                        do(dst, ps[n % 4][:, 0:seg.stop - seg.start], ACT.Copy, scale=col(R_QN + f)).then_inc(mlaT_ok, 1)
                        n += 1
                q0 = q_tiles(l)[0]
                for t in range(NT):
                    act.wait_ge(qk_up, before("qk_up", l) + t + 1)
                    if t:
                        act.wait_ge(qkT_up, before("qkT_up", l) + t)
                    qs = ps[4 + 2 * (t % 2)][:, 0:H * DQK].rearrange("p (h d) -> p h d", h=H)
                    kv = ps[5 + 2 * (t % 2)][:, :].rearrange("p (h d) -> p h d", h=H)
                    if t >= q0:
                        w = DH if t >= CT else DQK
                        do(q_tok[:, :, 0:w], qs[:, :, 0:w], ACT.Copy)
                    do(k_tok[:, :, 0:DH], kv[:, :, 0:DH], ACT.Copy)
                    do(mv[:, t, :, :], kv[:, :, DH:128], ACT.Copy).then_inc(q_nope, 1)
                    if t >= q0:
                        act.wait_ge(qkT_up, before("qkT_up", l) + t + 1)
                        do(qT[0:DQK, :, tile(t)], ps[0][0:DQK, :].rearrange("p (h d) -> p h d", h=H), ACT.Copy,
                           scale=DQK ** -0.5).then_inc(qkT_act, 1)
                attention(l, 1)
                act.wait_ge(oT_ok, before("oT_ok", 2 * l + 1) + NQ[l])

                def high_part(kind, k, j=0):
                    n = ring_at[("m", (l, j))]
                    if kind == "w":
                        act.wait_ge(ring_in[n % 2], ring_count(n))
                        if j:
                            act.wait_ge(m_up, before("m_up", l) + 3 * (NSEG[l] * j - 1) + k + 1)
                    raw, hi, _ = operand(l, n, kind, k)
                    do(hi, raw, ACT.Copy).then_inc(part_hi, 1)

                for kind, k in SPLITS:
                    high_part(kind, k)
                q = 0
                for j in range(KD):
                    for seg in segments(l):
                        size = seg.stop - seg.start
                        for b in range(3):
                            act.wait_ge(m_up, before("m_up", l) + q + 1)
                            if q >= 2:
                                act.wait_ge(m_ok, before("m_ok", l) + q - 1)
                            do(sig[q % 2][:, 0:size], ps[2 * (q % 4)][:, 0:size], ACT.Sigmoid).then_inc(m_sig, 1)
                            if j < KD - 1 and seg is segments(l)[-1]:
                                high_part("w", b, j + 1)
                            q += 1

                def out_high(half):
                    n = ring_at[("out", (l, half))]
                    act.wait_ge(ring_in[n % 2], ring_count(n))
                    for raw, hi, _ in out_operands(l, half):
                        do(hi, raw, ACT.Copy).then_inc(out_hi, 1)

                act.wait_ge(m_ok, before("m_ok", l) + q)
                out_high(0)
                n = 0
                for i in range(2):
                    if i == 1:
                        out_high(1)
                        act.wait_ge(y_up, before("y_up", l) + 2 * NQ[l])
                    for s in range(NSEG[l]):
                        for half in range(2):
                            act.wait_ge(grow_up, before("grow_up", l) + n + 1)
                            cols = slice(512 * half, 512 * half + 512)
                            if i == 0:
                                do(gate_row[:, s, cols], ps[n % 2][:, :], ACT.Copy).then_inc(grow_ok, 1)
                            else:
                                r = slice(0, CAPL) if s == 0 else slice(CAPL, CAPL + CAPC)
                                do(gate5[r, cols], ps[n % 2][r, :], ACT.Copy).then_inc(grow_ok, 1)
                            n += 1
                act.wait_ge(y_ok, before("y_ok", l) + 2 * NQ[l])
                squares(2 * l + 1, xn2)
                modulate(l, 1)
                act.wait_ge(aff_sh, before("aff_sh", l) + 1)
                do(aff[:, q0:NT, :], aff[:, q0:NT, :], ACT.Exp).then_inc(aff_exp, 1)
                has_ctx = NSEG[l] - 1
                ns = 2 + has_ctx

                def high(g, i):
                    act.wait_ge(ex_in[i % SLOTS], 16 * TURNS * PER_TURN // SLOTS * l + g * (16 * PER_TURN // SLOTS)
                                + 16 * (i // SLOTS + 1))
                    act.wait_ge(w_used, before("w_used", l) + g * PER_TURN + (i + 1 + SLOTS - HI_SLOTS))
                    do(w_hi[:, i % HI_SLOTS, :, :], w_raw[i % SLOTS], ACT.Copy).then_inc(w_hi_ok, 1)

                def silu(g, j, half):
                    act.wait_ge(w_used, before("w_used", l) + g * PER_TURN + used(j, "gate", half))
                    if j:
                        act.wait_ge(hid_ok, before("hid_ok", l) + g * 8 + (2 * (j - 1) + half + 1))
                    do(g_act[0:ROWS, half, :], ps[2 * half][0:ROWS, :], ACT.Silu).then_inc(gu_silu, 1)

                def hidden_high(g, j):
                    if j:
                        act.wait_ge(w_used, before("w_used", l) + g * PER_TURN + used(j - 1, "down", 1))
                    for b in range(2):
                        act.wait_ge(hidT_up, before("hidT_up", l) + g * 8 + (2 * j + b + 1))
                        do(hidT_hi[:, 4 * b:4 * b + 4, :], ps[4 + b][:, 0:4 * ROWS].rearrange("p (a b) -> p a b", a=4), ACT.Copy
                           ).then_inc(hidT_act, 1)

                def gathered(g, dt):
                    act.wait_ge(xg_up, before("xg_up", l) + g * KD + (dt + 1))
                    if dt >= 2:
                        act.wait_ge(xg_lo_ok, before("xg_lo_ok", l) + g * KD + (dt - 1))
                    for s in range(1 + has_ctx):
                        c, n = ((0, CAPL), (CAPL, CAPC))[s]
                        last = do(xg_sum[:, dt % 2, GE * c:GE * (c + n)], ps[dt % 4][:, GE * c:GE * (c + n)], ACT.Identity,
                                  scale=scl[:, 1, dt, s:s + 1], bias=modT[l][:, 24 + dt, s:s + 1])
                    last.then_inc(xg_sum_ok, 1)
                    act.wait_ge(xg_sum_ok, before("xg_sum_ok", l) + g * KD + (dt + 1))
                    for s in range(1 + has_ctx):
                        c, n = ((0, CAPL), (CAPL, CAPC))[s]
                        last = do(xg_hi[:, dt, :, c:c + n], xg_sum[:, dt % 2, GE * c:GE * (c + n)].rearrange("p (a b) -> p a b", a=GE),
                                  ACT.Copy)
                    last.then_inc(xg_hi_ok, 1)

                def selection(g):
                    for p in range(2):
                        act.wait_ge(selT_up, before("selT_up", l) + g * ns + (p + 1))
                        do(selT_l[:, p, :], ps[6 + p][:, :], ACT.Copy).then_inc(selT_ok, 1)
                    if has_ctx:
                        act.wait_ge(selT_up, before("selT_up", l) + g * ns + 3)
                        do(selT_c, ps[5][:, 0:CTX], ACT.Copy).then_inc(selT_ok, 1)

                def turn(g, final):
                    for i in range(PER_TURN):
                        j, matrix, half, part = LOADS[i]
                        if part == 1 and matrix == "gate":
                            silu(g, j, half)
                        if turned_after(i) is not None:
                            hidden_high(g, turned_after(i))
                        if not final or i + HI_SLOTS < PER_TURN:
                            high(g, i + HI_SLOTS)
                        if i == TURN_SEL:
                            selection(g)
                        if not final and i >= NEXT_GATHER:
                            gathered(g + 1, i - NEXT_GATHER)

                for i in range(HI_SLOTS):
                    high(0, i)
                for dt in range(KD):
                    gathered(0, dt)
                turn(0, False)
                with act.Fori(1, TURNS - 1) as g:
                    turn(g, False)
                turn(TURNS - 1, True)
            act.wait_ge(x_ok, before("x_ok", DEPTH - 1) + moe_done(DEPTH - 1))
            squares(2 * DEPTH, fin)

        @block.vector
        def _(dve):
            v = nc.vector
            own = [0]

            def link(ins):
                own[0] += 1
                ins.then_inc(dve_own, 1)
                dve.wait_ge(dve_own, own[0])

            def copies(l, name):
                for i, (_, width, kind, where, dst, scale) in enumerate(projections(l)[name]):
                    n = first_job(l, name) + i
                    if n % 2:
                        dve.wait_ge(proj_up, before("proj_up", l) + n + 1)
                        m, size = (width, where.stop - where.start) if kind == "F" else (P, width)
                        v.tensor_scalar(dst, ps[n % 4][0:m, 0:size], scale, None, ALU.mult).then_inc(proj_dve, 1)

            def root(s):
                t0 = NT - NORMS[s]
                dve.wait_ge(nrm_ss, sum(NORMS[:s + 1]))
                v.tensor_scalar(st[:, 8 + t0:8 + NT], st[:, t0:NT], 1.0 / D, EPS, ALU.mult, ALU.add).then_inc(nrm_ms, 1)
                dve.wait_ge(nrm_root, s + 1)
                link(v.reciprocal(st[:, 24 + t0:24 + NT], st[:, 16 + t0:16 + NT]))
                return t0

            def scaled(s, xn):
                for t in range(root(s), NT):
                    v.tensor_scalar(xn[:, t, :], x_sb[:, t, :], st[:, 24 + t:25 + t], None, ALU.mult).then_inc(xn_ok, 1)

            def modulation_rows(events):
                for h, k in events:
                    if k == KD - 1:
                        dve.wait_ge(ada_up, h + 1)
                        if h:
                            dve.wait_ge(ada_turned, h)
                        v.tensor_copy(ada_row[:, :], ada_bank(h)[0:2, 0:256]).then_inc(ada_copied, 1)
                    if k is None:
                        dve.wait_ge(ada_turned, h + 1)
                        m = 2 * (h % 24)
                        v.tensor_copy(modT[h // 24][:, m:m + 2, :], ada_bank(h)[:, 256:260].rearrange("p (a b) -> p a b", b=2)
                                      ).then_inc(ada_raw, 1)

            def biased(l, ms):
                link(v.tensor_tensor(modT[l][:, ms, :], modT[l][:, ms, :],
                                     vT[:, R_AB + ms.start:R_AB + ms.stop].unsqueeze(2).to_broadcast([P, ms.stop - ms.start, 2]),
                                     ALU.add))

            def gains(l, i):
                return v.scalar_tensor_tensor(scl[:, i, :, :], modT[l][:, 24 * i + 8:24 * i + 16, :], 1.0,
                                              vT[:, R_N1 + 8 * i:R_N1 + 8 * i + 8].unsqueeze(2).to_broadcast([P, KD, 2]),
                                              ALU.add, ALU.mult)

            def modulate(l, i):
                s = 2 * l + i
                if CTX_NORMS[s]:
                    for k in range(KD):
                        dve.wait_ge(hc_up, KD * sum(CTX_NORMS[:s]) + k + 1)
                        v.tensor_scalar(hT[:, k, CX], ps[4 + k % 2][:, 0:CTX], scl[:, i, k, 1:2], modT[l][:, 24 * i + k, 1:2],
                                        ALU.mult, ALU.add).then_inc(h_ctx, 1)

            def attention(l, i):
                idx = 2 * l + i
                us = units(l)
                n = len(us)

                def maxima(u):
                    h, t = us[u]
                    dve.wait_ge(s_up, before("s_up", idx) + u + 1)
                    if u >= 2:
                        dve.wait_ge(s_exp, before("s_exp", idx) + u - 1)
                    c = 32 + 8 * (u % 2)
                    lat, cx = ps[2 * (u % 2)], ps[2 * (u % 2) + 1]
                    if t < CT:
                        v.tensor_reduce(st[:, c + 2:c + 3], cx[:, 0:CTX], AX_X, ALU.max, negate=True).then_inc(s_max, 1)
                        return
                    if i == 0:
                        r = 6 - 2 * (t - CT)
                        v.tensor_tensor_reduce(s_bias[:, u % 2, :], lat[:, :], bias[:, h, r:r + 8, :].rearrange("p a b -> p (a b)"),
                                               1.0, NEG, ALU.add, ALU.max, st[:, c:c + 1])
                    else:
                        v.reduce_max(st[:, c:c + 1], lat[:, :], AX_X)
                    link(v.reduce_max(st[:, c + 1:c + 2], cx[:, 0:CTX], AX_X))
                    v.tensor_reduce(st[:, c + 2:c + 3], st[:, c:c + 2], AX_X, ALU.max, negate=True).then_inc(s_max, 1)

                def copy(u):
                    dve.wait_ge(p_up, before("p_up", idx) + u + 1)
                    if u >= 2:
                        dve.wait_ge(o_up, before("o_up", idx) + u - 1)
                    v.tensor_copy(probT[:, u % 2, 0:CT, :].rearrange("p a b -> p (a b)"), ps[5][:, 0:CTX]).then_inc(p_dve, 1)

                def normalise(u):
                    h, t = us[u]
                    c = 32 + 8 * (u % 2)
                    dve.wait_ge(o_up, before("o_up", idx) + u + 1)
                    if t >= CT:
                        link(v.tensor_tensor(st[:, c + 5:c + 6], st[:, c + 3:c + 4], st[:, c + 4:c + 5], ALU.add))
                        link(v.reciprocal(st[:, c + 6:c + 7], st[:, c + 5:c + 6]))
                    else:
                        link(v.reciprocal(st[:, c + 6:c + 7], st[:, c + 4:c + 5]))
                    v.tensor_scalar(o_tok[:, t, 64 * h:64 * h + 64], ps[6 + u % O_BANKS[l]][:, 0:64], st[:, c + 6:c + 7], None, ALU.mult
                                    ).then_inc(o_ok, 1)

                for u in range(n + 2):
                    if u < n:
                        maxima(u)
                    if l == 0:
                        modulation_rows(unit_events(("na", "mla")[i], u, "early"))
                    if 1 <= u <= n:
                        copy(u - 1)
                    if u >= 2:
                        normalise(u - 2)
                    if l == 0:
                        modulation_rows(unit_events(("na", "mla")[i], u, "last"))
                for ti, t in enumerate(q_tiles(l)):
                    dve.wait_ge(oT_up, before("oT_up", idx) + ti + 1)
                    v.tensor_copy(oT[:, 2 * i:2 * i + 2, tile(t)], ps[4 + ti % 2][:, 0:256].rearrange("p (a b) -> p a b", a=2)
                                  ).then_inc(oT_ok, 1)

            def turned(l, ti):
                t = q_tiles(l)[ti]
                dve.wait_ge(goT_up, before("goT_up", l) + ti + 1)
                v.tensor_scalar(oT[:, 4:8, tile(t)], ps[6 + ti % 2][:, :].rearrange("p (h n) -> p h n", h=H), col(R_ON), None,
                                ALU.mult).then_inc(goT_ok, 1)

            dve.wait_ge(cst_in, 16)
            for l in range(DEPTH):
                q0 = q_tiles(l)[0]
                dve.wait_ge(vecs_up, before("vecs_up", l) + 1)
                v.tensor_copy(vT[:, :], ps[1][:, 0:R_ALL]).then_inc(vecs_ok, 1)
                dve.wait_ge(rpb_landed, before("rpb_landed", l) + 16)
                link(v.memset(rpb_pad[0:H * 15, :], 0.0))
                v.tensor_copy(rpb_pad[0:H * 15, 48:48 + WIN], rpb_in[0:H * 15, ::-1]).then_inc(rpb_padded, 1)
                dve.wait_ge(vecs_ok, before("vecs_ok", l) + 1)
                scaled(2 * l, xn1)
                if l == 0:
                    modulation_rows(ada_events("first", 0, 1))
                dve.wait_ge(ada_raw, (8, 48)[l])
                biased(l, slice(0, (16, 48)[l]))
                for i in range(1 + l):
                    last = gains(l, i)
                last.then_inc(mod_ok, 1)
                dve.wait_ge(mod_ok, before("mod_ok", l) + 1)
                modulate(l, 0)
                for name in ("gqk", "ga", "gv"):
                    copies(l, name)
                link(v.memset(scan_keep, 1.0))
                link(v.memset(scan_keep[:, 0:TOK:C], 0.0))
                def sums(u):
                    d, kt, g = u // 2, u % 2, g_log[u % 2]
                    for i, seg in enumerate((LAT, CX)):
                        dve.wait_ge(z_act, before("z_act", l) + 2 * u + i + 1)
                        v.tensor_scalar(g[:, seg], ps[4 + 2 * (u % 2) + i][:, 0:seg.stop - seg.start],
                                        col((R_BF, R_BB)[d] + kt), 0.0, ALU.add, ALU.min).then_inc(z_dve, 1)
                    dve.wait_ge(z_dve, before("z_dve", l) + 2 * u + 2)
                    dve.wait_ge(sp_ok, before("sp_ok", l) + u + 1)
                    link(v.tensor_tensor(g, g, softp[u % 2], ALU.subtract))
                    if u >= 2:
                        dve.wait_ge(g_exp, before("g_exp", l) + 2 * (u - 1))
                    way = slice(None, None, -1 if d else 1)
                    v.tensor_tensor_scan(b_cum[u % 2][:, way], scan_keep, g[:, way], 0.0, ALU.mult, ALU.add).then_inc(g_scan, 1)

                def decayed(u):
                    d, kt = u // 2, u % 2
                    dve.wait_ge(g_exp, before("g_exp", l) + 2 * u + 2)
                    v.tensor_copy(decay[:, d, kt, :], e_pos[u % 2][:, (0 if d else C - 1):TOK:C])
                    qs = slice(q0 * P, TOK)
                    v.tensor_tensor(qd[:, d, kt, qs], g_raw[:, kt, qs], e_pos[u % 2][:, qs], ALU.mult)
                    link(v.tensor_tensor(kd[:, d, kt, :], g_raw[:, 2 + kt, :], e_neg[u % 2], ALU.mult))
                    if l == 0:
                        modulation_rows(ada_events("gates", u, 4))
                    if u >= 2:
                        dve.wait_ge(ke_up, before("ke_up", l) + 2 * (u - 1))
                    v.tensor_tensor(k_end[u % 2].rearrange("p (c n) -> p c n", n=C), kd[:, d, kt, :].rearrange("p (c n) -> p c n", n=C),
                                    decay[:, d, kt, :].unsqueeze(2).to_broadcast([P, NCH, C]), ALU.mult).then_inc(ke_ok, 1)

                sums(0)
                for u in range(4):
                    if u < 3:
                        sums(u + 1)
                    decayed(u)
                dve.wait_ge(ke_up, before("ke_up", l) + 8)
                for d in range(2):
                    last = v.memset(states[:, d, order(d)[0], :, :], 0.0)
                link(last)
                for i in range(KV_STEPS):
                    for d in range(2):
                        c, nxt = order(d)[i], order(d)[i + 1]
                        dve.wait_ge(kv_up, before("kv_up", l) + 2 * i + d + 1)
                        if i:
                            dve.wait_ge(state_ok, before("state_ok", l) + 2 * (i - 1) + d + 1)
                        for kt in range(2):
                            last = v.scalar_tensor_tensor(states[:, d, nxt, kt, :], states[:, d, c, kt, :],
                                                          decay[:, d, kt, c:c + 1], ps[4 + 2 * d + i % 2][:, tile(kt)],
                                                          ALU.mult, ALU.add)
                        last.then_inc(state_ok, 1)
                dve.wait_ge(ke_ok, before("ke_ok", l) + 4)
                copies(l, "og")
                def masked(u):
                    dve.wait_ge(a_up, before("a_up", l) + u + 1)
                    link(v.tensor_tensor(a_mask[:, u % 2, :], ps[u % 2][:, 0:256], tri, ALU.mult))
                    if u >= 2:
                        dve.wait_ge(go_up, before("go_up", l) + u - 1)
                    v.tensor_tensor(a_sum[:, u % 2, :], a_mask[:, u % 2, 0:P], a_mask[:, u % 2, P:2 * P], ALU.add
                                    ).then_inc(a_ok, 1)

                def mean_squares(ti):
                    dve.wait_ge(go_copied, before("go_copied", l) + 2 * ti + 2)
                    o = g_o[:, ti % 2, :, :]
                    link(v.tensor_tensor(g_sq, o, o, ALU.mult))
                    link(v.tensor_reduce(stm[:, 0, 0:H], g_sq, AX_X, ALU.add))
                    v.tensor_scalar(stm[:, 1, 0:H], stm[:, 0, 0:H], 1.0 / DV, EPS, ALU.mult, ALU.add).then_inc(go_ms, 1)

                def normed(ti):
                    o, t = g_o[:, ti % 2, :, :], q_tiles(l)[ti]
                    dve.wait_ge(go_root, before("go_root", l) + ti + 1)
                    link(v.reciprocal(stm[:, 3, 0:H], stm[:, 2, 0:H]))
                    link(v.tensor_tensor(o, o, stm[:, 3, 0:H].unsqueeze(2).to_broadcast([P, H, DV]), ALU.mult))
                    dve.wait_ge(og_silu, before("og_silu", l) + ti + 1)
                    v.tensor_tensor(o, o, g_og[:, t, :].rearrange("p (h n) -> p h n", h=H), ALU.mult).then_inc(go_ok, 1)

                for u in range(H * NQ[l]):
                    ti, h = u // H, u % H
                    masked(u)
                    if h == 0 and ti >= 2:
                        turned(l, ti - 2)
                    if h == 1 and ti:
                        mean_squares(ti - 1)
                    if h == 2 and ti:
                        normed(ti - 1)
                mean_squares(NQ[l] - 1)
                normed(NQ[l] - 1)
                turned(l, NQ[l] - 2)
                turned(l, NQ[l] - 1)
                for name in ("naqk", "navdq", "dkv"):
                    copies(l, name)
                dve.wait_ge(bias_in, before("bias_in", l) + 128)
                for h in range(H):
                    last = v.tensor_tensor(bias[:, h, :, :], bias_raw[:, h, :, ::-1],
                                           window.unsqueeze(1).to_broadcast([P, 14, 64]), ALU.add)
                link(last)
                attention(l, 0)
                dve.wait_ge(mla_ss, before("mla_ss", l) + 1)
                v.tensor_scalar(mst[:, 1, 0:6], mst[:, 0, 0:6], 1.0 / KVR, EPS, ALU.mult, ALU.add)
                v.tensor_scalar(mst[:, 1, 6:12], mst[:, 0, 6:12], 1.0 / QR, EPS, ALU.mult, ALU.add).then_inc(mla_ms, 1)
                dve.wait_ge(mla_root, before("mla_root", l) + 1)
                link(v.reciprocal(mst[:, 3, :], mst[:, 2, :]))
                cosr = cst[:, K_COS:K_COS + 128].rearrange("p (t r) -> p t r", r=ROPE)
                sinr = cst[:, K_SIN:K_SIN + 128].rearrange("p (t r) -> p t r", r=ROPE)
                for t in range(NT):
                    if t >= q0:
                        v.tensor_scalar(dqb[:, t, 0:QR], dqb[:, t, 0:QR], mst[:, 3, 6 + t:7 + t], None, ALU.mult)
                    if t >= CT:
                        kr = dqb[:, t, QR + KVR:DMLA]
                        v.tensor_tensor(rot[:, 0, 0, :], kr, cosr[:, t - CT, :], ALU.mult)
                        for pair in range(2):
                            last = v.tensor_tensor(rot[:, 1, 0, :].rearrange("p (f r e) -> p f r e", f=2, r=2)[:, :, pair, :],
                                                   kr.rearrange("p (f r e) -> p f r e", f=2, r=2)[:, :, 1 - pair, :],
                                                   sinr[:, t - CT, :].rearrange("p (f r e) -> p f r e", f=2, r=2)[:, :, pair, :],
                                                   ALU.mult)
                        link(last)
                        link(v.tensor_tensor(kr, rot[:, 0, 0, :], rot[:, 1, 0, :], ALU.add))
                    v.tensor_scalar(dqb[:, t, QR:QR + KVR], dqb[:, t, QR:QR + KVR], mst[:, 3, t:t + 1], None, ALU.mult
                                    ).then_inc(mla_n, 1)
                for t in range(NT):
                    dve.wait_ge(q_nope, before("q_nope", l) + t + 1)
                    if t:
                        dve.wait_ge(qkT_up, before("qkT_up", l) + t)
                    if t >= CT:
                        qr = ps[4 + 2 * (t % 2)][:, 0:H * DQK].rearrange("p (h d) -> p h d", h=H)[:, :, DH:DQK]
                        v.tensor_tensor(rot[:, 0, :, :], qr, cosr[:, t - CT, :].unsqueeze(1).to_broadcast([P, H, ROPE]), ALU.mult)
                        for piece in range(4):
                            to, fr = 8 * piece, 8 * (piece ^ 1)
                            last = v.tensor_tensor(rot[:, 1, :, to:to + 8], qr[:, :, fr:fr + 8],
                                                   sinr[:, t - CT, to:to + 8].unsqueeze(1).to_broadcast([P, H, 8]), ALU.mult)
                        link(last)
                        v.tensor_tensor(q_tok[:, :, DH:DQK], rot[:, 0, :, :], rot[:, 1, :, :], ALU.add)
                    v.tensor_copy(k_tok[:, :, DH:DQK], dqb[:, t, QR + KVR:DMLA].unsqueeze(1).to_broadcast([P, H, ROPE])
                                  ).then_inc(qk_tok, 1)
                    dve.wait_ge(qkT_up, before("qkT_up", l) + t + 1)
                    v.tensor_copy(kT[0:DQK, :, tile(t)], ps[1][0:DQK, :].rearrange("p (h d) -> p h d", h=H)).then_inc(qkT_dve, 1)
                attention(l, 1)
                if l == 0:
                    dve.wait_ge(ada_raw, 48)
                    biased(l, slice(16, 48))
                    gains(l, 1).then_inc(mod_late, 1)
                    dve.wait_ge(mod_late, 1)
                def low_part(kind, k, j=0):
                    dve.wait_ge(part_hi, split_count(l, kind, k, j))
                    raw, hi, lo = operand(l, ring_at[("m", (l, j))], kind, k)
                    v.tensor_tensor(lo, raw, hi.bitcast(F32), ALU.subtract).then_inc(part_lo, 1)

                for kind, k in SPLITS:
                    low_part(kind, k)
                q = 0
                for j in range(KD):
                    for seg in segments(l):
                        size = seg.stop - seg.start
                        for b in range(3):
                            dve.wait_ge(m_sig, before("m_sig", l) + q + 1)
                            br = ps[2 * (q % 4) + 1][:, 0:size]
                            if b == 0:
                                v.tensor_tensor(yT[:, j, seg], sig[q % 2][:, 0:size], br, ALU.mult).then_inc(m_ok, 1)
                            else:
                                link(v.tensor_tensor(branch[:, 0:size], sig[q % 2][:, 0:size], br, ALU.mult))
                                v.tensor_tensor(yT[:, j, seg], yT[:, j, seg], branch[:, 0:size], ALU.add).then_inc(m_ok, 1)
                                if b == 1:
                                    dve.wait_ge(m_ok, before("m_ok", l) + q + 1)
                            if j < KD - 1 and seg is segments(l)[-1]:
                                low_part("w", b, j + 1)
                            q += 1

                def diagonals(i):
                    n = 2 * NSEG[l] * i
                    for s in range(NSEG[l]):
                        for half in range(2):
                            if n:
                                dve.wait_ge(grow_up, before("grow_up", l) + n)
                            m0 = 24 * i + 16 + 4 * half
                            v.tensor_tensor(diag, ident.unsqueeze(1).to_broadcast([P, 4, P]),
                                            modT[l][:, m0:m0 + 4, s:s + 1].to_broadcast([P, 4, P]), ALU.mult).then_inc(diag_ok, 1)
                            n += 1

                def out_low_parts(half):
                    for i, (raw, hi, lo) in enumerate(out_operands(l, half)):
                        dve.wait_ge(out_hi, before("out_hi", l) + 2 * KD * half + i + 1)
                        v.tensor_tensor(lo, raw, hi.bitcast(F32), ALU.subtract).then_inc(out_lo, 1)

                dve.wait_ge(m_ok, before("m_ok", l) + q)
                out_low_parts(0)
                diagonals(0)
                dve.wait_ge(grow_ok, before("grow_ok", l) + 2 * NSEG[l])
                q = 0
                for half in range(2):
                    cols = slice(512 * half, 512 * half + 512)
                    for t in q_tiles(l):
                        dve.wait_ge(y_up, before("y_up", l) + q + 1)
                        if q:
                            dve.wait_ge(y_ok, before("y_ok", l) + q)
                        link(v.tensor_tensor(gated, ps[2 + q % 4][:, :], gate_row[:, 0 if t >= CT else 1, cols], ALU.mult))
                        v.tensor_tensor(x_sb[:, t, cols], x_sb[:, t, cols], gated, ALU.add).then_inc(y_ok, 1)
                        if q == 1:
                            out_low_parts(1)
                        q += 1
                dve.wait_ge(y_ok, before("y_ok", l) + q)
                diagonals(1)
                scaled(2 * l + 1, xn2)
                modulate(l, 1)
                dve.wait_ge(lg_up, before("lg_up", l) + 1)
                nt = NT - q0
                lg = ps[0][:, q0 * E:NT * E].rearrange("p (t e) -> p t e", e=E)
                link(v.tensor_reduce(st[:, 48 + q0:48 + NT], lg, AX_X, ALU.max))
                v.tensor_tensor(aff[:, q0:NT, :], lg, st[:, 48 + q0:48 + NT].unsqueeze(2).to_broadcast([P, nt, E]), ALU.subtract
                                ).then_inc(aff_sh, 1)
                dve.wait_ge(aff_exp, before("aff_exp", l) + 1)
                link(v.tensor_reduce(st[:, 48 + q0:48 + NT], aff[:, q0:NT, :], AX_X, ALU.add))
                link(v.reciprocal(st[:, 56 + q0:56 + NT], st[:, 48 + q0:48 + NT]))
                v.tensor_tensor(aff[:, q0:NT, :], aff[:, q0:NT, :], st[:, 56 + q0:56 + NT].unsqueeze(2).to_broadcast([P, nt, E]),
                                ALU.mult).then_inc(aff_ok, 1)
                dve.wait_ge(affT_up, before("affT_up", l) + 1)
                segs = segments(l)
                for i, seg in enumerate(segs):
                    last = v.tensor_copy(work[0:E, seg], ps[1 + i][0:E, 0:seg.stop - seg.start])
                link(last)
                for i, seg in enumerate(segs):
                    for _ in range((CAPL, CAPC)[i] // 8):
                        link(v.max(top8[0:E, i, :], work[0:E, seg]))
                        link(v.match_replace(work[0:E, seg], top8[0:E, i, :], work[0:E, seg], -1.0))
                cols = slice(q0 * P, TOK)
                link(v.tensor_scalar(chosen[0:E, cols], work[0:E, cols], 0.0, None, ALU.is_lt))
                for seg in segs:
                    last = v.tensor_tensor_scan(slotT[0:E, seg], ones[0:E, 0:1].to_broadcast([E, seg.stop - seg.start]),
                                                chosen[0:E, seg], 0.0, ALU.mult, ALU.add)
                link(last)
                link(v.tensor_tensor(slotT[0:E, cols], slotT[0:E, cols], chosen[0:E, cols], ALU.mult))
                v.tensor_scalar(slotT[0:E, cols], slotT[0:E, cols], 1.0, None, ALU.subtract).then_inc(top_ok, 1)
                dve.wait_ge(slot_up, before("slot_up", l) + 1)
                v.tensor_copy(slot[:, q0:NT, :], ps[3][:, q0 * E:NT * E].rearrange("p (t e) -> p t e", e=E)).then_inc(slot_ok, 1)
                dve.wait_ge(slot_ok, before("slot_ok", l) + 1)
                has_ctx = NSEG[l] - 1
                ns = 2 + has_ctx
                nq = 2 * NQ[l]
                if not has_ctx:
                    for buf in (xg_hi, xg_lo):
                        v.tensor_scalar(buf[:, :, :, CAPL:ROWS].rearrange("p a b c -> p (a b) c"),
                                        ones[:, 0:CAPC].unsqueeze(1).to_broadcast([P, KD * GE, CAPC]), 0.0, None, ALU.mult
                                        ).then_inc(xg_zero, 1)

                def low(g, i):
                    dve.wait_ge(w_hi_ok, before("w_hi_ok", l) + g * PER_TURN + (i + 1))
                    v.tensor_tensor(w_lo[:, i % SLOTS, :, :], w_raw[i % SLOTS], w_hi[:, i % HI_SLOTS, :, :].bitcast(F32),
                                    ALU.subtract).then_inc(w_lo_ok, 1)

                def hidden(g, j, half):
                    dve.wait_ge(w_used, before("w_used", l) + g * PER_TURN + used(j, "up", half))
                    dve.wait_ge(gu_silu, before("gu_silu", l) + g * 8 + (2 * j + half + 1))
                    if j:
                        dve.wait_ge(hidT_up, before("hidT_up", l) + g * 8 + 2 * j)
                    v.tensor_tensor(hid[0:ROWS, 512 * half:512 * half + 512], g_act[0:ROWS, half, :],
                                    ps[2 * half + 1][0:ROWS, :], ALU.mult).then_inc(hid_ok, 1)

                def hidden_low(g, j):
                    if j:
                        dve.wait_ge(w_used, before("w_used", l) + g * PER_TURN + used(j - 1, "down", 1))
                    for b in range(2):
                        dve.wait_ge(hidT_act, before("hidT_act", l) + g * 8 + (2 * j + b + 1))
                        v.tensor_tensor(hidT_lo[:, 4 * b:4 * b + 4, :], ps[4 + b][:, 0:4 * ROWS].rearrange("p (a b) -> p a b", a=4),
                                        hidT_hi[:, 4 * b:4 * b + 4, :].bitcast(F32), ALU.subtract).then_inc(hidT_dve, 1)

                def results(g, j, half):
                    cols = slice(512 * half, 512 * half + 512)
                    dve.wait_ge(w_used, before("w_used", l) + g * PER_TURN + used(j, "down", half))
                    r = 64 * (j % 2)
                    last = v.tensor_tensor(ye_l[r:r + 64, j // 2, cols], ps[6 + half][0:64, :], gate5[0:64, cols], ALU.mult)
                    if has_ctx:
                        last = v.tensor_tensor(ye_c[32 * j:32 * j + 32, cols], ps[6 + half][64:96, :], gate5[64:96, cols], ALU.mult)
                    last.then_inc(ye_ok, 1)

                def one_hot(g, first):
                    if not first:
                        dve.wait_ge(selT_up, before("selT_up", l) + g * ns)
                    v.tensor_copy(turn_s[:, 0, q0:NT, :], slot[:, q0:NT, bass.ds(g * GE, GE)]).then_inc(turn_own, 1)
                    v.tensor_copy(turn_s[:, 1, q0:NT, :], aff[:, q0:NT, bass.ds(g * GE, GE)]).then_inc(turn_own, 1)
                    dve.wait_ge(turn_own, before("turn_own", l) + g * 3 + 2)
                    for t in range(q0, NT):
                        dst, i, cap = (sel_l, t - CT, CAPL) if t >= CT else (sel_c, t, CAPC)
                        last = v.tensor_tensor(dst[:, i, :, :], iota[:, 0:cap].unsqueeze(1).to_broadcast([P, GE, cap]),
                                               turn_s[:, 0, t, :].unsqueeze(2).to_broadcast([P, GE, cap]), ALU.is_equal)
                    last.then_inc(turn_own, 1)

                def weighted(g):
                    dve.wait_ge(turn_own, before("turn_own", l) + g * 3 + 3)
                    for t in range(q0, NT):
                        src, dst, i, cap = (sel_l, selw_l, t - CT, CAPL) if t >= CT else (sel_c, selw_c, t, CAPC)
                        last = v.tensor_tensor(dst[:, i, :, :], src[:, i, :, :],
                                               turn_s[:, 1, t, :].unsqueeze(2).to_broadcast([P, GE, cap]), ALU.mult)
                    last.then_inc(sel_ok, 1)

                def gathered_low(g, dt):
                    dve.wait_ge(xg_hi_ok, before("xg_hi_ok", l) + g * KD + (dt + 1))
                    for s in range(1 + has_ctx):
                        c, n = ((0, CAPL), (CAPL, CAPC))[s]
                        last = v.tensor_tensor(xg_lo[:, dt, :, c:c + n],
                                               xg_sum[:, dt % 2, GE * c:GE * (c + n)].rearrange("p (a b) -> p a b", a=GE),
                                               xg_hi[:, dt, :, c:c + n].bitcast(F32), ALU.subtract)
                    last.then_inc(xg_lo_ok, 1)

                def added(g, q):
                    t, cols = q_tiles(l)[q // 2], slice(512 * (q % 2), 512 * (q % 2) + 512)
                    dve.wait_ge(sc_up, before("sc_up", l) + g * nq + (q + 1))
                    v.tensor_tensor(x_sb[:, t, cols], x_sb[:, t, cols], ps[6 + q % 2][:, :], ALU.add).then_inc(x_ok, 1)

                def turn(g, first, final):
                    for i in range(PER_TURN):
                        j, matrix, half, part = LOADS[i]
                        if part == 1 and matrix == "up":
                            hidden(g, j, half)
                        if part == 1 and matrix == "down":
                            results(g, j, half)
                        if turned_after(i) is not None:
                            hidden_low(g, turned_after(i))
                        if not final or i + HI_SLOTS < PER_TURN:
                            low(g, i + HI_SLOTS)
                        if not first and i < nq:
                            added(g - 1, i)
                        if not final and i == NEXT_SEL:
                            one_hot(g + 1, False)
                        if not final and i == NEXT_SEL + 1:
                            weighted(g + 1)
                        if not final and i >= NEXT_GATHER:
                            gathered_low(g + 1, i - NEXT_GATHER)

                one_hot(0, True)
                weighted(0)
                for i in range(HI_SLOTS):
                    low(0, i)
                for dt in range(KD):
                    gathered_low(0, dt)
                turn(0, True, False)
                with dve.Fori(1, TURNS - 1) as g:
                    turn(g, False, False)
                turn(TURNS - 1, False, True)
                for q in range(nq):
                    added(TURNS - 1, q)
            dve.wait_ge(fin_in, 16)
            for t in range(root(2 * DEPTH), NT):
                v.scalar_tensor_tensor(fin[:, t - CT, :], x_sb[:, t, :], st[:, 24 + t:25 + t], fin_row, ALU.mult, ALU.mult
                                       ).then_inc(fin_ok, 1)


NAMES = ["x", "c", "ctx", "c_ctx", "ada_w", "ada_b", "norm1", "norm2", "w_in", "na_rpb", "mla_q_norm", "mla_w_uq", "mla_kv_norm",
         "mla_w_ukv", "gla_w_af", "gla_b_af", "gla_w_ab", "gla_b_ab", "gla_o_norm", "w_br_a", "w_br_b", "w_br_c", "w_out",
         "moe_router", "moe_w_gate", "moe_w_up", "moe_w_down", "final_norm"]


def kernel(**inputs):
    import concourse.bacc as bacc
    from concourse.bass_utils import run_bass_kernel_spmd

    nc = bacc.Bacc("TRN2", target_bir_lowering=False, num_devices=1)
    arrays, aps = {}, {}
    for name in NAMES + ["constants"]:
        v = constants() if name == "constants" else np.ascontiguousarray(inputs[name])
        arrays["in_" + name] = v
        aps[name] = nc.dram_tensor("in_" + name, v.shape, mybir.dt.from_np(v.dtype), kind="ExternalInput").ap()
    out = nc.dram_tensor("out", (1, SEQ, D), F32, kind="ExternalOutput").ap()
    hybrid_kernel(nc, aps, out)
    r = run_bass_kernel_spmd(nc, [arrays], core_ids=[0])
    return r.results[0]["out"]
```
